# Optimizing a Trainium2 kernel written in Bass

```python
import jax, jax.numpy as jnp
from jax import lax
import numpy as np

D_MODEL = 1024
BATCH = 1
SEQ = 256
DEPTH = 2

POOL_WIDTH = D_MODEL // 2
N_POOL_GROUPS = 4
POOL_GROUP_DIM = POOL_WIDTH // N_POOL_GROUPS
POOL_WINDOWS = (2, 4, 8, 16)
HGRN_WIDTH = D_MODEL // 2
HGRN_EXPAND = 128
HGRN_HEADS = HGRN_WIDTH // HGRN_EXPAND
HGRN_HK = HGRN_HEADS * HGRN_EXPAND
HGRN_HEAD_V = HGRN_WIDTH // HGRN_HEADS
CHUNK = 64
N_BRANCHES = 2
OFF_Q = POOL_WIDTH
OFF_F = OFF_Q + HGRN_HK
OFF_I = OFF_F + HGRN_HK
OFF_G = OFF_I + HGRN_WIDTH
OFF_GATES = OFF_G + HGRN_WIDTH
IN_COLS = OFF_GATES + N_BRANCHES * D_MODEL
D_FF_DENSE = 2816
N_EXPERTS = 8
TOP_K = 2
D_FF_EXPERT = 3584
N_DENSE = (DEPTH + 1) // 2
N_MOE = DEPTH // 2
EPS = 1e-6
LB_FLOOR = 1e-30

kernel_name = "hybrid_pool_hgrn2_gated_moe_trunk"

def _rmsnorm(x, w):
    xf = x.astype(jnp.float32)
    y = xf * lax.rsqrt(jnp.mean(xf * xf, axis=-1, keepdims=True) + EPS)
    return (y * w.astype(jnp.float32)).astype(x.dtype)

def _swiglu(h, w_gate, w_up, w_down):
    return (jax.nn.silu(h @ w_gate) * (h @ w_up)) @ w_down

def _pool_mixer(u, pool_w, pool_scale):
    B, S, _ = u.shape
    ug = u.reshape(B, S, N_POOL_GROUPS, POOL_GROUP_DIM).astype(jnp.float32)
    csum = jnp.cumsum(ug, axis=1)
    pos = jnp.arange(1, S + 1, dtype=jnp.float32)[None, :, None]
    outs = []
    for gi, w in enumerate(POOL_WINDOWS):
        c = csum[:, :, gi]
        c_prev = jnp.pad(c, ((0, 0), (w, 0), (0, 0)))[:, :S]
        outs.append((c - c_prev) / jnp.minimum(pos, float(w)))
    pooled = (jnp.stack(outs, axis=2) - ug).astype(u.dtype)
    mixed = jnp.einsum('bsgc,gcd->bsgd', pooled, pool_w)
    return mixed.reshape(B, S, POOL_WIDTH) * pool_scale

def _hgrn2_chunked(q, k, v, log_f):
    B, S, H, dk = q.shape
    dv = v.shape[-1]
    n_chunks = S // CHUNK

    def to_chunks(t):
        return t.reshape(B, n_chunks, CHUNK, H, t.shape[-1]).transpose(1, 0, 3, 2, 4)

    qc, kc, vc = to_chunks(q), to_chunks(k), to_chunks(v)
    G = jnp.cumsum(to_chunks(log_f), axis=3)
    mask = jnp.tril(jnp.ones((CHUNK, CHUNK), dtype=bool))[:, :, None]

    def step(state, xs):
        qb, kb, vb, Gb = xs
        diff = Gb[:, :, :, None, :] - Gb[:, :, None, :, :]
        decay = jnp.where(mask, jnp.exp(jnp.where(mask, diff, 0.0)), 0.0)
        scores = jnp.einsum('bhtk,bhsk,bhtsk->bhts', qb, kb, decay)
        o = jnp.einsum('bhts,bhsv->bhtv', scores, vb) + jnp.einsum('bhtk,bhkv->bhtv', qb * jnp.exp(Gb), state)
        G_last = Gb[:, :, -1:, :]
        new_state = jnp.exp(G_last[:, :, 0, :])[..., None] * state + jnp.einsum(
            'bhsk,bhsv->bhkv', kb * jnp.exp(G_last - Gb), vb)
        return new_state, o

    state0 = jnp.zeros((B, H, dk, dv), jnp.float32)
    _, o = lax.scan(step, state0, (qc, kc, vc, G))
    return o.transpose(1, 0, 3, 2, 4).reshape(B, S, H, dv)

def _hgrn2_mixer(q_pre, f_pre, i_pre, g_pre, lb, norm_w):
    B, S, _ = q_pre.shape
    f32 = jnp.float32
    q = jax.nn.silu(q_pre.astype(f32)).reshape(B, S, HGRN_HEADS, HGRN_EXPAND)
    log_lb = jnp.log(jnp.maximum(lb, LB_FLOOR))
    log_f = jnp.logaddexp(log_lb, jnp.log1p(-lb) + jax.nn.log_sigmoid(f_pre.astype(f32)))
    k = -jnp.expm1(log_f)
    log_f = log_f.reshape(B, S, HGRN_HEADS, HGRN_EXPAND)
    k = k.reshape(B, S, HGRN_HEADS, HGRN_EXPAND)
    v = i_pre.astype(f32).reshape(B, S, HGRN_HEADS, HGRN_HEAD_V)
    o = _hgrn2_chunked(q, k, v, log_f)
    o = o * lax.rsqrt(jnp.mean(o * o, axis=-1, keepdims=True) + EPS) * norm_w.astype(f32)
    g = jax.nn.silu(g_pre.astype(f32)).reshape(B, S, HGRN_HEADS, HGRN_HEAD_V)
    return (o * g).reshape(B, S, HGRN_WIDTH).astype(q_pre.dtype)

def _token_mixer(h, w_in, gate_bias, pool_w, pool_scale, pool_up, lb, hgrn_norm_w, hgrn_up, w_out):
    proj = h @ w_in
    u = proj[..., :OFF_Q]
    q_pre = proj[..., OFF_Q:OFF_F]
    f_pre = proj[..., OFF_F:OFF_I]
    i_pre = proj[..., OFF_I:OFF_G]
    g_pre = proj[..., OFF_G:OFF_GATES]
    gates = jax.nn.sigmoid(proj[..., OFF_GATES:] + gate_bias)
    y_pool = _pool_mixer(u, pool_w, pool_scale) @ pool_up
    y_hgrn = _hgrn2_mixer(q_pre, f_pre, i_pre, g_pre, lb, hgrn_norm_w) @ hgrn_up
    merged = gates[..., :D_MODEL] * y_pool + gates[..., D_MODEL:] * y_hgrn
    return merged @ w_out

def _moe(h, router, w_gate, w_up, w_down):
    logits = (h @ router).astype(jnp.float32)
    top_v, top_i = lax.top_k(logits, TOP_K)
    top_w = jax.nn.softmax(top_v, axis=-1)
    combine = jnp.sum(jax.nn.one_hot(top_i, N_EXPERTS, dtype=jnp.float32) * top_w[..., None], axis=-2)
    y = jnp.zeros_like(h)
    for e in range(N_EXPERTS):
        y = y + combine[..., e:e + 1].astype(h.dtype) * _swiglu(h, w_gate[e], w_up[e], w_down[e])
    return y

def setup_inputs(seed: int = 0) -> dict:
    key = jax.random.key(seed)
    ks = jax.random.split(key, 24)
    f32 = jnp.float32

    def w(k, shape, fan_in):
        return jax.random.normal(k, shape, f32) * (fan_in ** -0.5)

    def gain(k, shape):
        return 1.0 + 0.05 * jax.random.normal(k, shape, f32)

    return {
        "x": jax.random.normal(ks[0], (BATCH, SEQ, D_MODEL), f32),
        "attn_norm_w": gain(ks[1], (DEPTH, D_MODEL)),
        "w_in": w(ks[2], (DEPTH, D_MODEL, IN_COLS), D_MODEL),
        "gate_bias": 0.01 * jax.random.normal(ks[3], (DEPTH, N_BRANCHES * D_MODEL), f32),
        "pool_w": w(ks[4], (DEPTH, N_POOL_GROUPS, POOL_GROUP_DIM, POOL_GROUP_DIM), POOL_GROUP_DIM),
        "pool_scale": gain(ks[5], (DEPTH, POOL_WIDTH)),
        "pool_up": w(ks[6], (DEPTH, POOL_WIDTH, D_MODEL), POOL_WIDTH),
        "hgrn_lower_bounds": 0.5 * jax.random.normal(ks[7], (DEPTH, HGRN_HK), f32),
        "hgrn_norm_w": gain(ks[8], (DEPTH, HGRN_HEAD_V)),
        "hgrn_up": w(ks[9], (DEPTH, HGRN_WIDTH, D_MODEL), HGRN_WIDTH),
        "w_out": w(ks[10], (DEPTH, D_MODEL, D_MODEL), D_MODEL),
        "ffn_norm_w": gain(ks[11], (DEPTH, D_MODEL)),
        "dense_w_gate": w(ks[12], (N_DENSE, D_MODEL, D_FF_DENSE), D_MODEL),
        "dense_w_up": w(ks[13], (N_DENSE, D_MODEL, D_FF_DENSE), D_MODEL),
        "dense_w_down": w(ks[14], (N_DENSE, D_FF_DENSE, D_MODEL), D_FF_DENSE),
        "moe_router": w(ks[15], (N_MOE, D_MODEL, N_EXPERTS), D_MODEL),
        "moe_w_gate": w(ks[16], (N_MOE, N_EXPERTS, D_MODEL, D_FF_EXPERT), D_MODEL),
        "moe_w_up": w(ks[17], (N_MOE, N_EXPERTS, D_MODEL, D_FF_EXPERT), D_MODEL),
        "moe_w_down": w(ks[18], (N_MOE, N_EXPERTS, D_FF_EXPERT, D_MODEL), D_FF_EXPERT),
        "final_norm_w": gain(ks[19], (D_MODEL,)),
    }

def reference(x, attn_norm_w, w_in, gate_bias, pool_w, pool_scale, pool_up, hgrn_lower_bounds,
              hgrn_norm_w, hgrn_up, w_out, ffn_norm_w, dense_w_gate, dense_w_up, dense_w_down,
              moe_router, moe_w_gate, moe_w_up, moe_w_down, final_norm_w):
    lb_soft = jax.nn.softmax(hgrn_lower_bounds.astype(jnp.float32), axis=0)
    lower_bounds = jnp.clip(jnp.cumsum(lb_soft, axis=0) - lb_soft[0:1], 0.0, 1.0 - 1e-6)
    for l in range(DEPTH):
        h = _rmsnorm(x, attn_norm_w[l])
        x = x + _token_mixer(h, w_in[l], gate_bias[l], pool_w[l], pool_scale[l], pool_up[l],
                             lower_bounds[l], hgrn_norm_w[l], hgrn_up[l], w_out[l])
        h = _rmsnorm(x, ffn_norm_w[l])
        if l % 2 == 0:
            j = l // 2
            x = x + _swiglu(h, dense_w_gate[j], dense_w_up[j], dense_w_down[j])
        else:
            j = l // 2
            x = x + _moe(h, moe_router[j], moe_w_gate[j], moe_w_up[j], moe_w_down[j])
    return _rmsnorm(x, final_norm_w)


_drawn_inputs = setup_inputs


def setup_inputs(seed=0):
    import zlib

    import numpy as np

    out = dict(_drawn_inputs(seed))
    spreads = {}
    factors = {'gate_bias': 4.382}
    for name, (base, spread) in spreads.items():
        noise = np.random.default_rng([zlib.crc32(name.encode()), seed]).standard_normal(out[name].shape)
        drawn = base * np.exp(spread * noise) if base else spread * noise
        out[name] = __import__('jax').numpy.asarray(drawn.astype(out[name].dtype))
    for name, factor in factors.items():
        out[name] = (out[name] * factor).astype(out[name].dtype)
    return out
```

```python
from contextlib import ExitStack

import concourse.bass as bass
from concourse import mybir

F32 = mybir.dt.float32
I32 = mybir.dt.int32
U32 = mybir.dt.uint32
ALU = mybir.AluOpType
ACT = mybir.ActivationFunctionType
AX_X = mybir.AxisListType.X

P = 128
T = 256
TH = T // P
D = 1024
KT = D // P
DEPTH = 2
HEADS = 4
POOL_TILES = 4
WINDOWS = (2, 4, 8, 16)
PAD = 16
F_DENSE = 2816
N_EXP = 8
F_EXP = 3584
EPS = 1e-6
LB_FLOOR = 1e-30
LB_CEIL = 1.0 - 1e-6
EXP_CEIL = 1e37

RING = 7
SLOT = 4096
GROUP = 512
GT = GROUP // P
CAP = 96
MAX_EXTRA = (2 * T) // (CAP + 1)
ITEMS = N_EXP + MAX_EXTRA
COLS = ITEMS + 1

LEVELS = ["diag", "cross"] + [64, 32, 16, 8, 4, 2, 1]
NL = len(LEVELS)

C_ATTN, C_FFN, C_BIAS, C_PSCALE, C_LB, C_HNORM, C_ROWS = 0, 16, 32, 64, 72, 80, 82


def dense_groups(width):
    out = []
    while width > 0:
        out.append(min(GT, width // P))
        width -= GROUP
    return out


DENSE = dense_groups(F_DENSE)
EXPERT = dense_groups(F_EXP)


def swiglu_order(groups):
    out = []
    for i in range(len(groups)):
        out += [("g", i), ("u", i)]
        if i >= 1:
            out.append(("d", i - 1))
    return out + [("d", len(groups) - 1)]


def plan():
    jobs, chunks = {}, []

    def job(*key):
        jobs[key if len(key) > 1 else key[0]] = len(jobs)

    job("params")
    for i in range(4):
        job("x_in", i)
    for l in range(DEPTH):
        job("norm", l, 0)
        for name, n, last in (("f", 4, 3), ("q", 4, 3), ("v", 2, 1), ("u", 4, 3), ("g", 4, 3)):
            for j in range(n):
                job(name, l, j)
            chunks.append((name, l, 0, "job", (name, l, last)))
        for j in range(POOL_TILES):
            job("mix", l, j)
        for c in range(4):
            for j in range(4):
                job("gate", l, 4 * c + j)
            chunks.append(("gate", l, c, "job", ("gate", l, 4 * c + 3)))
        for j in range(KT):
            job("y_pool", l, j)
        chunks.append(("pool_up", l, 0, "job", ("y_pool", l, KT - 1)))
        for j in range(KT):
            job("y_hgrn", l, j)
        chunks.append(("hgrn_up", l, 0, "job", ("y_hgrn", l, KT - 1)))
        for c in range(2):
            for j in range(4):
                job("w_out", l, 4 * c + j)
            chunks.append(("w_out", l, c, "job", ("w_out", l, 4 * c + 3)))
        job("norm", l, 1)
        if l == 0:
            first = [sum(DENSE[:i]) for i in range(len(DENSE))]
            for j in range(sum(DENSE)):
                job("ffn", j)
            for kind, i in swiglu_order(DENSE):
                if kind == "d":
                    chunks.append(("dense_d", l, i, "down", i + 1))
                else:
                    chunks.append(("dense_" + kind, l, i, "job", ("ffn", first[i] + DENSE[i] - 1)))
    job("logits")
    for i in range(4):
        job("h_tok", i)
    for i in range(4):
        job("x_tok", i)
    job("ranks")
    return jobs, chunks


def build(nc, x, attn_norm_w, w_in, gate_bias, pool_w, pool_scale, pool_up, hgrn_lower_bounds,
          hgrn_norm_w, hgrn_up, w_out, ffn_norm_w, dense_w_gate, dense_w_up, dense_w_down,
          moe_router, moe_w_gate, moe_w_up, moe_w_down, final_norm_w, out):
    JOB, CHUNKS = plan()
    J_LOOP = len(JOB)
    ITEM_JOBS = sum(EXPERT) + 4
    C_LOOP = len(CHUNKS)
    MOE = swiglu_order(EXPERT)
    ITEM_CHUNKS = len(MOE)
    assert ITEM_CHUNKS % RING == 0 and ITEM_JOBS % 4 == 0
    DN_LOOP = len(DENSE)
    TH_LOOP = DEPTH * 8 + sum(DENSE)
    TH_OF = {}
    for l in range(DEPTH):
        for name in "qg":
            for j in range(4):
                TH_OF[name, l, j] = len(TH_OF)
        if l == 0:
            for j in range(sum(DENSE)):
                TH_OF["ffn", j] = len(TH_OF)
    CHUNK_OF = {c[:3]: n for n, c in enumerate(CHUNKS)}
    MOE_CHUNK = {c: n for n, c in enumerate(MOE)}

    with ExitStack() as ctx:
        def sb(name, shape, dt=F32):
            return ctx.enter_context(nc.sbuf_tensor(name, shape, dt))

        def sem(name):
            return ctx.enter_context(nc.semaphore(name))

        ring = sb("ring", [P, RING, SLOT])
        xT = sb("xT", [P, KT, T])
        hT_mem = sb("hT_mem", [P, KT * T])
        qk_mem = sb("qk_mem", [P, KT * T])
        gates_mem = sb("gates_mem", [P, 16 * T])
        G = sb("G", [P, HEADS, T])
        og_mem = sb("og_mem", [P, HEADS * T])
        v_tok = sb("v_tok", [P, TH, HEADS * P])
        e_mem = sb("e_mem", [P, 2, HEADS * T])
        pool_mem = sb("pool_mem", [P, 3 * POOL_TILES * (PAD + T)])
        th = sb("th", [P, 4, T])
        masks = sb("masks", [P, NL - 2, P])
        ident = sb("ident", [P, P])
        mean_d = sb("mean_d", [P, P])
        mean_h = sb("mean_h", [P, P])
        ones = sb("ones", [P, P])
        before = sb("before", [P, P])
        scan_keep = sb("scan_keep", [P, T])
        rows = sb("rows", [C_ROWS, P])
        cols = sb("cols", [P, C_ROWS])
        half_bias = sb("half_bias", [P, 32])
        half_hnorm = sb("half_hnorm", [P, DEPTH])
        lb = sb("lb", [P, DEPTH, HEADS])
        lb_floor = sb("lb_floor", [P, DEPTH, HEADS])
        one_lb = sb("one_lb", [P, DEPTH, HEADS])
        half_one_lb = sb("half_one_lb", [P, DEPTH, HEADS])
        lb_tmp = sb("lb_tmp", [P, 4, HEADS])
        eps = sb("eps", [P, 1])
        poolw = sb("poolw", [P, DEPTH, POOL_TILES, P])
        rms_ln = sb("rms_ln", [P, T])
        rstd = sb("rstd", [P, T])
        inv_pos = sb("inv_pos", [P, POOL_TILES, PAD])
        pool_head = sb("pool_head", [P, POOL_TILES, PAD])
        router = sb("router", [P, KT, N_EXP])
        iota_e = sb("iota_e", [P, N_EXP])
        iota_c = sb("iota_c", [P, CAP])
        iota_j = sb("iota_j", [P, COLS, N_EXP])
        top_i = sb("top_i", [P, TH, 8], U32)
        pos_item = sb("pos_item", [P, TH, COLS])
        w_item = sb("w_item", [P, TH, COLS])
        item_e = sb("item_e", [P, COLS], I32)
        n_items = sb("n_items", [P, 1], I32)
        fin = sb("fin", [P, 6])

        hT = hT_mem[:, :].rearrange("p (k t) -> p k t", k=KT)
        oT = hT_mem[:, 0:HEADS * T].rearrange("p (h t) -> p h t", h=HEADS)
        sq = e_mem[:, :, :].rearrange("p a (k t) -> p (a k) t", t=T)
        merged = qk_mem[:, :].rearrange("p (k t) -> p k t", k=KT)
        qT = qk_mem[:, 0:HEADS * T].rearrange("p (h t) -> p h t", h=HEADS)
        kT = qk_mem[:, HEADS * T:].rearrange("p (h t) -> p h t", h=HEADS)
        hid = qk_mem[:, :].rearrange("p (b f t) -> p b f t", b=2, f=GT)
        gates = gates_mem[:, :].rearrange("p (k t) -> p k t", k=16)
        og = og_mem[:, :].rearrange("p (h t) -> p h t", h=HEADS)
        expf = e_mem[:, 0, :].rearrange("p (h t) -> p h t", h=HEADS)
        sig = e_mem[:, 1, :].rearrange("p (h t) -> p h t", h=HEADS)
        PW = POOL_TILES * (PAD + T)
        pu, pb, pc = (pool_mem[:, i * PW:(i + 1) * PW].rearrange("p (g t) -> p g t", g=POOL_TILES) for i in range(3))
        score = pool_mem[:, 0:TH * HEADS * P].rearrange("p (a h t) -> p a h t", a=TH, h=HEADS)
        score_x = pool_mem[:, 1024:1536].rearrange("p (h t) -> p h t", h=HEADS)
        masked = pool_mem[:, 1536:2560].rearrange("p (a h t) -> p a h t", a=TH, h=HEADS)
        o_sq = pool_mem[:, 1536:2560]
        mixed = th
        h_tok = gates_mem[:, 0:TH * D].rearrange("p (a d) -> p a d", a=TH)
        x_tok = gates_mem[:, TH * D:].rearrange("p (a d) -> p a d", a=TH)
        hTe = e_mem[:, 0, 0:KT * CAP].rearrange("p (k c) -> p k c", k=KT)
        yT = e_mem[:, 1, 0:KT * CAP].rearrange("p (k c) -> p k c", k=KT)
        y_tok = G[0:CAP, :, :].rearrange("p h t -> p (h t)")
        sel = og_mem[:, 0:TH * CAP].rearrange("p (a c) -> p a c", a=TH)
        sel_w = og_mem[:, TH * CAP:2 * TH * CAP].rearrange("p (a c) -> p a c", a=TH)
        sel_wT = og_mem[0:CAP, 2 * TH * CAP:2 * TH * CAP + T].rearrange("p (a c) -> p a c", a=TH)
        hid_e = qk_mem[:, 0:2 * GT * CAP].rearrange("p (b f t) -> p b f t", b=2, f=GT)
        at = [0]

        def scratch(*shape):
            n = 1
            for s in shape:
                n *= s
            v = pool_mem[:, at[0]:at[0] + n]
            at[0] += n
            return v

        lg = scratch(TH, 8).rearrange("p (a e) -> p a e", a=TH)
        top_v = scratch(TH, 8).rearrange("p (a e) -> p a e", a=TH)
        top_f = scratch(TH, 8).rearrange("p (a e) -> p a e", a=TH)
        gap = scratch(TH)
        gap_e = scratch(TH)
        gap_1 = scratch(TH)
        w1 = scratch(TH)
        w2 = scratch(TH)
        hot1 = scratch(TH, 8).rearrange("p (a e) -> p a e", a=TH)
        hot2 = scratch(TH, 8).rearrange("p (a e) -> p a e", a=TH)
        wt1 = scratch(TH, 8).rearrange("p (a e) -> p a e", a=TH)
        wt2 = scratch(TH, 8).rearrange("p (a e) -> p a e", a=TH)
        chosen = scratch(TH, 8).rearrange("p (a e) -> p a e", a=TH)
        comb = scratch(TH, 8).rearrange("p (a e) -> p a e", a=TH)
        rank1 = scratch(TH, 8).rearrange("p (a e) -> p a e", a=TH)
        count = scratch(8)
        over1 = scratch(8)
        over2 = scratch(8)
        over = scratch(8)
        cum = scratch(8)
        start = scratch(8)
        start1 = scratch(8)
        ones8 = scratch(8)
        one1 = scratch(COLS, 8).rearrange("p (j e) -> p j e", e=8)
        one2 = scratch(COLS, 8).rearrange("p (j e) -> p j e", e=8)
        hot = scratch(COLS, 8).rearrange("p (j e) -> p j e", e=8)
        prod = scratch(3, COLS, 8).rearrange("p (a j e) -> p a j e", a=3, e=8)
        base1 = scratch(COLS)
        base2 = scratch(COLS)
        base = scratch(COLS)
        e_f = scratch(COLS)
        n_f = scratch(1)

        job_bank = [ctx.enter_context(nc.psum_tensor(f"job_bank{i}", [P, 512], F32)) for i in range(4)]
        acc = [ctx.enter_context(nc.psum_tensor(f"acc{i}", [P, 512], F32)) for i in range(4)]

        landed = [sem(f"landed{i}") for i in range(RING)]
        x_landed = sem("x_landed")
        params_landed = sem("params_landed")
        poolw_landed = sem("poolw_landed")
        router_landed = sem("router_landed")
        fnw_landed = sem("fnw_landed")
        consts = sem("consts")
        job_done = sem("job_done")
        job_taken = [sem(f"job_taken{i}") for i in range(4)]
        down_done = sem("down_done")
        lb_max_ready = sem("lb_max_ready")
        lb_exp_ready = sem("lb_exp_ready")
        params_ready = sem("params_ready")
        sq_ready = sem("sq_ready")
        rstd_ready = sem("rstd_ready")
        h_ready = sem("h_ready")
        x_ready = sem("x_ready")
        forget_ready = sem("forget_ready")
        key_ready = sem("key_ready")
        logf_ready = sem("logf_ready")
        gsum_ready = sem("gsum_ready")
        th_ready = sem("th_ready")
        win_ready = sem("win_ready")
        pooled_ready = sem("pooled_ready")
        arg_ready = sem("arg_ready")
        exp_ready = sem("exp_ready")
        scaled_ready = sem("scaled_ready")
        level_done = sem("level_done")
        level_taken = sem("level_taken")
        o_done = sem("o_done")
        o_sq_ready = sem("o_sq_ready")
        o_mean_done = sem("o_mean_done")
        o_ln = sem("o_ln")
        o_rstd_ready = sem("o_rstd_ready")
        o_ready = sem("o_ready")
        merged_ready = sem("merged_ready")
        gap_ready = sem("gap_ready")
        gap_exp_ready = sem("gap_exp_ready")
        chosen_ready = sem("chosen_ready")
        tables_ready = sem("tables_ready")
        sel_ready = sem("sel_ready")
        gathered = sem("gathered")
        hTe_ready = sem("hTe_ready")
        yT_dve = sem("yT_dve")
        yT_act = sem("yT_act")
        y_turned = sem("y_turned")
        y_dve = sem("y_dve")
        y_act = sem("y_act")
        silu_half = sem("silu_half")
        fin_sq = sem("fin_sq")
        fin_ln = sem("fin_ln")
        fin_rstd = sem("fin_rstd")
        fin_ready = sem("fin_ready")
        stored = sem("stored")
        pool_step = sem("pool_step")
        dve_step = sem("dve_step")

        def done(eng, n):
            eng.wait_ge(job_done, n + 1)

        def taken(eng, n):
            eng.wait_ge(job_taken[n % 4], n // 4 + 1)

        def bank_free(eng, n):
            if n >= 4:
                taken(eng, n - 4)

        def done_i(eng, jj, it):
            eng.wait_ge(job_done, it * ITEM_JOBS + (J_LOOP + jj + 1))

        def taken_i(eng, jj, it):
            n = J_LOOP + jj
            eng.wait_ge(job_taken[n % 4], it * (ITEM_JOBS // 4) + (n // 4 + 1))

        w_in_v = w_in.rearrange("l (k p) f -> l p k f", p=P)
        column = {"u": 0, "q": 512, "f": 1024, "v": 1536, "g": 2048, "gate": 2560}
        ups = {"pool_up": pool_up.rearrange("l (k p) d -> l p k d", p=P),
               "hgrn_up": hgrn_up.rearrange("l (k p) d -> l p k d", p=P)}
        w_out_v = w_out.rearrange("l (k p) d -> l p k d", p=P)

        def slot_kf(s, width=GROUP):
            return ring[:, s, 0:KT * width].rearrange("p (k f) -> p k f", k=KT)

        def slot_fd(s, tiles=GT):
            return ring[:, s, 0:tiles * D].rearrange("p (f d) -> p f d", d=D)

        block = ctx.enter_context(nc.Block())

        @block.sync
        def _(sp):
            def freed(n):
                kind, key = CHUNKS[n][3], CHUNKS[n][4]
                if kind == "down":
                    sp.wait_ge(down_done, key)
                else:
                    done(sp, JOB[key])

            sp.dma_start(x_tok, x[0].rearrange("(a p) d -> p a d", p=P)).then_inc(x_landed, 16)
            for n, (name, l, c, _, _) in enumerate(CHUNKS):
                if n >= RING:
                    freed(n - RING)
                s = n % RING
                if name in column:
                    a = column[name] + c * GROUP
                    sp.dma_start(slot_kf(s), w_in_v[l, :, :, a:a + GROUP]).then_inc(landed[s], 16)
                elif name in ups:
                    sp.dma_start(slot_fd(s), ups[name][l]).then_inc(landed[s], 16)
                elif name == "w_out":
                    sp.dma_start(slot_kf(s), w_out_v[l, :, :, c * GROUP:(c + 1) * GROUP]).then_inc(landed[s], 16)
                elif name == "dense_d":
                    a = c * GROUP
                    sp.dma_start(slot_fd(s, DENSE[c]),
                                 dense_w_down[0, a:a + DENSE[c] * P, :].rearrange("(f p) d -> p f d", p=P)
                                 ).then_inc(landed[s], 16)
                else:
                    w = dense_w_gate if name == "dense_g" else dense_w_up
                    a, width = c * GROUP, DENSE[c] * P
                    sp.dma_start(slot_kf(s, width),
                                 w[0, :, a:a + width].rearrange("(k p) f -> p k f", p=P)).then_inc(landed[s], 16)

            def load_item(it, e, after_loop_start):
                for c, (kind, i) in enumerate(MOE):
                    n = C_LOOP + c
                    s = n % RING
                    if c >= RING or after_loop_start:
                        back = 0 if c >= RING else 1
                        pk, pi = MOE[(c - RING) % ITEM_CHUNKS]
                        if pk == "d":
                            sp.wait_ge(down_done, it * len(EXPERT) + (DN_LOOP + pi + 1 - back * len(EXPERT)))
                        else:
                            sp.wait_ge(job_done, it * ITEM_JOBS + (J_LOOP + GT * (pi + 1) - back * ITEM_JOBS))
                    else:
                        freed(n - RING)
                    a = i * GROUP
                    if kind == "d":
                        src = moe_w_down[0, bass.ds(e, 1), a:a + GROUP, :].rearrange("o (f p) d -> p (o f) d", p=P)
                        sp.dma_start(slot_fd(s), src).then_inc(landed[s], 16)
                    else:
                        w = moe_w_gate if kind == "g" else moe_w_up
                        src = w[0, bass.ds(e, 1), :, a:a + GROUP].rearrange("o (k p) f -> p (o k) f", p=P)
                        sp.dma_start(slot_kf(s), src).then_inc(landed[s], 16)

            load_item(0, 0, False)
            with sp.Fori(1, N_EXP) as it:
                load_item(it, it, True)
            sp.wait_ge(tables_ready, 1)
            n = sp.value_load(n_items[0:1, 0:1], min_val=N_EXP, max_val=ITEMS)
            with sp.If(n > N_EXP):
                with sp.Fori(N_EXP, n) as it:
                    e = sp.value_load(item_e[0:1, bass.ds(it, 1)], min_val=0, max_val=N_EXP - 1)
                    load_item(it, e, True)
            for a in range(TH):
                sp.wait_ge(fin_ready, a + 1)
                sp.dma_start(out[0, a * P:(a + 1) * P, :], h_tok[:, a, :]).then_inc(stored, 16)
            sp.wait_ge(stored, 16 * TH)

        @block.gpsimd
        def _(pool):
            steps = [0]

            def step(ins):
                steps[0] += 1
                ins.then_inc(pool_step, 1)

            def settle():
                pool.wait_ge(pool_step, steps[0])

            g = nc.gpsimd
            step(g.memset(ident[:], 0.0))
            step(g.memset(mean_d[:], 1.0 / D))
            step(g.memset(mean_h[:], 1.0 / P))
            step(g.memset(ones[:], 1.0))
            step(g.memset(before[:], 1.0))
            step(g.memset(scan_keep[:], 1.0))
            step(g.memset(masks[:], 0.0))
            step(g.memset(eps[:], EPS))
            step(g.iota(iota_e[:], pattern=[[1, N_EXP]], base=0, channel_multiplier=0,
                        allow_small_or_imprecise_dtypes=True))
            step(g.iota(iota_c[:], pattern=[[1, CAP]], base=0, channel_multiplier=0,
                        allow_small_or_imprecise_dtypes=True))
            step(g.iota(iota_j[:], pattern=[[1, COLS], [0, N_EXP]], base=0, channel_multiplier=0,
                        allow_small_or_imprecise_dtypes=True))
            step(g.iota(inv_pos[:], pattern=[[0, POOL_TILES], [1, PAD]], base=1, channel_multiplier=0,
                        allow_small_or_imprecise_dtypes=True))
            settle()
            step(g.affine_select(out=ident[:], in_=ident[:], compare_op=ALU.not_equal, fill=1.0, base=0,
                                 pattern=[[-1, P]], channel_multiplier=1))
            step(g.affine_select(out=before[:], in_=before[:], compare_op=ALU.is_gt, fill=0.0, base=0,
                                 pattern=[[1, P]], channel_multiplier=-1))
            step(g.memset(scan_keep[:].rearrange("p (a t) -> p a t", a=TH)[:, :, 0:1], 0.0))
            for m, h in enumerate(LEVELS[2:]):
                step(g.memset(masks[:, m, :].rearrange("p (b r) -> p b r", r=2 * h)[:, :, h:], 1.0))
            settle()
            for m, h in enumerate(LEVELS[2:]):
                v = masks[:, m, :].rearrange("p (b r) -> p b r", r=2 * h)
                step(g.affine_select(out=v, in_=v, compare_op=ALU.is_ge, fill=0.0, base=0,
                                     pattern=[[-2 * h, P // (2 * h)], [0, 2 * h]], channel_multiplier=1))
            settle()
            for m, h in enumerate(LEVELS[2:]):
                v = masks[:, m, :].rearrange("p (b r) -> p b r", r=2 * h)
                step(g.affine_select(out=v, in_=v, compare_op=ALU.is_ge, fill=0.0, base=h - 1,
                                     pattern=[[2 * h, P // (2 * h)], [0, 2 * h]], channel_multiplier=-1))
            settle()
            g.memset(fin[:], 0.0).then_inc(consts, 1)
            for l in range(DEPTH):
                for j in range(4):
                    taken(pool, JOB["u", l, j])
                for buf in (pu, pb, pc):
                    step(g.memset(buf[:, :, 0:PAD], 0.0))
                settle()
                span = {1: (pu, pb, 0), 2: (pb, pc, 1), 4: (pc, pb, 2), 8: (pb, pc, 3)}
                for shift, (src, dst, first) in span.items():
                    a = src[:, first:, PAD:]
                    b = src[:, first:, PAD - shift:PAD - shift + T]
                    ins = g.tensor_tensor(dst[:, first:, PAD:], a, b, ALU.add)
                    if shift == 8:
                        ins.then_inc(win_ready, 1)
                    else:
                        step(ins)
                        settle()

        @block.scalar
        def _(act):
            for src, a, n in ((attn_norm_w.rearrange("l (k p) -> (l k) p", p=P), C_ATTN, 16),
                              (ffn_norm_w.rearrange("l (k p) -> (l k) p", p=P), C_FFN, 16),
                              (gate_bias.rearrange("l (k p) -> (l k) p", p=P), C_BIAS, 32),
                              (pool_scale.rearrange("l (k p) -> (l k) p", p=P), C_PSCALE, 8),
                              (hgrn_lower_bounds.rearrange("l (k p) -> (l k) p", p=P), C_LB, 8),
                              (hgrn_norm_w, C_HNORM, 2)):
                act.dma_start(rows[a:a + n, :], src).then_inc(params_landed, 16)
            act.dma_start(poolw[:], pool_w.rearrange("l g c d -> c l g d")).then_inc(poolw_landed, 16)
            act.dma_start(router[:], moe_router[0].rearrange("(k p) e -> p k e", p=P)).then_inc(router_landed, 16)
            act.wait_ge(consts, 1)

            def bank(n):
                return job_bank[n % 4]

            for i in range(4):
                n = JOB["x_in", i]
                done(act, n)
                a, k0 = i // 2, 4 * (i % 2)
                nc.scalar.activation(xT[:, k0:k0 + 4, a * P:(a + 1) * P],
                                     bank(n)[:].rearrange("p (k t) -> p k t", k=4), ACT.Copy
                                     ).then_inc(job_taken[n % 4], 1)
            act.wait_ge(lb_max_ready, 1)
            nc.scalar.activation(lb_tmp[:, 0:2, :], lb[:, :, :], ACT.Exp).then_inc(lb_exp_ready, 1)

            def norm(l, w):
                for half in range(2):
                    ks = slice(4 * half, 4 * half + 4)
                    if w == 1:
                        for j in range(4):
                            taken(act, JOB["w_out", l, 4 * half + j])
                    elif l == 0:
                        for i in range(4):
                            taken(act, JOB["x_in", i])
                    else:
                        act.wait_ge(x_ready, 2 * half + 2)
                    nc.scalar.activation(sq[:, ks, :], xT[:, ks, :], ACT.Square).then_inc(sq_ready, 1)
                n = JOB["norm", l, w]
                done(act, n)
                nc.scalar.activation(rms_ln[:], bank(n)[:, 0:T], ACT.Ln, bias=eps[:, 0:1]
                                     ).then_inc(job_taken[n % 4], 1)
                taken(act, n)
                nc.scalar.activation(rstd[:], rms_ln[:], ACT.Exp, scale=-0.5).then_inc(rstd_ready, 1)

            def tanh_half(n):
                done(act, n)
                nc.scalar.activation(th[:, n % 4, :], bank(n)[:, 0:T], ACT.Tanh, scale=0.5).then_inc(th_ready, 1)

            for l in range(DEPTH):
                norm(l, 0)
                for j in range(HEADS):
                    n = JOB["f", l, j]
                    done(act, n)
                    nc.scalar.activation(expf[:, j, :], bank(n)[:, 0:T], ACT.Exp, scale=-1.0
                                         ).then_inc(job_taken[n % 4], 1)
                for j in range(HEADS):
                    tanh_half(JOB["q", l, j])
                for a in range(TH):
                    n = JOB["v", l, a]
                    done(act, n)
                    nc.scalar.activation(v_tok[:, a, :], bank(n)[:], ACT.Copy).then_inc(job_taken[n % 4], 1)
                act.wait_ge(forget_ready, HEADS * (l + 1))
                nc.scalar.activation(sig, sig, ACT.Ln).then_inc(logf_ready, 1)
                for j in range(POOL_TILES):
                    n = JOB["u", l, j]
                    done(act, n)
                    nc.scalar.activation(pu[:, j, PAD:], bank(n)[:, 0:T], ACT.Copy).then_inc(job_taken[n % 4], 1)
                for j in range(HEADS):
                    tanh_half(JOB["g", l, j])
                for j in range(POOL_TILES):
                    n = JOB["mix", l, j]
                    c = C_PSCALE + POOL_TILES * l + j
                    done(act, n)
                    nc.scalar.activation(mixed[:, j, :], bank(n)[:, 0:T], ACT.Copy, scale=cols[:, c:c + 1]
                                         ).then_inc(job_taken[n % 4], 1)
                for j in range(16):
                    n = JOB["gate", l, j]
                    done(act, n)
                    c = 16 * l + j
                    nc.scalar.activation(gates[:, j, :], bank(n)[:, 0:T], ACT.Tanh, scale=0.5,
                                         bias=half_bias[:, c:c + 1]).then_inc(job_taken[n % 4], 1)
                    if j % 2:
                        lev = j // 2 + 1
                        act.wait_ge(arg_ready, 2 * ((NL - 1) * l + lev))
                        nc.scalar.activation(e_mem[:, lev % 2, :], e_mem[:, lev % 2, :], ACT.Exp
                                             ).then_inc(exp_ready, 1)
                for i in range(2):
                    act.wait_ge(o_done, 2 * l + i + 1)
                    nc.scalar.activation(o_sq[:, i * 512:(i + 1) * 512], acc[i][:], ACT.Square
                                         ).then_inc(o_sq_ready, 1)
                for i in range(2):
                    act.wait_ge(o_mean_done, 2 * l + i + 1)
                    nc.scalar.activation(e_mem[:, 0, i * 512:(i + 1) * 512], acc[2 + i][:], ACT.Ln,
                                         bias=eps[:, 0:1]).then_inc(o_ln, 1)
                for i in range(2):
                    act.wait_ge(o_ln, 2 * l + i + 1)
                    nc.scalar.activation(e_mem[:, 0, i * 512:(i + 1) * 512], e_mem[:, 0, i * 512:(i + 1) * 512],
                                         ACT.Exp, scale=-0.5).then_inc(o_rstd_ready, 1)
                norm(l, 1)
                if l == 0:
                    for j in range(sum(DENSE)):
                        tanh_half(JOB["ffn", j])

            for name, dst in (("h_tok", h_tok), ("x_tok", x_tok)):
                for i in range(4):
                    n = JOB[name, i]
                    done(act, n)
                    nc.scalar.activation(dst[:, i // 2, (i % 2) * 512:(i % 2) * 512 + 512], bank(n)[:], ACT.Copy
                                         ).then_inc(job_taken[n % 4], 1)
                if name == "h_tok":
                    act.wait_ge(gap_ready, 1)
                    nc.scalar.activation(gap_e, gap, ACT.Exp).then_inc(gap_exp_ready, 1)
            act.dma_start(hT_mem[:, 0:D], final_norm_w.rearrange("(o d) -> o d", o=1).to_broadcast([P, D])
                          ).then_inc(fnw_landed, 16)

            act.wait_ge(tables_ready, 1)
            n_reg = act.value_load(n_items[0:1, 0:1], min_val=N_EXP, max_val=ITEMS)
            with act.Fori(0, n_reg) as it:
                for f in range(sum(EXPERT)):
                    b = (J_LOOP + f) % 4
                    done_i(act, f, it)
                    nc.scalar.activation(th[:, b, 0:CAP], job_bank[b][:, 0:CAP], ACT.Tanh, scale=0.5
                                         ).then_inc(th_ready, 1)
                act.wait_ge(down_done, it * len(EXPERT) + (DN_LOOP + len(EXPERT)))
                nc.scalar.activation(yT[:, 4:8, :], acc[1][:, 0:4 * CAP].rearrange("p (k c) -> p k c", k=4),
                                     ACT.Copy).then_inc(yT_act, 1)
                act.wait_ge(y_turned, it * 2 + 2)
                nc.scalar.activation(y_tok[:, 512:1024], acc[3][0:CAP, :], ACT.Copy).then_inc(y_act, 1)

            for a in range(TH):
                for q in range(2):
                    n = J_LOOP + sum(EXPERT) + 2 * a + q
                    act.wait_ge(job_taken[n % 4], n_reg * (ITEM_JOBS // 4) + (n // 4 + 1 - ITEM_JOBS // 4))
                nc.scalar.activation(hT_mem[:, D:2 * D], x_tok[:, a, :], ACT.Square,
                                     accum_out=fin[:, a:a + 1]).then_inc(fin_sq, 1)
                act.wait_ge(fin_sq, a + 1)
            nc.scalar.activation(fin[:, 2:4], fin[:, 0:2], ACT.Ln, scale=1.0 / D, bias=eps[:, 0:1]).then_inc(fin_ln, 1)
            act.wait_ge(fin_ln, 1)
            nc.scalar.activation(fin[:, 4:6], fin[:, 2:4], ACT.Exp, scale=-0.5).then_inc(fin_rstd, 1)

        @block.vector
        def _(dve):
            v = nc.vector
            steps = [0]

            def step(ins):
                steps[0] += 1
                ins.then_inc(dve_step, 1)

            def settle():
                dve.wait_ge(dve_step, steps[0])

            def bank(n):
                return job_bank[n % 4]

            dve.wait_ge(consts, 1)
            for g, w in enumerate(WINDOWS):
                step(v.tensor_scalar(inv_pos[:, g, :], inv_pos[:, g, :], float(w), None, ALU.min))
            settle()
            step(v.reciprocal(inv_pos[:], inv_pos[:]))
            n = JOB["params"]
            done(dve, n)
            v.tensor_copy(cols[:], bank(n)[:, 0:C_ROWS]).then_inc(job_taken[n % 4], 1)
            taken(dve, n)
            step(v.tensor_scalar(half_bias[:], cols[:, C_BIAS:C_BIAS + 32], 0.5, None, ALU.mult))
            step(v.tensor_scalar(half_hnorm[:], cols[:, C_HNORM:C_HNORM + DEPTH], 0.5, None, ALU.mult))
            l0, l1 = cols[:, C_LB:C_LB + HEADS], cols[:, C_LB + HEADS:C_LB + 2 * HEADS]
            step(v.tensor_tensor(lb_tmp[:, 2, :], l0, l1, ALU.max))
            settle()
            step(v.tensor_tensor(lb[:, 0, :], l0, lb_tmp[:, 2, :], ALU.subtract))
            v.tensor_tensor(lb[:, 1, :], l1, lb_tmp[:, 2, :], ALU.subtract).then_inc(lb_max_ready, 1)
            dve.wait_ge(lb_exp_ready, 1)
            step(v.tensor_tensor(lb_tmp[:, 2, :], lb_tmp[:, 0, :], lb_tmp[:, 1, :], ALU.add))
            settle()
            step(v.reciprocal(lb_tmp[:, 3, :], lb_tmp[:, 2, :]))
            settle()
            step(v.tensor_tensor(lb_tmp[:, 0, :], lb_tmp[:, 0, :], lb_tmp[:, 3, :], ALU.mult))
            step(v.tensor_tensor(lb_tmp[:, 1, :], lb_tmp[:, 1, :], lb_tmp[:, 3, :], ALU.mult))
            settle()
            step(v.tensor_tensor(lb[:, 0, :], lb_tmp[:, 0, :], lb_tmp[:, 0, :], ALU.subtract))
            step(v.tensor_tensor(lb[:, 1, :], lb_tmp[:, 0, :], lb_tmp[:, 1, :], ALU.add))
            settle()
            step(v.tensor_tensor(lb[:, 1, :], lb[:, 1, :], lb_tmp[:, 0, :], ALU.subtract))
            settle()
            step(v.tensor_scalar(lb[:], lb[:], 0.0, LB_CEIL, ALU.max, ALU.min))
            settle()
            step(v.tensor_scalar(lb_floor[:], lb[:], LB_FLOOR, None, ALU.max))
            step(v.tensor_scalar(one_lb[:], lb[:], -1.0, 1.0, ALU.mult, ALU.add))
            settle()
            v.tensor_scalar(half_one_lb[:], one_lb[:], 0.5, None, ALU.mult).then_inc(params_ready, 1)

            def norm(l, w):
                dve.wait_ge(rstd_ready, 2 * l + w + 1)
                for k in range(KT):
                    c = (C_FFN if w else C_ATTN) + KT * l + k
                    v.scalar_tensor_tensor(out=hT[:, k, :], in0=xT[:, k, :], scalar=cols[:, c:c + 1], in1=rstd[:],
                                           op0=ALU.mult, op1=ALU.mult).then_inc(h_ready, 1)

            def twice_silu(dst, name, l, j):
                n = JOB[name, l, j]
                dve.wait_ge(th_ready, TH_OF[name, l, j] + 1)
                v.scalar_tensor_tensor(out=dst, in0=th[:, n % 4, :], scalar=1.0, in1=bank(n)[:, 0:T],
                                       op0=ALU.add, op1=ALU.mult).then_inc(job_taken[n % 4], 1)

            for l in range(DEPTH):
                norm(l, 0)
                if l == 0:
                    dve.wait_ge(params_ready, 1)
                for j in range(HEADS):
                    taken(dve, JOB["f", l, j])
                    step(v.tensor_scalar(expf[:, j, :], expf[:, j, :], EXP_CEIL, None, ALU.min))
                    settle()
                    step(v.tensor_scalar(sig[:, j, :], expf[:, j, :], 1.0, None, ALU.add))
                    settle()
                    step(v.reciprocal(sig[:, j, :], sig[:, j, :]))
                    settle()
                    v.scalar_tensor_tensor(out=kT[:, j, :], in0=expf[:, j, :], scalar=half_one_lb[:, l, j:j + 1],
                                           in1=sig[:, j, :], op0=ALU.mult, op1=ALU.mult).then_inc(key_ready, 1)
                    v.tensor_scalar(sig[:, j, :], sig[:, j, :], one_lb[:, l, j:j + 1], lb_floor[:, l, j:j + 1],
                                    ALU.mult, ALU.add).then_inc(forget_ready, 1)
                for j in range(HEADS):
                    twice_silu(qT[:, j, :], "q", l, j)
                dve.wait_ge(logf_ready, l + 1)
                for j in range(HEADS):
                    v.tensor_tensor_scan(G[:, j, :], scan_keep[:], sig[:, j, :], 0.0, ALU.mult, ALU.add
                                         ).then_inc(gsum_ready, 1)
                dve.wait_ge(gsum_ready, HEADS * (l + 1))
                dve.wait_ge(key_ready, HEADS * (l + 1))

                def blocks(t, h):
                    return t.rearrange("p h t -> p (h t)").rearrange("p (b s r) -> p b s r", s=2, r=h)

                def scaled(lev):
                    return e_mem[:, lev % 2, :].rearrange("p (h t) -> p h t", h=HEADS)

                def arguments(lev):
                    if lev >= 3:
                        dve.wait_ge(level_done, NL * l + lev - 1)
                    h = P if LEVELS[lev] == "cross" else LEVELS[lev]
                    gb, eb = blocks(G[:], h), blocks(scaled(lev), h)
                    ref = gb[:, :, 0, h - 1:h].to_broadcast([P, HEADS * T // (2 * h), h])
                    v.tensor_tensor(eb[:, :, 0, :], ref, gb[:, :, 0, :], ALU.subtract).then_inc(arg_ready, 1)
                    if LEVELS[lev] == "cross":
                        v.tensor_copy(eb[:, :, 1, :], gb[:, :, 1, :]).then_inc(arg_ready, 1)
                    else:
                        v.tensor_tensor(eb[:, :, 1, :], gb[:, :, 1, :], ref, ALU.subtract).then_inc(arg_ready, 1)

                def scale_qk(lev):
                    dve.wait_ge(exp_ready, (NL - 1) * l + lev)
                    h = P if LEVELS[lev] == "cross" else LEVELS[lev]
                    eb, kb, qb = blocks(scaled(lev), h), blocks(kT, h), blocks(qT, h)
                    v.tensor_tensor(eb[:, :, 0, :], eb[:, :, 0, :], kb[:, :, 0, :], ALU.mult).then_inc(scaled_ready, 1)
                    v.tensor_tensor(eb[:, :, 1, :], eb[:, :, 1, :], qb[:, :, 1, :], ALU.mult).then_inc(scaled_ready, 1)

                def take(lev):
                    dve.wait_ge(level_done, NL * l + lev + 1)
                    pair = acc[2 * (lev % 2)], acc[2 * (lev % 2) + 1]
                    if LEVELS[lev] == "cross":
                        v.tensor_copy(score_x.rearrange("p h t -> p (h t)"), pair[0][:]).then_inc(level_taken, 2)
                        return
                    m = ident[:, :] if LEVELS[lev] == "diag" else masks[:, lev - 2, :]
                    m = m.unsqueeze(1).to_broadcast([P, HEADS, P])
                    if lev:
                        dve.wait_ge(level_taken, 2 * (NL * l + lev))
                    for a in range(TH):
                        ps = pair[a][:].rearrange("p (h t) -> p h t", h=HEADS)
                        dst = score if LEVELS[lev] == "diag" else masked
                        ins = v.tensor_tensor(dst[:, a], ps, m, ALU.mult)
                        if LEVELS[lev] == "diag":
                            ins.then_inc(level_taken, 1)
                        else:
                            step(ins)
                    if LEVELS[lev] != "diag":
                        settle()
                        for a in range(TH):
                            v.tensor_tensor(score[:, a], score[:, a], masked[:, a], ALU.add).then_inc(level_taken, 1)

                arguments(1)
                for j in range(HEADS):
                    twice_silu(og[:, j, :], "g", l, j)
                dve.wait_ge(win_ready, l + 1)
                step(v.tensor_tensor(pool_head[:, 0::2, :], pb[:, 0::2, PAD:2 * PAD], inv_pos[:, 0::2, :], ALU.mult))
                step(v.tensor_tensor(pool_head[:, 1::2, :], pc[:, 1::2, PAD:2 * PAD], inv_pos[:, 1::2, :], ALU.mult))
                settle()
                v.tensor_tensor(pu[:, :, PAD:2 * PAD], pool_head[:], pu[:, :, PAD:2 * PAD], ALU.subtract
                                ).then_inc(pooled_ready, 1)
                for g, w in enumerate(WINDOWS):
                    src = (pb, pc)[g % 2]
                    v.scalar_tensor_tensor(out=pu[:, g, 2 * PAD:], in0=src[:, g, 2 * PAD:], scalar=1.0 / w,
                                           in1=pu[:, g, 2 * PAD:], op0=ALU.mult, op1=ALU.subtract
                                           ).then_inc(pooled_ready, 1)
                for j in range(HEADS):
                    taken(dve, JOB["q", l, j])
                for lev in range(1, NL):
                    scale_qk(lev)
                    if lev + 1 < NL:
                        arguments(lev + 1)
                    take(lev - 1)
                take(NL - 1)

                def y_pool_jobs(which):
                    for d in which:
                        n = JOB["y_pool", l, d]
                        done(dve, n)
                        v.scalar_tensor_tensor(out=merged[:, d, :], in0=gates[:, d, :], scalar=1.0,
                                               in1=bank(n)[:, 0:T], op0=ALU.add, op1=ALU.mult
                                               ).then_inc(job_taken[n % 4], 1)

                y_pool_jobs(range(4))
                for i in range(2):
                    dve.wait_ge(o_sq_ready, 2 * l + i + 1)
                    step(v.tensor_copy(hT_mem[:, i * 512:(i + 1) * 512], acc[i][:]))
                settle()
                y_pool_jobs(range(4, KT))
                for i in range(2):
                    part = hT_mem[:, i * 512:(i + 1) * 512]
                    dve.wait_ge(o_rstd_ready, 2 * l + i + 1)
                    step(v.scalar_tensor_tensor(out=part, in0=part, scalar=half_hnorm[:, l:l + 1],
                                                in1=e_mem[:, 0, i * 512:(i + 1) * 512], op0=ALU.mult, op1=ALU.mult))
                for j in range(HEADS):
                    taken(dve, JOB["g", l, j])
                settle()
                for i in range(2):
                    part = hT_mem[:, i * 512:(i + 1) * 512]
                    v.tensor_tensor(part, part, og_mem[:, i * 512:(i + 1) * 512], ALU.mult).then_inc(o_ready, 1)
                for d in range(KT):
                    n = JOB["y_hgrn", l, d]
                    done(dve, n)
                    v.scalar_tensor_tensor(out=gates[:, KT + d, :], in0=gates[:, KT + d, :], scalar=1.0,
                                           in1=bank(n)[:, 0:T], op0=ALU.add, op1=ALU.mult
                                           ).then_inc(job_taken[n % 4], 1)
                    taken(dve, n)
                    taken(dve, JOB["y_pool", l, d])
                    v.tensor_tensor(merged[:, d, :], merged[:, d, :], gates[:, KT + d, :], ALU.add
                                    ).then_inc(merged_ready, 1)
                for d in range(KT):
                    n = JOB["w_out", l, d]
                    done(dve, n)
                    v.scalar_tensor_tensor(out=xT[:, d, :], in0=bank(n)[:, 0:T], scalar=0.5, in1=xT[:, d, :],
                                           op0=ALU.mult, op1=ALU.add).then_inc(job_taken[n % 4], 1)
                for d in range(KT):
                    taken(dve, JOB["w_out", l, d])
                norm(l, 1)
                if l == 0:
                    tile = 0
                    for i, tiles in enumerate(DENSE):
                        for f in range(tiles):
                            n = JOB["ffn", tile]
                            dve.wait_ge(th_ready, TH_OF["ffn", tile] + 1)
                            if i >= 2:
                                dve.wait_ge(down_done, i - 1)
                            v.scalar_tensor_tensor(out=th[:, n % 4, :], in0=th[:, n % 4, :], scalar=1.0,
                                                   in1=bank(n)[:, 0:T], op0=ALU.add, op1=ALU.mult
                                                   ).then_inc(silu_half, 1)
                            tile += 1
                            dve.wait_ge(silu_half, tile)
                            v.scalar_tensor_tensor(out=hid[:, i % 2, f, :], in0=th[:, n % 4, :], scalar=0.5,
                                                   in1=bank(n)[:, T:2 * T], op0=ALU.mult, op1=ALU.mult
                                                   ).then_inc(job_taken[n % 4], 1)
                    dve.wait_ge(down_done, len(DENSE))
                    for i in range(4):
                        v.tensor_tensor(xT[:, 2 * i:2 * i + 2, :], acc[i][:].rearrange("p (d t) -> p d t", d=2),
                                        xT[:, 2 * i:2 * i + 2, :], ALU.add).then_inc(x_ready, 1)
                    dve.wait_ge(x_ready, 4)

            n = JOB["logits"]
            done(dve, n)
            v.tensor_copy(lg, bank(n)[:, 0:16].rearrange("p (a e) -> p a e", a=TH)).then_inc(job_taken[n % 4], 1)
            taken(dve, n)
            for a in range(TH):
                step(v.max(top_v[:, a, :], lg[:, a, :]))
            settle()
            for a in range(TH):
                step(v.max_index(top_i[:, a, :], top_v[:, a, :], lg[:, a, :]))
            v.tensor_tensor(gap, top_v[:, :, 1], top_v[:, :, 0], ALU.subtract).then_inc(gap_ready, 1)
            settle()
            step(v.tensor_copy(top_f, top_i[:]))
            settle()
            for a in range(TH):
                step(v.tensor_scalar(hot1[:, a, :], iota_e[:], top_f[:, a, 0:1], None, ALU.is_equal))
                step(v.tensor_scalar(hot2[:, a, :], iota_e[:], top_f[:, a, 1:2], None, ALU.is_equal))
            settle()
            v.tensor_tensor(chosen, hot1, hot2, ALU.add).then_inc(chosen_ready, 1)
            dve.wait_ge(gap_exp_ready, 1)
            step(v.tensor_scalar(gap_1, gap_e, 1.0, None, ALU.add))
            settle()
            step(v.reciprocal(w1, gap_1))
            settle()
            step(v.tensor_tensor(w2, w1, gap_e, ALU.mult))
            settle()
            for a in range(TH):
                step(v.tensor_scalar(wt1[:, a, :], hot1[:, a, :], w1[:, a:a + 1], None, ALU.mult))
                step(v.tensor_scalar(wt2[:, a, :], hot2[:, a, :], w2[:, a:a + 1], None, ALU.mult))
            settle()
            step(v.tensor_tensor(comb, wt1, wt2, ALU.add))
            step(v.memset(ones8, 1.0))
            n = JOB["ranks"]
            done(dve, n)
            step(v.tensor_scalar(rank1, bank(n)[:, 0:16].rearrange("p (a e) -> p a e", a=TH), 1.0, None, ALU.add))
            v.tensor_copy(count, bank(n)[:, 16:24]).then_inc(job_taken[n % 4], 1)
            settle()
            taken(dve, n)
            dve.wait_ge(chosen_ready, 1)
            step(v.tensor_tensor(rank1, rank1, chosen, ALU.mult))
            step(v.tensor_scalar(over1, count, float(CAP), None, ALU.is_gt))
            step(v.tensor_scalar(over2, count, 2.0 * CAP, None, ALU.is_gt))
            settle()
            step(v.tensor_scalar(rank1, rank1, -1.0, None, ALU.add))
            step(v.tensor_tensor(over, over1, over2, ALU.add))
            settle()
            step(v.tensor_tensor_scan(cum, ones8, over, 0.0, ALU.mult, ALU.add))
            settle()
            step(v.scalar_tensor_tensor(out=start, in0=cum, scalar=float(N_EXP), in1=over, op0=ALU.add,
                                        op1=ALU.subtract))
            step(v.tensor_scalar(n_f, cum[:, 7:8], float(N_EXP), None, ALU.add))
            settle()
            step(v.tensor_scalar(start1, start, 1.0, None, ALU.add))
            step(v.tensor_copy(n_items[:], n_f))

            def over_items(t):
                return t.unsqueeze(1).to_broadcast([P, COLS, N_EXP])

            settle()
            step(v.tensor_tensor(hot, iota_j[:], over_items(iota_e[:]), ALU.is_equal))
            step(v.tensor_tensor(one1, iota_j[:], over_items(start), ALU.is_equal))
            step(v.tensor_tensor(one2, iota_j[:], over_items(start1), ALU.is_equal))
            settle()
            step(v.tensor_tensor(one1, one1, over_items(over1), ALU.mult))
            step(v.tensor_tensor(one2, one2, over_items(over2), ALU.mult))
            settle()
            step(v.tensor_tensor(hot, hot, one1, ALU.add))
            step(v.tensor_reduce(base1, one1, AX_X, ALU.add))
            step(v.tensor_reduce(base2, one2, AX_X, ALU.add))
            settle()
            step(v.tensor_tensor(hot, hot, one2, ALU.add))
            step(v.scalar_tensor_tensor(out=base, in0=base2, scalar=2.0, in1=base1, op0=ALU.mult, op1=ALU.add))
            settle()
            step(v.tensor_scalar(base, base, float(CAP), None, ALU.mult))
            step(v.tensor_tensor(prod[:, 0], hot, over_items(iota_e[:]), ALU.mult))
            settle()
            step(v.tensor_reduce(e_f, prod[:, 0], AX_X, ALU.add))
            for a in range(TH):
                step(v.tensor_tensor(prod[:, 1 + a], hot, over_items(rank1[:, a, :]), ALU.mult))
            settle()
            step(v.tensor_copy(item_e[:], e_f))
            for a in range(TH):
                step(v.tensor_reduce(pos_item[:, a, :], prod[:, 1 + a], AX_X, ALU.add))
            settle()
            for a in range(TH):
                step(v.tensor_tensor(pos_item[:, a, :], pos_item[:, a, :], base, ALU.subtract))
                step(v.tensor_tensor(prod[:, 1 + a], hot, over_items(comb[:, a, :]), ALU.mult))
            settle()
            for a in range(TH):
                step(v.tensor_reduce(w_item[:, a, :], prod[:, 1 + a], AX_X, ALU.add))
            settle()
            v.memset(gap, 0.0).then_inc(tables_ready, 1)

            for a in range(TH):
                v.tensor_scalar(sel[:, a, :], iota_c[:], pos_item[:, a, 0:1], None, ALU.is_equal).then_inc(sel_ready, 1)

            def take_gathered():
                for i in range(2):
                    v.tensor_copy(hTe[:, 4 * i:4 * i + 4, :], acc[2 + i][:, 0:4 * CAP].rearrange("p (k c) -> p k c", k=4)
                                  ).then_inc(hTe_ready, 1)

            dve.wait_ge(gathered, 1)
            v.memset(sel_wT[:, 0, :], 0.0).then_inc(hTe_ready, 1)
            v.memset(sel_wT[:, 1, :], 0.0).then_inc(hTe_ready, 1)
            take_gathered()
            n_reg = dve.value_load(n_items[0:1, 0:1], min_val=N_EXP, max_val=ITEMS)
            with dve.Fori(0, n_reg) as it:
                dve.wait_ge(gathered, it + 1)
                dve.wait_ge(sel_ready, it * 4 + 2)
                for a in range(TH):
                    v.tensor_scalar(sel[:, a, :], iota_c[:], pos_item[:, a, bass.ds(it + 1, 1)], None, ALU.is_equal
                                    ).then_inc(sel_ready, 1)
                    v.tensor_scalar(sel_w[:, a, :], iota_c[:], pos_item[:, a, bass.ds(it, 1)],
                                    w_item[:, a, bass.ds(it, 1)], ALU.is_equal, ALU.mult).then_inc(sel_ready, 1)
                tile = 0
                for i, tiles in enumerate(EXPERT):
                    for f in range(tiles):
                        b = (J_LOOP + tile) % 4
                        dve.wait_ge(th_ready, it * sum(EXPERT) + (TH_LOOP + tile + 1))
                        if f == 0:
                            dve.wait_ge(down_done, it * len(EXPERT) + (DN_LOOP + max(i - 1, 0)))
                        v.scalar_tensor_tensor(out=th[:, b, 0:CAP], in0=th[:, b, 0:CAP], scalar=1.0,
                                               in1=job_bank[b][:, 0:CAP], op0=ALU.add, op1=ALU.mult
                                               ).then_inc(silu_half, 1)
                        tile += 1
                        dve.wait_ge(silu_half, it * sum(EXPERT) + (sum(DENSE) + tile))
                        v.scalar_tensor_tensor(out=hid_e[:, i % 2, f, :], in0=th[:, b, 0:CAP], scalar=0.5,
                                               in1=job_bank[b][:, CAP:2 * CAP], op0=ALU.mult, op1=ALU.mult
                                               ).then_inc(job_taken[b], 1)
                dve.wait_ge(gathered, it + 2)
                done_i(dve, sum(EXPERT) - 1, it)
                for a in range(TH):
                    v.tensor_copy(sel_wT[:, a, :], acc[2 + a][0:CAP, 4 * CAP:4 * CAP + P]).then_inc(hTe_ready, 1)
                take_gathered()
                dve.wait_ge(down_done, it * len(EXPERT) + (DN_LOOP + len(EXPERT)))
                v.tensor_copy(yT[:, 0:4, :], acc[0][:, 0:4 * CAP].rearrange("p (k c) -> p k c", k=4)).then_inc(yT_dve, 1)
                dve.wait_ge(y_turned, it * 2 + 1)
                v.tensor_copy(y_tok[:, 0:512], acc[2][0:CAP, :]).then_inc(y_dve, 1)
                for q in range(4):
                    jj = sum(EXPERT) + q
                    b = (J_LOOP + jj) % 4
                    done_i(dve, jj, it)
                    taken_i(dve, jj - 4, it)
                    dst = x_tok[:, q // 2, (q % 2) * 512:(q % 2) * 512 + 512]
                    v.tensor_tensor(dst, job_bank[b][:], dst, ALU.add).then_inc(job_taken[b], 1)

            dve.wait_ge(fin_rstd, 1)
            dve.wait_ge(fnw_landed, 16)
            for a in range(TH):
                v.scalar_tensor_tensor(out=h_tok[:, a, :], in0=x_tok[:, a, :], scalar=fin[:, 4 + a:5 + a],
                                       in1=hT_mem[:, 0:D], op0=ALU.mult, op1=ALU.mult).then_inc(fin_ready, 1)

        @block.tensor
        def _(pe):
            def bank(n):
                return job_bank[n % 4]

            def arrived(n):
                pe.wait_ge(landed[n % RING], 16 * (n // RING + 1))
                return n % RING

            pe.wait_ge(consts, 1)
            n = JOB["params"]
            pe.wait_ge(params_landed, 16 * 6)
            nc.tensor.transpose(bank(n)[:, 0:C_ROWS], rows[:, :], ident[0:C_ROWS, 0:C_ROWS]).then_inc(job_done, 1)
            pe.wait_ge(x_landed, 16)
            for i in range(4):
                n = JOB["x_in", i]
                bank_free(pe, n)
                a, k0 = i // 2, 4 * (i % 2)
                for k in range(4):
                    mm = nc.tensor.transpose(bank(n)[:, k * P:(k + 1) * P],
                                             x_tok[:, a, (k0 + k) * P:(k0 + k + 1) * P], ident[:])
                mm.then_inc(job_done, 1)

            def norm(l, w):
                n = JOB["norm", l, w]
                bank_free(pe, n)
                for k in range(KT):
                    if k % 4 == 0:
                        pe.wait_ge(sq_ready, 2 * (2 * l + w) + k // 4 + 1)
                    mm = nc.tensor.matmul(bank(n)[:, 0:T], mean_d[:], sq[:, k, :], start=(k == 0), stop=(k == KT - 1))
                mm.then_inc(job_done, 1)

            def project(n, s, j, src, kts=KT, width=GROUP, at=0, first_wait=None):
                for k in range(kts):
                    if first_wait:
                        first_wait(k)
                    mm = nc.tensor.matmul(bank(n)[:, at:at + T], slot_kf(s, width)[:, k, j * P:(j + 1) * P], src[:, k, :],
                                          start=(k == 0), stop=(k == kts - 1))
                return mm

            def level(l, lev):
                if lev >= 2:
                    pe.wait_ge(level_taken, 2 * (NL * l + lev - 1))
                if LEVELS[lev] != "diag":
                    pe.wait_ge(scaled_ready, 2 * ((NL - 1) * l + lev))
                e = e_mem[:, lev % 2, :].rearrange("p (h t) -> p h t", h=HEADS)
                pair = acc[2 * (lev % 2)], acc[2 * (lev % 2) + 1]
                for hd in range(HEADS):
                    for a in range(1 if LEVELS[lev] == "cross" else TH):
                        ts = slice(a * P, (a + 1) * P)
                        if LEVELS[lev] == "diag":
                            s_op, t_op = kT[:, hd, ts], qT[:, hd, ts]
                        elif LEVELS[lev] == "cross":
                            s_op, t_op = e[:, hd, 0:P], e[:, hd, P:T]
                        else:
                            s_op, t_op = e[:, hd, ts], e[:, hd, ts]
                        mm = nc.tensor.matmul(pair[a][:, hd * P:(hd + 1) * P], s_op, t_op, start=True, stop=True)
                mm.then_inc(level_done, 1)

            for l in range(DEPTH):
                norm(l, 0)
                first = [True]

                def h_wait(k, l=l, w=0):
                    pe.wait_ge(h_ready, KT * (2 * l + w) + k + 1)

                for name in "fq":
                    s = arrived(CHUNK_OF[name, l, 0])
                    for j in range(4):
                        n = JOB[name, l, j]
                        bank_free(pe, n)
                        project(n, s, j, hT, first_wait=h_wait if (name, j) == ("f", 0) else None).then_inc(job_done, 1)
                s = arrived(CHUNK_OF["v", l, 0])
                for a in range(TH):
                    n = JOB["v", l, a]
                    bank_free(pe, n)
                    for k in range(KT):
                        mm = nc.tensor.matmul(bank(n)[:], hT[:, k, a * P:(a + 1) * P], slot_kf(s)[:, k, :],
                                              start=(k == 0), stop=(k == KT - 1))
                    mm.then_inc(job_done, 1)
                for name in "ug":
                    s = arrived(CHUNK_OF[name, l, 0])
                    for j in range(4):
                        n = JOB[name, l, j]
                        bank_free(pe, n)
                        project(n, s, j, hT).then_inc(job_done, 1)
                pe.wait_ge(pooled_ready, 5 * (l + 1))
                pe.wait_ge(poolw_landed, 16)
                for g in range(POOL_TILES):
                    n = JOB["mix", l, g]
                    bank_free(pe, n)
                    nc.tensor.matmul(bank(n)[:, 0:T], poolw[:, l, g, :], pu[:, g, PAD:], start=True, stop=True
                                     ).then_inc(job_done, 1)
                for j in range(16):
                    n = JOB["gate", l, j]
                    if j % 4 == 0:
                        s = arrived(CHUNK_OF["gate", l, j // 4])
                    bank_free(pe, n)
                    project(n, s, j % 4, hT).then_inc(job_done, 1)
                    if j % 2:
                        if j == 1:
                            for q in range(HEADS):
                                taken(pe, JOB["q", l, q])
                            pe.wait_ge(key_ready, HEADS * (l + 1))
                        level(l, j // 2)
                level(l, NL - 1)

                s = arrived(CHUNK_OF["pool_up", l, 0])
                for j in range(POOL_TILES):
                    taken(pe, JOB["mix", l, j])
                for d in range(KT):
                    n = JOB["y_pool", l, d]
                    bank_free(pe, n)
                    for k in range(POOL_TILES):
                        mm = nc.tensor.matmul(bank(n)[:, 0:T], slot_fd(s)[:, k, d * P:(d + 1) * P], mixed[:, k, :],
                                              start=(k == 0), stop=(k == POOL_TILES - 1))
                    mm.then_inc(job_done, 1)
                    if d == 3:
                        pe.wait_ge(level_taken, 2 * NL * (l + 1))
                        for j in range(TH):
                            taken(pe, JOB["v", l, j])
                        for hd in range(HEADS):
                            hs = slice(hd * P, (hd + 1) * P)
                            o_a = acc[hd // 2][:, (hd % 2) * T:(hd % 2) * T + P]
                            o_b = acc[hd // 2][:, (hd % 2) * T + P:(hd % 2) * T + T]
                            nc.tensor.matmul(o_a, v_tok[:, 0, hs], score[:, 0, hd, :], start=True, stop=True)
                            nc.tensor.matmul(o_b, v_tok[:, 0, hs], score_x[:, hd, :], start=True, stop=False)
                            mm = nc.tensor.matmul(o_b, v_tok[:, 1, hs], score[:, 1, hd, :], start=False, stop=True)
                            if hd % 2:
                                mm.then_inc(o_done, 1)
                for i in range(2):
                    pe.wait_ge(o_sq_ready, 2 * l + i + 1)
                    nc.tensor.matmul(acc[2 + i][:], mean_h[:], o_sq[:, i * 512:(i + 1) * 512], start=True, stop=True
                                     ).then_inc(o_mean_done, 1)
                s = arrived(CHUNK_OF["hgrn_up", l, 0])
                pe.wait_ge(o_ready, 2 * (l + 1))
                for d in range(KT):
                    n = JOB["y_hgrn", l, d]
                    bank_free(pe, n)
                    for k in range(HEADS):
                        mm = nc.tensor.matmul(bank(n)[:, 0:T], slot_fd(s)[:, k, d * P:(d + 1) * P], oT[:, k, :],
                                              start=(k == 0), stop=(k == HEADS - 1))
                    mm.then_inc(job_done, 1)
                for d in range(KT):
                    n = JOB["w_out", l, d]
                    if d % 4 == 0:
                        s = arrived(CHUNK_OF["w_out", l, d // 4])
                    bank_free(pe, n)
                    project(n, s, d % 4, merged,
                            first_wait=(lambda k: pe.wait_ge(merged_ready, KT * l + k + 1)) if d == 0 else None
                            ).then_inc(job_done, 1)
                norm(l, 1)
                if l == 0:
                    def down(i):
                        s = arrived(CHUNK_OF["dense_d", 0, i])
                        base = sum(DENSE[:i])
                        for f in range(DENSE[i]):
                            taken(pe, JOB["ffn", base + f])
                            for d in range(KT):
                                last = i == len(DENSE) - 1 and f == DENSE[i] - 1
                                mm = nc.tensor.matmul(acc[d // 2][:, (d % 2) * T:(d % 2) * T + T],
                                                      slot_fd(s, DENSE[i])[:, f, d * P:(d + 1) * P],
                                                      hid[:, i % 2, f, :], start=(i == 0 and f == 0 and d % 2 == 0),
                                                      stop=last, skip_group_check=True)
                        mm.then_inc(down_done, 1)

                    tile = 0
                    for i, tiles in enumerate(DENSE):
                        sg = arrived(CHUNK_OF["dense_g", 0, i])
                        su = arrived(CHUNK_OF["dense_u", 0, i])
                        for f in range(tiles):
                            n = JOB["ffn", tile]
                            bank_free(pe, n)
                            project(n, sg, f, hT, width=tiles * P,
                                    first_wait=(lambda k: h_wait(k, l, 1)) if tile == 0 else None)
                            project(n, su, f, hT, width=tiles * P, at=T).then_inc(job_done, 1)
                            tile += 1
                        if i >= 1:
                            down(i - 1)
                    down(len(DENSE) - 1)

            n = JOB["logits"]
            bank_free(pe, n)
            pe.wait_ge(router_landed, 16)
            for a in range(TH):
                for k in range(KT):
                    if a == 0:
                        pe.wait_ge(h_ready, KT * (2 * DEPTH - 1) + k + 1)
                    mm = nc.tensor.matmul(bank(n)[:, a * N_EXP:(a + 1) * N_EXP], hT[:, k, a * P:(a + 1) * P],
                                          router[:, k, :], start=(k == 0), stop=(k == KT - 1))
            mm.then_inc(job_done, 1)
            for name, src in (("h_tok", hT), ("x_tok", xT)):
                for i in range(4):
                    n = JOB[name, i]
                    bank_free(pe, n)
                    for k in range(4):
                        kk = (i % 2) * 4 + k
                        mm = nc.tensor.transpose(bank(n)[:, k * P:(k + 1) * P],
                                                 src[:, kk, (i // 2) * P:(i // 2 + 1) * P], ident[:])
                    mm.then_inc(job_done, 1)
            n = JOB["ranks"]
            bank_free(pe, n)
            pe.wait_ge(chosen_ready, 1)
            b = bank(n)
            nc.tensor.matmul(b[:, 0:8], before[:], chosen[:, 0, :], start=True, stop=True)
            nc.tensor.matmul(b[:, 8:16], ones[:], chosen[:, 0, :], start=True, stop=False)
            nc.tensor.matmul(b[:, 8:16], before[:], chosen[:, 1, :], start=False, stop=True)
            nc.tensor.matmul(b[:, 16:24], ones[:], chosen[:, 0, :], start=True, stop=False)
            nc.tensor.matmul(b[:, 16:24], ones[:], chosen[:, 1, :], start=False, stop=True).then_inc(job_done, 1)

            def gather():
                for k in range(KT):
                    for a in range(TH):
                        mm = nc.tensor.matmul(acc[2 + k // 4][:, (k % 4) * CAP:(k % 4 + 1) * CAP],
                                              h_tok[:, a, k * P:(k + 1) * P], sel[:, a, :],
                                              start=(a == 0), stop=(a == TH - 1))
                mm.then_inc(gathered, 1)

            for i in range(4):
                taken(pe, JOB["h_tok", i])
            pe.wait_ge(sel_ready, TH)
            gather()
            pe.wait_ge(tables_ready, 1)
            n_reg = pe.value_load(n_items[0:1, 0:1], min_val=N_EXP, max_val=ITEMS)
            with pe.Fori(0, n_reg) as it:
                def arrived_i(c):
                    n = C_LOOP + c
                    pe.wait_ge(landed[n % RING], it * (16 * ITEM_CHUNKS // RING) + 16 * (n // RING + 1))
                    return n % RING

                def down_i(i):
                    s = arrived_i(MOE_CHUNK["d", i])
                    base = sum(EXPERT[:i])
                    for f in range(EXPERT[i]):
                        taken_i(pe, base + f, it)
                        for d in range(KT):
                            last = i == len(EXPERT) - 1 and f == EXPERT[i] - 1
                            mm = nc.tensor.matmul(acc[d // 4][:, (d % 4) * CAP:(d % 4 + 1) * CAP],
                                                  slot_fd(s)[:, f, d * P:(d + 1) * P], hid_e[:, i % 2, f, :],
                                                  start=(i == 0 and f == 0 and d % 4 == 0), stop=last,
                                                  skip_group_check=True)
                    mm.then_inc(down_done, 1)

                pe.wait_ge(hTe_ready, it * 4 + 4)
                tile = 0
                for i, tiles in enumerate(EXPERT):
                    slots = arrived_i(MOE_CHUNK["g", i]), arrived_i(MOE_CHUNK["u", i])
                    for f in range(tiles):
                        b = (J_LOOP + tile) % 4
                        taken_i(pe, tile - 4, it)
                        for q, s in enumerate(slots):
                            for k in range(KT):
                                mm = nc.tensor.matmul(job_bank[b][:, q * CAP:(q + 1) * CAP],
                                                      slot_kf(s)[:, k, f * P:(f + 1) * P], hTe[:, k, :],
                                                      start=(k == 0), stop=(k == KT - 1))
                        mm.then_inc(job_done, 1)
                        tile += 1
                    if i >= 1:
                        down_i(i - 1)
                    if i == len(EXPERT) - 3:
                        pe.wait_ge(sel_ready, it * 4 + 6)
                        for a in range(TH):
                            nc.tensor.transpose(acc[2 + a][0:CAP, 4 * CAP:4 * CAP + P], sel_w[:, a, :], ident[:])
                        gather()
                down_i(len(EXPERT) - 1)
                pe.wait_ge(yT_dve, it + 1)
                pe.wait_ge(hTe_ready, it * 4 + 8)
                for d in range(KT):
                    if d == 4:
                        pe.wait_ge(yT_act, it + 1)
                    mm = nc.tensor.transpose(acc[2 + d // 4][0:CAP, (d % 4) * P:(d % 4 + 1) * P], yT[:, d, :], ident[:])
                    if d % 4 == 3:
                        mm.then_inc(y_turned, 1)
                for q in range(4):
                    jj = sum(EXPERT) + q
                    if q % 2:
                        pe.wait_ge(y_act, it + 1)
                    else:
                        pe.wait_ge(y_dve, it + 1)
                    taken_i(pe, jj - 4, it)
                    nc.tensor.matmul(job_bank[(J_LOOP + jj) % 4][:], sel_wT[:, q // 2, :],
                                     y_tok[:, (q % 2) * 512:(q % 2) * 512 + 512], start=True, stop=True
                                     ).then_inc(job_done, 1)


_INS = ["x", "attn_norm_w", "w_in", "gate_bias", "pool_w", "pool_scale", "pool_up", "hgrn_lower_bounds",
        "hgrn_norm_w", "hgrn_up", "w_out", "ffn_norm_w", "dense_w_gate", "dense_w_up", "dense_w_down",
        "moe_router", "moe_w_gate", "moe_w_up", "moe_w_down", "final_norm_w"]


def kernel(**inputs):
    import numpy as _np
    import concourse.bacc as _bacc
    from concourse import mybir as _mybir
    from concourse.bass_utils import run_bass_kernel_spmd as _run

    nc = _bacc.Bacc("TRN2", target_bir_lowering=False, num_devices=1)
    arrays, args = {}, []
    for name in _INS:
        a = _np.ascontiguousarray(inputs[name])
        arrays[f"in_{name}"] = a
        args.append(nc.dram_tensor(f"in_{name}", a.shape, _mybir.dt.from_np(a.dtype), kind="ExternalInput").ap())
    args.append(nc.dram_tensor("out_0", (1, T, D), F32, kind="ExternalOutput").ap())
    build(nc, *args)
    r = _run(nc, [arrays], core_ids=[0])
    return r.results[0]["out_0"]
```

```python
from contextlib import ExitStack

import concourse.bass as bass
from concourse import mybir

F32 = mybir.dt.float32
F32R = mybir.dt.float32r
I32 = mybir.dt.int32
U32 = mybir.dt.uint32
ALU = mybir.AluOpType
ACT = mybir.ActivationFunctionType
AX_X = mybir.AxisListType.X

P = 128
T = 256
TH = T // P
D = 1024
KT = D // P
DEPTH = 2
HEADS = 4
POOL_TILES = 4
WINDOWS = (2, 4, 8, 16)
PAD = 16
F_DENSE = 2816
N_EXP = 8
F_EXP = 3584
EPS = 1e-6
LB_FLOOR = 1e-30
LB_CEIL = 1.0 - 1e-6
EXP_CEIL = 1e37

RING = 6
UNIT = 2048
SPLITS = 3
POOL_QUARTERS = 2
POOL_QUARTERS_EXP = 1
GROUP = 512
GT = GROUP // P
CAP = 96
MAX_EXTRA = (2 * T) // (CAP + 1)
ITEMS = N_EXP + MAX_EXTRA
COLS = ITEMS + 1

LEVELS = ["diag", "cross"] + [64, 32, 16, 8, 4, 2, 1]
NL = len(LEVELS)

C_ATTN, C_FFN, C_BIAS, C_PSCALE, C_LB, C_HNORM, C_ROWS = 0, 16, 32, 64, 72, 80, 82


def dense_groups(width):
    out = []
    while width > 0:
        out.append(min(GT, width // P))
        width -= GROUP
    return out


DENSE = dense_groups(F_DENSE)
EXPERT = dense_groups(F_EXP)


def swiglu_order(groups):
    out = []
    for i in range(len(groups)):
        out += [("g", i), ("u", i)]
        if i >= 1:
            out.append(("d", i - 1))
    return out + [("d", len(groups) - 1)]


def plan():
    jobs, units, ahead = {}, [], {}
    a_units = [0]

    def job(*key):
        jobs[key if len(key) > 1 else key[0]] = len(jobs)
        event(*key)

    def event(*key):
        ahead[key if len(key) > 1 else key[0]] = len(units) + SPLITS

    def chunk(name, l, c, parts, keys, last="job", value=None):
        for key in keys:
            job(*key)
        for part in range(parts):
            if part < parts - 1:
                a_units[0] += 1
                units.append((name, l, c, part, "unit", a_units[0]))
            else:
                units.append((name, l, c, part, last, keys[-1] if last == "job" else value))
        for key in keys:
            ahead[key] = len(units) - 1 + SPLITS
        if last == "down":
            ahead["down", c] = len(units) - 1 + SPLITS

    job("params")
    for i in range(4):
        job("x_in", i)
    for l in range(DEPTH):
        job("norm", l, 0)
        for name, n in (("f", 4), ("q", 4), ("v", 2), ("u", 4), ("g", 4)):
            chunk(name, l, 0, 2, [(name, l, j) for j in range(n)])
        for j in range(POOL_TILES):
            job("mix", l, j)
        for c in range(4):
            chunk("gate", l, c, 2, [("gate", l, 4 * c + j) for j in range(4)])
            for lev in (2 * c, 2 * c + 1):
                event("level", l, lev)
        event("level", l, NL - 1)
        chunk("pool_up", l, 0, 2, [("y_pool", l, j) for j in range(4)])
        event("o", l)
        chunk("hgrn_up", l, 0, 2, [("y_hgrn", l, j) for j in range(4)])
        for c in range(2):
            chunk("w_out", l, c, 2, [("w_out", l, 4 * c + j) for j in range(4)])
        job("norm", l, 1)
        if l == 0:
            for kind, i in swiglu_order(DENSE):
                full = 2 if DENSE[i] == GT else 1
                first = sum(DENSE[:i])
                if kind == "g":
                    for part in range(full):
                        a_units[0] += 1
                        units.append(("dense_g", l, i, part, "unit", a_units[0]))
                elif kind == "u":
                    chunk("dense_u", l, i, full, [("ffn", first + j) for j in range(DENSE[i])])
                else:
                    chunk("dense_d", l, i, full, [], "down", i + 1)
    job("logits")
    for i in range(4):
        job("h_tok", i)
    for i in range(4):
        job("x_tok", i)
    job("ranks")
    return jobs, units, ahead, a_units[0]


def build(nc, x, attn_norm_w, w_in, gate_bias, pool_w, pool_scale, pool_up, hgrn_lower_bounds,
          hgrn_norm_w, hgrn_up, w_out, ffn_norm_w, dense_w_gate, dense_w_up, dense_w_down,
          moe_router, moe_w_gate, moe_w_up, moe_w_down, final_norm_w, out):
    JOB, UNITS, AHEAD, A_LOOP = plan()
    U_LOOP = len(UNITS)
    UNIT_OF = {u[:4]: n for n, u in enumerate(UNITS)}
    MOE = [(kind, i, part) for kind, i in swiglu_order(EXPERT) for part in range(2)]
    ITEM_UNITS = len(MOE)
    MOE_UNIT = {c: n for n, c in enumerate(MOE)}
    NG = len(EXPERT)
    assert ITEM_UNITS % RING == 0 and ITEM_UNITS % SPLITS == 0 and set(EXPERT) == {GT} and NG % 2 == 1
    MOE_FREED, a_item = [], 0
    for kind, i, part in MOE:
        if part == 1 and kind == "u":
            MOE_FREED.append(("pair", i + 1))
        elif part == 1 and kind == "d":
            MOE_FREED.append(("down", i + 1))
        else:
            a_item += 1
            MOE_FREED.append(("unit", a_item))
    DN_LOOP = len(DENSE)
    TH_LOOP = DEPTH * 8 + sum(DENSE)
    TH_OF = {}
    for l in range(DEPTH):
        for name in "qg":
            for j in range(4):
                TH_OF[name, l, j] = len(TH_OF)
        if l == 0:
            for j in range(sum(DENSE)):
                TH_OF["ffn", j] = len(TH_OF)

    with ExitStack() as ctx:
        def sb(name, shape, dt=F32):
            return ctx.enter_context(nc.sbuf_tensor(name, shape, dt))

        def sem(name):
            return ctx.enter_context(nc.semaphore(name))

        ring = sb("ring", [P, RING, UNIT])
        w_hi = sb("w_hi", [P, SPLITS, UNIT], F32R)
        w_lo = sb("w_lo", [P, SPLITS, UNIT], F32R)
        xT = sb("xT", [P, KT, T])
        a_hi = sb("a_hi", [P, KT * T], F32R)
        a_lo = sb("a_lo", [P, KT * T], F32R)
        b_hi = sb("b_hi", [P, KT * T], F32R)
        b_lo = sb("b_lo", [P, KT * T], F32R)
        qk_mem = sb("qk_mem", [P, KT * T])
        gates_mem = sb("gates_mem", [P, 16 * T])
        G = sb("G", [P, HEADS, T])
        og_mem = sb("og_mem", [P, HEADS * T])
        v_tok = sb("v_tok", [P, TH, HEADS * P])
        e_mem = sb("e_mem", [P, 2, HEADS * T])
        score_mem = sb("score_mem", [P, 3 * 512])
        th_mem = sb("th_mem", [P, 4 * T])
        masks = sb("masks", [P, NL - 2, P])
        ident = sb("ident", [P, P])
        mean_d = sb("mean_d", [P, P])
        mean_h = sb("mean_h", [P, P])
        ones = sb("ones", [P, P])
        before = sb("before", [P, P])
        scan_keep = sb("scan_keep", [P, T])
        rows = sb("rows", [C_ROWS, P])
        cols = sb("cols", [P, C_ROWS])
        half_bias = sb("half_bias", [P, 32])
        half_hnorm = sb("half_hnorm", [P, DEPTH])
        lb = sb("lb", [P, DEPTH, HEADS])
        lb_floor = sb("lb_floor", [P, DEPTH, HEADS])
        one_lb = sb("one_lb", [P, DEPTH, HEADS])
        half_one_lb = sb("half_one_lb", [P, DEPTH, HEADS])
        lb_tmp = sb("lb_tmp", [P, 4, HEADS])
        eps = sb("eps", [P, 1])
        poolw = sb("poolw", [P, POOL_TILES, P])
        rms_ln = sb("rms_ln", [P, T])
        rstd = sb("rstd", [P, T])
        inv_pos = sb("inv_pos", [P, POOL_TILES, PAD])
        pool_head = sb("pool_head", [P, POOL_TILES, PAD])
        router = sb("router", [P, KT, N_EXP])
        iota_e = sb("iota_e", [P, N_EXP])
        iota_c = sb("iota_c", [P, CAP])
        iota_j = sb("iota_j", [P, COLS, N_EXP])
        top_i = sb("top_i", [P, TH, 8], U32)
        pos_item = sb("pos_item", [P, TH, COLS])
        w_item = sb("w_item", [P, TH, COLS])
        item_e = sb("item_e", [P, COLS], I32)
        n_items = sb("n_items", [P, 1], I32)
        fin = sb("fin", [P, 6])

        h_full = qk_mem[:, :].rearrange("p (k t) -> p k t", k=KT)
        sq = e_mem[:, :, :].rearrange("p a (k t) -> p (a k) t", t=T)
        qT = qk_mem[:, 0:HEADS * T].rearrange("p (h t) -> p h t", h=HEADS)
        kT = qk_mem[:, HEADS * T:].rearrange("p (h t) -> p h t", h=HEADS)
        gates = gates_mem[:, :].rearrange("p (k t) -> p k t", k=16)
        og = og_mem[:, :].rearrange("p (h t) -> p h t", h=HEADS)
        expf = e_mem[:, 0, :].rearrange("p (h t) -> p h t", h=HEADS)
        sig = e_mem[:, 1, :].rearrange("p (h t) -> p h t", h=HEADS)
        PW = POOL_TILES * (PAD + T)
        pu, pb, pc = (gates_mem[:, i * PW:(i + 1) * PW].rearrange("p (g t) -> p g t", g=POOL_TILES) for i in range(3))
        th = th_mem[:, :].rearrange("p (b t) -> p b t", b=4)
        score = score_mem[:, 0:TH * HEADS * P].rearrange("p (a h t) -> p a h t", a=TH, h=HEADS)
        score_x = score_mem[:, 1024:1536].rearrange("p (h t) -> p h t", h=HEADS)
        mixed = score_mem[:, 0:POOL_TILES * T].rearrange("p (g t) -> p g t", g=POOL_TILES)
        masked = th_mem[:, :].rearrange("p (a h t) -> p a h t", a=TH, h=HEADS)
        o_sq = th_mem
        o_full = e_mem[:, 1, :]
        h_tok = gates_mem[:, 0:TH * D].rearrange("p (a d) -> p a d", a=TH)
        x_tok = gates_mem[:, TH * D:].rearrange("p (a d) -> p a d", a=TH)

        def tiles_of(mem, n=KT, at=0):
            return mem[:, at:at + n * T].rearrange("p (k t) -> p k t", k=n)

        h_parts = tiles_of(a_hi), tiles_of(a_lo)
        mix_parts = tiles_of(b_hi, 4), tiles_of(b_lo, 4)
        o_parts = tiles_of(b_hi, 4, 4 * T), tiles_of(b_lo, 4, 4 * T)
        merged_parts = h_parts
        hid_parts = tuple(m[:, :].rearrange("p (b f t) -> p b f t", b=2, f=GT) for m in (b_hi, b_lo))
        xe_parts = tuple(m[:, 0:KT * CAP].rearrange("p (k c) -> p k c", k=KT) for m in (a_hi, a_lo))
        he_parts = tuple(m[:, 0:2 * GT * CAP].rearrange("p (b f c) -> p b f c", b=2, f=GT) for m in (b_hi, b_lo))
        th_e = th_mem[0:CAP, :].rearrange("p (b f) -> p b f", b=2)
        y_tok = G[0:CAP, :, :].rearrange("p h t -> p (h t)")
        sel = og_mem[:, 0:TH * CAP].rearrange("p (a c) -> p a c", a=TH)
        sel_w = og_mem[:, TH * CAP:2 * TH * CAP].rearrange("p (a c) -> p a c", a=TH)
        sel_wT = og_mem[0:CAP, 2 * TH * CAP:2 * TH * CAP + T].rearrange("p (a c) -> p a c", a=TH)
        at = [0]

        def scratch(*shape):
            n = 1
            for s in shape:
                n *= s
            v = score_mem[:, at[0]:at[0] + n]
            at[0] += n
            return v

        lg = scratch(TH, 8).rearrange("p (a e) -> p a e", a=TH)
        top_v = scratch(TH, 8).rearrange("p (a e) -> p a e", a=TH)
        top_f = scratch(TH, 8).rearrange("p (a e) -> p a e", a=TH)
        gap = scratch(TH)
        gap_e = scratch(TH)
        gap_1 = scratch(TH)
        w1 = scratch(TH)
        w2 = scratch(TH)
        hot1 = scratch(TH, 8).rearrange("p (a e) -> p a e", a=TH)
        hot2 = scratch(TH, 8).rearrange("p (a e) -> p a e", a=TH)
        wt1 = scratch(TH, 8).rearrange("p (a e) -> p a e", a=TH)
        wt2 = scratch(TH, 8).rearrange("p (a e) -> p a e", a=TH)
        chosen = scratch(TH, 8).rearrange("p (a e) -> p a e", a=TH)
        comb = scratch(TH, 8).rearrange("p (a e) -> p a e", a=TH)
        rank1 = scratch(TH, 8).rearrange("p (a e) -> p a e", a=TH)
        count = scratch(8)
        over1 = scratch(8)
        over2 = scratch(8)
        over = scratch(8)
        cum = scratch(8)
        start = scratch(8)
        start1 = scratch(8)
        ones8 = scratch(8)
        one1 = scratch(COLS, 8).rearrange("p (j e) -> p j e", e=8)
        one2 = scratch(COLS, 8).rearrange("p (j e) -> p j e", e=8)
        hot = scratch(COLS, 8).rearrange("p (j e) -> p j e", e=8)
        prod = scratch(3, COLS, 8).rearrange("p (a j e) -> p a j e", a=3, e=8)
        base1 = scratch(COLS)
        base2 = scratch(COLS)
        base = scratch(COLS)
        e_f = scratch(COLS)
        n_f = scratch(1)

        job_bank = [ctx.enter_context(nc.psum_tensor(f"job_bank{i}", [P, 512], F32)) for i in range(4)]
        acc = [ctx.enter_context(nc.psum_tensor(f"acc{i}", [P, 512], F32)) for i in range(4)]

        landed = [sem(f"landed{i}") for i in range(RING)]
        hi_done = sem("hi_done")
        lo_dve = sem("lo_dve")
        lo_pool = sem("lo_pool")
        unit_done = sem("unit_done")
        pair_done = sem("pair_done")
        pair_taken = [sem("pair_taken0"), sem("pair_taken1")]
        h_full_ready = sem("h_full_ready")
        h_hi_ready = sem("h_hi_ready")
        mix_hi_ready = sem("mix_hi_ready")
        mix_ready = sem("mix_ready")
        o_full_ready = sem("o_full_ready")
        o_hi_ready = sem("o_hi_ready")
        merged_full_ready = sem("merged_full_ready")
        merged_hi_ready = sem("merged_hi_ready")
        hid_hi_ready = sem("hid_hi_ready")
        hid_ready = sem("hid_ready")
        turned = sem("turned")
        xe_hi_ready = sem("xe_hi_ready")
        xe_ready = sem("xe_ready")
        out_taken = sem("out_taken")
        out_done = sem("out_done")
        x_landed = sem("x_landed")
        params_landed = sem("params_landed")
        poolw_landed = sem("poolw_landed")
        router_landed = sem("router_landed")
        fnw_landed = sem("fnw_landed")
        consts = sem("consts")
        job_done = sem("job_done")
        job_taken = [sem(f"job_taken{i}") for i in range(4)]
        down_done = sem("down_done")
        lb_max_ready = sem("lb_max_ready")
        lb_exp_ready = sem("lb_exp_ready")
        params_ready = sem("params_ready")
        sq_ready = sem("sq_ready")
        rstd_ready = sem("rstd_ready")
        h_ready = sem("h_ready")
        x_ready = sem("x_ready")
        forget_ready = sem("forget_ready")
        key_ready = sem("key_ready")
        logf_ready = sem("logf_ready")
        gsum_ready = sem("gsum_ready")
        th_ready = sem("th_ready")
        win_ready = sem("win_ready")
        pooled_ready = sem("pooled_ready")
        arg_ready = sem("arg_ready")
        exp_ready = sem("exp_ready")
        scaled_ready = sem("scaled_ready")
        level_done = sem("level_done")
        level_taken = sem("level_taken")
        o_done = sem("o_done")
        o_sq_ready = sem("o_sq_ready")
        o_mean_done = sem("o_mean_done")
        o_ln = sem("o_ln")
        o_rstd_ready = sem("o_rstd_ready")
        o_ready = sem("o_ready")
        merged_ready = sem("merged_ready")
        gap_ready = sem("gap_ready")
        gap_exp_ready = sem("gap_exp_ready")
        chosen_ready = sem("chosen_ready")
        tables_ready = sem("tables_ready")
        sel_ready = sem("sel_ready")
        y_dve = sem("y_dve")
        y_act = sem("y_act")
        silu_half = sem("silu_half")
        fin_sq = sem("fin_sq")
        fin_ln = sem("fin_ln")
        fin_rstd = sem("fin_rstd")
        fin_ready = sem("fin_ready")
        stored = sem("stored")
        pool_step = sem("pool_step")
        dve_step = sem("dve_step")

        def done(eng, n):
            eng.wait_ge(job_done, n + 1)

        def taken(eng, n):
            eng.wait_ge(job_taken[n % 4], n // 4 + 1)

        def bank_free(eng, n):
            if n >= 4:
                taken(eng, n - 4)

        def unit_freed(eng, n):
            kind, key = UNITS[n][4:]
            if kind == "unit":
                eng.wait_ge(unit_done, key)
            elif kind == "down":
                eng.wait_ge(down_done, key)
            else:
                done(eng, JOB[key])

        def unit_freed_i(eng, c, it):
            back = 1 if c < 0 else 0
            kind, value = MOE_FREED[c % ITEM_UNITS]
            if kind == "unit":
                eng.wait_ge(unit_done, it * a_item + (A_LOOP + value - back * a_item))
            elif kind == "down":
                eng.wait_ge(down_done, it * NG + (DN_LOOP + value - back * NG))
            else:
                eng.wait_ge(pair_done, it * (NG + 1) + (1 + value - back * (NG + 1)))

        def landed_wait(eng, n, it=None):
            if it is None:
                eng.wait_ge(landed[n % RING], 16 * (n // RING + 1))
            else:
                eng.wait_ge(landed[n % RING], it * (16 * ITEM_UNITS // RING) + 16 * (n // RING + 1))

        def feeder(eng, split_one):
            fed = [0]

            def feed(limit):
                while fed[0] < min(limit, U_LOOP):
                    split_one(fed[0])
                    fed[0] += 1
            return feed

        def feeder_i(eng, it, n_reg, split_item):
            fed = [SPLITS]

            def feed(limit):
                while fed[0] < limit:
                    c = fed[0]
                    if c < ITEM_UNITS:
                        split_item(c, it)
                    else:
                        with eng.If(n_reg > it + 1):
                            split_item(c - ITEM_UNITS, it + 1)
                    fed[0] += 1
            return feed

        w_in_v = w_in.rearrange("l (k p) f -> l p k f", p=P)
        column = {"u": 0, "q": 512, "f": 1024, "v": 1536, "g": 2048, "gate": 2560}
        ups = {"pool_up": pool_up.rearrange("l (k p) d -> l p k d", p=P),
               "hgrn_up": hgrn_up.rearrange("l (k p) d -> l p k d", p=P)}
        w_out_v = w_out.rearrange("l (k p) d -> l p k d", p=P)

        def kf(mem, s, width=GROUP):
            return mem[:, s, :].rearrange("p (k f) -> p k f", f=width)

        def fd(mem, s):
            return mem[:, s, :].rearrange("p (f d) -> p f d", d=D)

        block = ctx.enter_context(nc.Block())

        @block.sync
        def _(sp):
            def slot_free(n):
                sp.wait_ge(lo_dve, n - RING + 1)
                sp.wait_ge(lo_pool, n - RING + 1)

            sp.dma_start(x_tok, x[0].rearrange("(a p) d -> p a d", p=P)).then_inc(x_landed, 16)
            for n, (name, l, c, part, _, _) in enumerate(UNITS):
                if n >= RING:
                    slot_free(n)
                s = n % RING
                ks = slice(4 * part, 4 * part + 4)
                if name in column:
                    a = column[name] + c * GROUP
                    sp.dma_start(kf(ring, s), w_in_v[l, :, ks, a:a + GROUP]).then_inc(landed[s], 16)
                elif name in ups:
                    sp.dma_start(fd(ring, s), ups[name][l, :, 2 * part:2 * part + 2, :]).then_inc(landed[s], 16)
                elif name == "w_out":
                    sp.dma_start(kf(ring, s), w_out_v[l, :, ks, c * GROUP:(c + 1) * GROUP]).then_inc(landed[s], 16)
                elif name == "dense_d":
                    a = c * GROUP + part * 2 * P
                    sp.dma_start(fd(ring, s), dense_w_down[0, a:a + 2 * P, :].rearrange("(f p) d -> p f d", p=P)
                                 ).then_inc(landed[s], 16)
                else:
                    w = dense_w_gate if name == "dense_g" else dense_w_up
                    a, width = c * GROUP, DENSE[c] * P
                    if width < GROUP:
                        ks = slice(0, KT)
                    sp.dma_start(kf(ring, s, width),
                                 w[0, :, a:a + width].rearrange("(k p) f -> p k f", p=P)[:, ks, :]
                                 ).then_inc(landed[s], 16)

            def load_item(it, e):
                for c, (kind, i, part) in enumerate(MOE):
                    n = U_LOOP + c
                    s = n % RING
                    sp.wait_ge(lo_dve, it * ITEM_UNITS + (n - RING + 1))
                    sp.wait_ge(lo_pool, it * ITEM_UNITS + (n - RING + 1))
                    a = i * GROUP
                    if kind == "d":
                        a += part * 2 * P
                        src = moe_w_down[0, bass.ds(e, 1), a:a + 2 * P, :].rearrange("o (f p) d -> p (o f) d", p=P)
                        sp.dma_start(fd(ring, s), src).then_inc(landed[s], 16)
                    else:
                        w = moe_w_gate if kind == "g" else moe_w_up
                        r = part * 4 * P
                        src = w[0, bass.ds(e, 1), r:r + 4 * P, a:a + GROUP].rearrange("o (k p) f -> p (o k) f", p=P)
                        sp.dma_start(kf(ring, s), src).then_inc(landed[s], 16)

            with sp.Fori(0, N_EXP) as it:
                load_item(it, it)
            sp.wait_ge(tables_ready, 1)
            n = sp.value_load(n_items[0:1, 0:1], min_val=N_EXP, max_val=ITEMS)
            with sp.If(n > N_EXP):
                with sp.Fori(N_EXP, n) as it:
                    e = sp.value_load(item_e[0:1, bass.ds(it, 1)], min_val=0, max_val=N_EXP - 1)
                    load_item(it, e)
            for a in range(TH):
                sp.wait_ge(fin_ready, a + 1)
                sp.dma_start(out[0, a * P:(a + 1) * P, :], h_tok[:, a, :]).then_inc(stored, 16)
            sp.wait_ge(stored, 16 * TH)

        @block.gpsimd
        def _(pool):
            steps = [0]

            def step(ins):
                steps[0] += 1
                ins.then_inc(pool_step, 1)

            def settle():
                pool.wait_ge(pool_step, steps[0])

            g = nc.gpsimd
            step(g.memset(ident[:], 0.0))
            step(g.memset(mean_d[:], 1.0 / D))
            step(g.memset(mean_h[:], 1.0 / P))
            step(g.memset(ones[:], 1.0))
            step(g.memset(before[:], 1.0))
            step(g.memset(scan_keep[:], 1.0))
            step(g.memset(masks[:], 0.0))
            step(g.memset(eps[:], EPS))
            step(g.iota(iota_e[:], pattern=[[1, N_EXP]], base=0, channel_multiplier=0,
                        allow_small_or_imprecise_dtypes=True))
            step(g.iota(iota_c[:], pattern=[[1, CAP]], base=0, channel_multiplier=0,
                        allow_small_or_imprecise_dtypes=True))
            step(g.iota(iota_j[:], pattern=[[1, COLS], [0, N_EXP]], base=0, channel_multiplier=0,
                        allow_small_or_imprecise_dtypes=True))
            step(g.iota(inv_pos[:], pattern=[[0, POOL_TILES], [1, PAD]], base=1, channel_multiplier=0,
                        allow_small_or_imprecise_dtypes=True))
            settle()
            step(g.affine_select(out=ident[:], in_=ident[:], compare_op=ALU.not_equal, fill=1.0, base=0,
                                 pattern=[[-1, P]], channel_multiplier=1))
            step(g.affine_select(out=before[:], in_=before[:], compare_op=ALU.is_gt, fill=0.0, base=0,
                                 pattern=[[1, P]], channel_multiplier=-1))
            step(g.memset(scan_keep[:].rearrange("p (a t) -> p a t", a=TH)[:, :, 0:1], 0.0))
            for m, h in enumerate(LEVELS[2:]):
                step(g.memset(masks[:, m, :].rearrange("p (b r) -> p b r", r=2 * h)[:, :, h:], 1.0))
            settle()
            for m, h in enumerate(LEVELS[2:]):
                v = masks[:, m, :].rearrange("p (b r) -> p b r", r=2 * h)
                step(g.affine_select(out=v, in_=v, compare_op=ALU.is_ge, fill=0.0, base=0,
                                     pattern=[[-2 * h, P // (2 * h)], [0, 2 * h]], channel_multiplier=1))
            settle()
            for m, h in enumerate(LEVELS[2:]):
                v = masks[:, m, :].rearrange("p (b r) -> p b r", r=2 * h)
                step(g.affine_select(out=v, in_=v, compare_op=ALU.is_ge, fill=0.0, base=h - 1,
                                     pattern=[[2 * h, P // (2 * h)], [0, 2 * h]], channel_multiplier=-1))
            settle()
            g.memset(fin[:], 0.0).then_inc(consts, 1)

            def lo_part(n, it=None):
                m = n if it is None else it * ITEM_UNITS + n
                q = UNIT // 4 * (4 - (POOL_QUARTERS if it is None else POOL_QUARTERS_EXP))
                s, b = n % RING, n % SPLITS
                pool.wait_ge(hi_done, m + 1)
                g.tensor_tensor(w_lo[:, b, q:], ring[:, s, q:], w_hi[:, b, q:].bitcast(F32), ALU.subtract
                                ).then_inc(lo_pool, 1)

            feed = feeder(pool, lo_part)
            for l in range(DEPTH):
                feed(AHEAD["u", l, 3])
                for j in range(4):
                    taken(pool, JOB["u", l, j])
                for buf in (pu, pb, pc):
                    step(g.memset(buf[:, :, 0:PAD], 0.0))
                settle()
                span = {1: (pu, pb, 0), 2: (pb, pc, 1), 4: (pc, pb, 2), 8: (pb, pc, 3)}
                for shift, (src, dst, first) in span.items():
                    a = src[:, first:, PAD:]
                    b = src[:, first:, PAD - shift:PAD - shift + T]
                    ins = g.tensor_tensor(dst[:, first:, PAD:], a, b, ALU.add)
                    if shift == 8:
                        ins.then_inc(win_ready, 1)
                    else:
                        step(ins)
                        settle()
            feed(U_LOOP)
            for c in range(SPLITS):
                lo_part(U_LOOP + c)
            pool.wait_ge(tables_ready, 1)
            n_reg = pool.value_load(n_items[0:1, 0:1], min_val=N_EXP, max_val=ITEMS)
            with pool.Fori(0, n_reg) as it:
                feeder_i(pool, it, n_reg, lambda c, i: lo_part(U_LOOP + c, i))(ITEM_UNITS + SPLITS)

        @block.scalar
        def _(act):
            for src, a, n in ((attn_norm_w.rearrange("l (k p) -> (l k) p", p=P), C_ATTN, 16),
                              (ffn_norm_w.rearrange("l (k p) -> (l k) p", p=P), C_FFN, 16),
                              (gate_bias.rearrange("l (k p) -> (l k) p", p=P), C_BIAS, 32),
                              (pool_scale.rearrange("l (k p) -> (l k) p", p=P), C_PSCALE, 8),
                              (hgrn_lower_bounds.rearrange("l (k p) -> (l k) p", p=P), C_LB, 8),
                              (hgrn_norm_w, C_HNORM, 2)):
                act.dma_start(rows[a:a + n, :], src).then_inc(params_landed, 16)
            act.dma_start(poolw[:], pool_w[0].rearrange("g c d -> c g d")).then_inc(poolw_landed, 16)
            act.dma_start(router[:], moe_router[0].rearrange("(k p) e -> p k e", p=P)).then_inc(router_landed, 16)
            act.wait_ge(consts, 1)

            def bank(n):
                return job_bank[n % 4]

            def hi_part(n, it=None, freed=None):
                if it is None:
                    landed_wait(act, n)
                    if n >= SPLITS:
                        unit_freed(act, n - SPLITS) if freed is None else freed()
                else:
                    landed_wait(act, n, it)
                    unit_freed_i(act, n - U_LOOP - SPLITS, it)
                nc.scalar.activation(w_hi[:, n % SPLITS, :], ring[:, n % RING, :], ACT.Copy).then_inc(hi_done, 1)

            feed = feeder(act, hi_part)
            feed(SPLITS)
            for i in range(4):
                n = JOB["x_in", i]
                done(act, n)
                a, k0 = i // 2, 4 * (i % 2)
                nc.scalar.activation(xT[:, k0:k0 + 4, a * P:(a + 1) * P],
                                     bank(n)[:].rearrange("p (k t) -> p k t", k=4), ACT.Copy
                                     ).then_inc(job_taken[n % 4], 1)
            act.wait_ge(lb_max_ready, 1)
            nc.scalar.activation(lb_tmp[:, 0:2, :], lb[:, :, :], ACT.Exp).then_inc(lb_exp_ready, 1)

            def norm(l, w):
                for half in range(2):
                    ks = slice(4 * half, 4 * half + 4)
                    if w == 1:
                        feed(AHEAD["w_out", l, 4 * half])
                        for j in range(4):
                            taken(act, JOB["w_out", l, 4 * half + j])
                    elif l == 0:
                        for i in range(4):
                            taken(act, JOB["x_in", i])
                    else:
                        act.wait_ge(x_ready, 2 * half + 2)
                    nc.scalar.activation(sq[:, ks, :], xT[:, ks, :], ACT.Square).then_inc(sq_ready, 1)
                n = JOB["norm", l, w]
                done(act, n)
                nc.scalar.activation(rms_ln[:], bank(n)[:, 0:T], ACT.Ln, bias=eps[:, 0:1]
                                     ).then_inc(job_taken[n % 4], 1)
                taken(act, n)
                nc.scalar.activation(rstd[:], rms_ln[:], ACT.Exp, scale=-0.5).then_inc(rstd_ready, 1)
                if (l, w) != (DEPTH - 1, 1):
                    for k in range(KT):
                        act.wait_ge(h_full_ready, KT * (2 * l + w) + k + 1)
                        nc.scalar.activation(h_parts[0][:, k, :], h_full[:, k, :], ACT.Copy).then_inc(h_hi_ready, 1)

            def tanh_half(*key):
                n = JOB[key]
                feed(AHEAD[key])
                done(act, n)
                nc.scalar.activation(th[:, n % 4, :], bank(n)[:, 0:T], ACT.Tanh, scale=0.5).then_inc(th_ready, 1)

            for l in range(DEPTH):
                norm(l, 0)
                for j in range(HEADS):
                    n = JOB["f", l, j]
                    feed(AHEAD["f", l, j])
                    done(act, n)
                    nc.scalar.activation(expf[:, j, :], bank(n)[:, 0:T], ACT.Exp, scale=-1.0
                                         ).then_inc(job_taken[n % 4], 1)
                for j in range(HEADS):
                    tanh_half("q", l, j)
                for a in range(TH):
                    n = JOB["v", l, a]
                    feed(AHEAD["v", l, a])
                    done(act, n)
                    nc.scalar.activation(v_tok[:, a, :], bank(n)[:], ACT.Copy).then_inc(job_taken[n % 4], 1)
                act.wait_ge(forget_ready, HEADS * (l + 1))
                nc.scalar.activation(sig, sig, ACT.Ln).then_inc(logf_ready, 1)
                for j in range(POOL_TILES):
                    n = JOB["u", l, j]
                    feed(AHEAD["u", l, j])
                    done(act, n)
                    nc.scalar.activation(pu[:, j, PAD:], bank(n)[:, 0:T], ACT.Copy).then_inc(job_taken[n % 4], 1)
                for j in range(HEADS):
                    tanh_half("g", l, j)
                for j in range(POOL_TILES):
                    n = JOB["mix", l, j]
                    c = C_PSCALE + POOL_TILES * l + j
                    done(act, n)
                    nc.scalar.activation(mixed[:, j, :], bank(n)[:, 0:T], ACT.Copy, scale=cols[:, c:c + 1]
                                         ).then_inc(job_taken[n % 4], 1)
                if l + 1 < DEPTH:
                    act.dma_start(poolw[:], pool_w[l + 1].rearrange("g c d -> c g d")).then_inc(poolw_landed, 16)
                for j in range(POOL_TILES):
                    taken(act, JOB["mix", l, j])
                    nc.scalar.activation(mix_parts[0][:, j, :], mixed[:, j, :], ACT.Copy).then_inc(mix_hi_ready, 1)
                for j in range(16):
                    n = JOB["gate", l, j]
                    feed(AHEAD["gate", l, j])
                    done(act, n)
                    c = 16 * l + j
                    nc.scalar.activation(gates[:, j, :], bank(n)[:, 0:T], ACT.Tanh, scale=0.5,
                                         bias=half_bias[:, c:c + 1]).then_inc(job_taken[n % 4], 1)
                    if j % 4 == 3:
                        for lev in (j // 4 * 2 + 1, j // 4 * 2 + 2):
                            act.wait_ge(arg_ready, 2 * ((NL - 1) * l + lev))
                            nc.scalar.activation(e_mem[:, lev % 2, :], e_mem[:, lev % 2, :], ACT.Exp
                                                 ).then_inc(exp_ready, 1)
                feed(AHEAD["o", l])
                for i in range(2):
                    act.wait_ge(o_done, 2 * l + i + 1)
                    nc.scalar.activation(o_sq[:, i * 512:(i + 1) * 512], acc[i][:], ACT.Square
                                         ).then_inc(o_sq_ready, 1)
                for i in range(2):
                    act.wait_ge(o_mean_done, 2 * l + i + 1)
                    nc.scalar.activation(e_mem[:, 0, i * 512:(i + 1) * 512], acc[2 + i][:], ACT.Ln,
                                         bias=eps[:, 0:1]).then_inc(o_ln, 1)
                for i in range(2):
                    act.wait_ge(o_ln, 2 * l + i + 1)
                    nc.scalar.activation(e_mem[:, 0, i * 512:(i + 1) * 512], e_mem[:, 0, i * 512:(i + 1) * 512],
                                         ACT.Exp, scale=-0.5).then_inc(o_rstd_ready, 1)
                for i in range(2):
                    act.wait_ge(o_full_ready, 2 * l + i + 1)
                    nc.scalar.activation(o_parts[0][:, 2 * i:2 * i + 2, :],
                                         o_full[:, i * 512:(i + 1) * 512].rearrange("p (h t) -> p h t", h=2), ACT.Copy
                                         ).then_inc(o_hi_ready, 1)
                feed(AHEAD["y_hgrn", l, 0])
                for i in range(4):
                    act.wait_ge(merged_full_ready, 4 * l + i + 1)
                    nc.scalar.activation(merged_parts[0][:, 2 * i:2 * i + 2, :], gates[:, 2 * i:2 * i + 2, :], ACT.Copy
                                         ).then_inc(merged_hi_ready, 1)
                norm(l, 1)
                if l == 0:
                    def hid_hi(tile):
                        n = JOB["ffn", tile]
                        i = tile // GT
                        taken(act, n)
                        nc.scalar.activation(hid_parts[0][:, i % 2, tile % GT, :], th[:, n % 4, :], ACT.Copy
                                             ).then_inc(hid_hi_ready, 1)

                    for j in range(sum(DENSE)):
                        if j >= 4:
                            act.wait_ge(hid_ready, j - 3)
                        tanh_half("ffn", j)
                        if j >= 1:
                            hid_hi(j - 1)
                    hid_hi(sum(DENSE) - 1)
                    feed(AHEAD["down", len(DENSE) - 1])

            for name, dst in (("h_tok", h_tok), ("x_tok", x_tok)):
                for i in range(4):
                    n = JOB[name, i]
                    done(act, n)
                    nc.scalar.activation(dst[:, i // 2, (i % 2) * 512:(i % 2) * 512 + 512], bank(n)[:], ACT.Copy
                                         ).then_inc(job_taken[n % 4], 1)
                if name == "h_tok":
                    act.wait_ge(gap_ready, 1)
                    nc.scalar.activation(gap_e, gap, ACT.Exp).then_inc(gap_exp_ready, 1)
            act.dma_start(qk_mem[:, 0:D], final_norm_w.rearrange("(o d) -> o d", o=1).to_broadcast([P, D])
                          ).then_inc(fnw_landed, 16)

            act.wait_ge(tables_ready, 1)
            n_reg = act.value_load(n_items[0:1, 0:1], min_val=N_EXP, max_val=ITEMS)
            def tokens_hi():
                for i in range(2):
                    nc.scalar.activation(xe_parts[0][:, 4 * i:4 * i + 4, :],
                                         job_bank[2 + i][:, 0:4 * CAP].rearrange("p (k c) -> p k c", k=4), ACT.Copy
                                         ).then_inc(xe_hi_ready, 1)

            for c in range(SPLITS):
                hi_part(U_LOOP + c)
            act.wait_ge(pair_done, 1)
            tokens_hi()
            with act.Fori(0, n_reg) as it:
                feed_i = feeder_i(act, it, n_reg, lambda c, i: hi_part(U_LOOP + c, i))

                def hidden_hi(i):
                    act.wait_ge(turned, it * NG + (i + 1))
                    nc.scalar.activation(he_parts[0][:, i % 2, :, :],
                                         acc[2 + i % 2][:, 0:GT * CAP].rearrange("p (f c) -> p f c", f=GT), ACT.Copy
                                         ).then_inc(hid_hi_ready, 1)

                for i in range(NG):
                    if i >= 1:
                        feed_i(MOE_UNIT["g", i, 1] + 1 + SPLITS)
                        hidden_hi(i - 1)
                    feed_i(MOE_UNIT["u", i, 1] + SPLITS)
                    act.wait_ge(pair_done, it * (NG + 1) + (i + 2))
                    nc.scalar.activation(th_e[:, i % 2, :], job_bank[2 * (i % 2)][0:CAP, :], ACT.Tanh, scale=0.5
                                         ).then_inc(th_ready, 1)
                feed_i(MOE_UNIT["d", NG - 2, 1] + 1 + SPLITS)
                hidden_hi(NG - 1)
                act.wait_ge(pair_done, it * (NG + 1) + (NG + 2))
                tokens_hi()
                feed_i(ITEM_UNITS - 1 + SPLITS)
                act.wait_ge(down_done, it * NG + (DN_LOOP + NG))
                nc.scalar.activation(y_tok[:, 512:1024], acc[1][0:CAP, :], ACT.Copy).then_inc(y_act, 1)
                feed_i(ITEM_UNITS + SPLITS)

            for a in range(TH):
                act.wait_ge(out_taken, n_reg * 4 + (4 - 2 * (TH - 1 - a)))
                nc.scalar.activation(qk_mem[:, D:2 * D], x_tok[:, a, :], ACT.Square,
                                     accum_out=fin[:, a:a + 1]).then_inc(fin_sq, 1)
                act.wait_ge(fin_sq, a + 1)
            nc.scalar.activation(fin[:, 2:4], fin[:, 0:2], ACT.Ln, scale=1.0 / D, bias=eps[:, 0:1]).then_inc(fin_ln, 1)
            act.wait_ge(fin_ln, 1)
            nc.scalar.activation(fin[:, 4:6], fin[:, 2:4], ACT.Exp, scale=-0.5).then_inc(fin_rstd, 1)

        @block.vector
        def _(dve):
            v = nc.vector
            steps = [0]

            def step(ins):
                steps[0] += 1
                ins.then_inc(dve_step, 1)

            def settle():
                dve.wait_ge(dve_step, steps[0])

            def bank(n):
                return job_bank[n % 4]

            def lo_part(n, it=None):
                m = n if it is None else it * ITEM_UNITS + n
                q = UNIT // 4 * (4 - (POOL_QUARTERS if it is None else POOL_QUARTERS_EXP))
                s, b = n % RING, n % SPLITS
                dve.wait_ge(hi_done, m + 1)
                v.tensor_tensor(w_lo[:, b, 0:q], ring[:, s, 0:q], w_hi[:, b, 0:q].bitcast(F32), ALU.subtract
                                ).then_inc(lo_dve, 1)

            def lo_of(parts, full, at):
                return v.tensor_tensor(parts[1][at], full, parts[0][at].bitcast(F32), ALU.subtract)

            feed = feeder(dve, lo_part)
            dve.wait_ge(consts, 1)
            for g, w in enumerate(WINDOWS):
                step(v.tensor_scalar(inv_pos[:, g, :], inv_pos[:, g, :], float(w), None, ALU.min))
            settle()
            step(v.reciprocal(inv_pos[:], inv_pos[:]))
            n = JOB["params"]
            done(dve, n)
            v.tensor_copy(cols[:], bank(n)[:, 0:C_ROWS]).then_inc(job_taken[n % 4], 1)
            taken(dve, n)
            step(v.tensor_scalar(half_bias[:], cols[:, C_BIAS:C_BIAS + 32], 0.5, None, ALU.mult))
            step(v.tensor_scalar(half_hnorm[:], cols[:, C_HNORM:C_HNORM + DEPTH], 0.5, None, ALU.mult))
            l0, l1 = cols[:, C_LB:C_LB + HEADS], cols[:, C_LB + HEADS:C_LB + 2 * HEADS]
            step(v.tensor_tensor(lb_tmp[:, 2, :], l0, l1, ALU.max))
            settle()
            step(v.tensor_tensor(lb[:, 0, :], l0, lb_tmp[:, 2, :], ALU.subtract))
            v.tensor_tensor(lb[:, 1, :], l1, lb_tmp[:, 2, :], ALU.subtract).then_inc(lb_max_ready, 1)
            dve.wait_ge(lb_exp_ready, 1)
            step(v.tensor_tensor(lb_tmp[:, 2, :], lb_tmp[:, 0, :], lb_tmp[:, 1, :], ALU.add))
            settle()
            step(v.reciprocal(lb_tmp[:, 3, :], lb_tmp[:, 2, :]))
            settle()
            step(v.tensor_tensor(lb_tmp[:, 0, :], lb_tmp[:, 0, :], lb_tmp[:, 3, :], ALU.mult))
            step(v.tensor_tensor(lb_tmp[:, 1, :], lb_tmp[:, 1, :], lb_tmp[:, 3, :], ALU.mult))
            settle()
            step(v.tensor_tensor(lb[:, 0, :], lb_tmp[:, 0, :], lb_tmp[:, 0, :], ALU.subtract))
            step(v.tensor_tensor(lb[:, 1, :], lb_tmp[:, 0, :], lb_tmp[:, 1, :], ALU.add))
            settle()
            step(v.tensor_tensor(lb[:, 1, :], lb[:, 1, :], lb_tmp[:, 0, :], ALU.subtract))
            settle()
            step(v.tensor_scalar(lb[:], lb[:], 0.0, LB_CEIL, ALU.max, ALU.min))
            settle()
            step(v.tensor_scalar(lb_floor[:], lb[:], LB_FLOOR, None, ALU.max))
            step(v.tensor_scalar(one_lb[:], lb[:], -1.0, 1.0, ALU.mult, ALU.add))
            settle()
            v.tensor_scalar(half_one_lb[:], one_lb[:], 0.5, None, ALU.mult).then_inc(params_ready, 1)

            def norm(l, w):
                if (l, w) == (0, 0):
                    feed(SPLITS)
                dve.wait_ge(rstd_ready, 2 * l + w + 1)
                last = (l, w) == (DEPTH - 1, 1)
                at = KT * (2 * l + w)

                def lo(k):
                    dve.wait_ge(h_hi_ready, at + k + 1)
                    sl = (slice(None), k, slice(None))
                    lo_of(h_parts, h_full[sl], sl).then_inc(h_ready, 1)

                for k in range(KT):
                    c = (C_FFN if w else C_ATTN) + KT * l + k
                    v.scalar_tensor_tensor(out=h_full[:, k, :], in0=xT[:, k, :], scalar=cols[:, c:c + 1], in1=rstd[:],
                                           op0=ALU.mult, op1=ALU.mult).then_inc(h_full_ready, 1)
                    if k >= 1 and not last:
                        lo(k - 1)
                if not last:
                    lo(KT - 1)

            def twice_silu(dst, name, l, j):
                n = JOB[name, l, j]
                feed(AHEAD[name, l, j])
                dve.wait_ge(th_ready, TH_OF[name, l, j] + 1)
                v.scalar_tensor_tensor(out=dst, in0=th[:, n % 4, :], scalar=1.0, in1=bank(n)[:, 0:T],
                                       op0=ALU.add, op1=ALU.mult).then_inc(job_taken[n % 4], 1)

            for l in range(DEPTH):
                norm(l, 0)
                if l == 0:
                    dve.wait_ge(params_ready, 1)
                for j in range(HEADS):
                    feed(AHEAD["f", l, j])
                    taken(dve, JOB["f", l, j])
                    step(v.tensor_scalar(expf[:, j, :], expf[:, j, :], EXP_CEIL, None, ALU.min))
                    settle()
                    step(v.tensor_scalar(sig[:, j, :], expf[:, j, :], 1.0, None, ALU.add))
                    settle()
                    step(v.reciprocal(sig[:, j, :], sig[:, j, :]))
                    settle()
                    v.scalar_tensor_tensor(out=kT[:, j, :], in0=expf[:, j, :], scalar=half_one_lb[:, l, j:j + 1],
                                           in1=sig[:, j, :], op0=ALU.mult, op1=ALU.mult).then_inc(key_ready, 1)
                    v.tensor_scalar(sig[:, j, :], sig[:, j, :], one_lb[:, l, j:j + 1], lb_floor[:, l, j:j + 1],
                                    ALU.mult, ALU.add).then_inc(forget_ready, 1)
                for k in range(KT):
                    dve.wait_ge(h_ready, KT * 2 * l + k + 1)
                for j in range(HEADS):
                    twice_silu(qT[:, j, :], "q", l, j)
                dve.wait_ge(logf_ready, l + 1)
                for j in range(HEADS):
                    v.tensor_tensor_scan(G[:, j, :], scan_keep[:], sig[:, j, :], 0.0, ALU.mult, ALU.add
                                         ).then_inc(gsum_ready, 1)
                dve.wait_ge(gsum_ready, HEADS * (l + 1))
                dve.wait_ge(key_ready, HEADS * (l + 1))

                def blocks(t, h):
                    return t.rearrange("p h t -> p (h t)").rearrange("p (b s r) -> p b s r", s=2, r=h)

                def scaled(lev):
                    return e_mem[:, lev % 2, :].rearrange("p (h t) -> p h t", h=HEADS)

                def arguments(lev):
                    if lev >= 3:
                        dve.wait_ge(level_done, NL * l + lev - 1)
                    h = P if LEVELS[lev] == "cross" else LEVELS[lev]
                    gb, eb = blocks(G[:], h), blocks(scaled(lev), h)
                    ref = gb[:, :, 0, h - 1:h].to_broadcast([P, HEADS * T // (2 * h), h])
                    v.tensor_tensor(eb[:, :, 0, :], ref, gb[:, :, 0, :], ALU.subtract).then_inc(arg_ready, 1)
                    if LEVELS[lev] == "cross":
                        v.tensor_copy(eb[:, :, 1, :], gb[:, :, 1, :]).then_inc(arg_ready, 1)
                    else:
                        v.tensor_tensor(eb[:, :, 1, :], gb[:, :, 1, :], ref, ALU.subtract).then_inc(arg_ready, 1)

                def scale_qk(lev):
                    dve.wait_ge(exp_ready, (NL - 1) * l + lev)
                    h = P if LEVELS[lev] == "cross" else LEVELS[lev]
                    eb, kb, qb = blocks(scaled(lev), h), blocks(kT, h), blocks(qT, h)
                    v.tensor_tensor(eb[:, :, 0, :], eb[:, :, 0, :], kb[:, :, 0, :], ALU.mult).then_inc(scaled_ready, 1)
                    v.tensor_tensor(eb[:, :, 1, :], eb[:, :, 1, :], qb[:, :, 1, :], ALU.mult).then_inc(scaled_ready, 1)

                def take(lev):
                    dve.wait_ge(level_done, NL * l + lev + 1)
                    pair = acc[2 * (lev % 2)], acc[2 * (lev % 2) + 1]
                    if LEVELS[lev] == "cross":
                        v.tensor_copy(score_x.rearrange("p h t -> p (h t)"), pair[0][:]).then_inc(level_taken, 2)
                        return
                    m = ident[:, :] if LEVELS[lev] == "diag" else masks[:, lev - 2, :]
                    m = m.unsqueeze(1).to_broadcast([P, HEADS, P])
                    if lev:
                        dve.wait_ge(level_taken, 2 * (NL * l + lev))
                    for a in range(TH):
                        ps = pair[a][:].rearrange("p (h t) -> p h t", h=HEADS)
                        dst = score if LEVELS[lev] == "diag" else masked
                        ins = v.tensor_tensor(dst[:, a], ps, m, ALU.mult)
                        if LEVELS[lev] == "diag":
                            ins.then_inc(level_taken, 1)
                        else:
                            step(ins)
                    if LEVELS[lev] != "diag":
                        settle()
                        for a in range(TH):
                            v.tensor_tensor(score[:, a], score[:, a], masked[:, a], ALU.add).then_inc(level_taken, 1)

                arguments(1)
                feed(AHEAD["u", l, 3])
                for j in range(HEADS):
                    twice_silu(og[:, j, :], "g", l, j)
                dve.wait_ge(win_ready, l + 1)
                step(v.tensor_tensor(pool_head[:, 0::2, :], pb[:, 0::2, PAD:2 * PAD], inv_pos[:, 0::2, :], ALU.mult))
                step(v.tensor_tensor(pool_head[:, 1::2, :], pc[:, 1::2, PAD:2 * PAD], inv_pos[:, 1::2, :], ALU.mult))
                settle()
                v.tensor_tensor(pu[:, :, PAD:2 * PAD], pool_head[:], pu[:, :, PAD:2 * PAD], ALU.subtract
                                ).then_inc(pooled_ready, 1)
                for g, w in enumerate(WINDOWS):
                    src = (pb, pc)[g % 2]
                    v.scalar_tensor_tensor(out=pu[:, g, 2 * PAD:], in0=src[:, g, 2 * PAD:], scalar=1.0 / w,
                                           in1=pu[:, g, 2 * PAD:], op0=ALU.mult, op1=ALU.subtract
                                           ).then_inc(pooled_ready, 1)
                for j in range(POOL_TILES):
                    dve.wait_ge(mix_hi_ready, POOL_TILES * l + j + 1)
                    sl = (slice(None), j, slice(None))
                    lo_of(mix_parts, mixed[sl], sl).then_inc(mix_ready, 1)
                dve.wait_ge(mix_ready, POOL_TILES * (l + 1))
                for j in range(HEADS):
                    taken(dve, JOB["q", l, j])
                    taken(dve, JOB["g", l, j])
                for lev in range(1, NL):
                    feed(AHEAD["gate", l, min(15, (lev - 1) // 2 * 4)])
                    scale_qk(lev)
                    if lev + 1 < NL:
                        feed(AHEAD["level", l, max(lev - 1, 0)] - 1)
                        arguments(lev + 1)
                    feed(AHEAD["level", l, lev - 1] - 1)
                    take(lev - 1)
                feed(AHEAD["level", l, NL - 1])
                take(NL - 1)

                def twice_gated(name, first):
                    for i in range(4):
                        n = JOB[name, l, i]
                        feed(AHEAD[name, l, i])
                        done(dve, n)
                        g = gates_mem[:, first * T + i * 512:first * T + (i + 1) * 512]
                        v.scalar_tensor_tensor(out=g, in0=g, scalar=1.0, in1=bank(n)[:], op0=ALU.add, op1=ALU.mult
                                               ).then_inc(job_taken[n % 4], 1)
                        yield i

                for _ in twice_gated("y_pool", 0):
                    pass
                feed(AHEAD["o", l])
                for i in range(2):
                    dve.wait_ge(o_sq_ready, 2 * l + i + 1)
                    step(v.tensor_copy(o_full[:, i * 512:(i + 1) * 512], acc[i][:]))
                settle()
                for i in range(2):
                    part = o_full[:, i * 512:(i + 1) * 512]
                    dve.wait_ge(o_rstd_ready, 2 * l + i + 1)
                    step(v.scalar_tensor_tensor(out=part, in0=part, scalar=half_hnorm[:, l:l + 1],
                                                in1=e_mem[:, 0, i * 512:(i + 1) * 512], op0=ALU.mult, op1=ALU.mult))
                settle()
                for i in range(2):
                    part = o_full[:, i * 512:(i + 1) * 512]
                    v.tensor_tensor(part, part, og_mem[:, i * 512:(i + 1) * 512], ALU.mult).then_inc(o_full_ready, 1)
                for i in range(2):
                    dve.wait_ge(o_hi_ready, 2 * l + i + 1)
                    sl = (slice(None), slice(2 * i, 2 * i + 2), slice(None))
                    lo_of(o_parts, o_full[:, i * 512:(i + 1) * 512].rearrange("p (h t) -> p h t", h=2), sl
                          ).then_inc(o_ready, 1)

                def merged_lo(i):
                    dve.wait_ge(merged_hi_ready, 4 * l + i + 1)
                    sl = (slice(None), slice(2 * i, 2 * i + 2), slice(None))
                    lo_of(merged_parts, gates[sl], sl).then_inc(merged_ready, 1)

                for i in twice_gated("y_hgrn", KT):
                    taken(dve, JOB["y_hgrn", l, i])
                    taken(dve, JOB["y_pool", l, i])
                    g = gates_mem[:, i * 512:(i + 1) * 512]
                    v.tensor_tensor(g, g, gates_mem[:, KT * T + i * 512:KT * T + (i + 1) * 512], ALU.add
                                    ).then_inc(merged_full_ready, 1)
                    if i >= 1:
                        merged_lo(i - 1)
                merged_lo(3)
                for d in range(KT):
                    n = JOB["w_out", l, d]
                    feed(AHEAD["w_out", l, d])
                    done(dve, n)
                    v.scalar_tensor_tensor(out=xT[:, d, :], in0=bank(n)[:, 0:T], scalar=0.5, in1=xT[:, d, :],
                                           op0=ALU.mult, op1=ALU.add).then_inc(job_taken[n % 4], 1)
                for d in range(KT):
                    taken(dve, JOB["w_out", l, d])
                norm(l, 1)
                if l == 0:
                    def hid_lo(tile):
                        n = JOB["ffn", tile]
                        dve.wait_ge(hid_hi_ready, tile + 1)
                        sl = (slice(None), tile // GT % 2, tile % GT, slice(None))
                        lo_of(hid_parts, th[:, n % 4, :], sl).then_inc(hid_ready, 1)

                    for tile in range(sum(DENSE)):
                        n = JOB["ffn", tile]
                        feed(AHEAD["ffn", tile])
                        dve.wait_ge(th_ready, TH_OF["ffn", tile] + 1)
                        v.scalar_tensor_tensor(out=th[:, n % 4, :], in0=th[:, n % 4, :], scalar=1.0,
                                               in1=bank(n)[:, 0:T], op0=ALU.add, op1=ALU.mult).then_inc(silu_half, 1)
                        dve.wait_ge(silu_half, tile + 1)
                        v.scalar_tensor_tensor(out=th[:, n % 4, :], in0=th[:, n % 4, :], scalar=0.5,
                                               in1=bank(n)[:, T:2 * T], op0=ALU.mult, op1=ALU.mult
                                               ).then_inc(job_taken[n % 4], 1)
                        if tile >= 1:
                            hid_lo(tile - 1)
                    hid_lo(sum(DENSE) - 1)
                    feed(AHEAD["down", len(DENSE) - 1])
                    dve.wait_ge(down_done, len(DENSE))
                    for i in range(4):
                        v.tensor_tensor(xT[:, 2 * i:2 * i + 2, :], acc[i][:].rearrange("p (d t) -> p d t", d=2),
                                        xT[:, 2 * i:2 * i + 2, :], ALU.add).then_inc(x_ready, 1)
                    dve.wait_ge(x_ready, 4)

            n = JOB["logits"]
            done(dve, n)
            v.tensor_copy(lg, bank(n)[:, 0:16].rearrange("p (a e) -> p a e", a=TH)).then_inc(job_taken[n % 4], 1)
            taken(dve, n)
            for a in range(TH):
                step(v.max(top_v[:, a, :], lg[:, a, :]))
            settle()
            for a in range(TH):
                step(v.max_index(top_i[:, a, :], top_v[:, a, :], lg[:, a, :]))
            v.tensor_tensor(gap, top_v[:, :, 1], top_v[:, :, 0], ALU.subtract).then_inc(gap_ready, 1)
            settle()
            step(v.tensor_copy(top_f, top_i[:]))
            settle()
            for a in range(TH):
                step(v.tensor_scalar(hot1[:, a, :], iota_e[:], top_f[:, a, 0:1], None, ALU.is_equal))
                step(v.tensor_scalar(hot2[:, a, :], iota_e[:], top_f[:, a, 1:2], None, ALU.is_equal))
            settle()
            v.tensor_tensor(chosen, hot1, hot2, ALU.add).then_inc(chosen_ready, 1)
            dve.wait_ge(gap_exp_ready, 1)
            step(v.tensor_scalar(gap_1, gap_e, 1.0, None, ALU.add))
            settle()
            step(v.reciprocal(w1, gap_1))
            settle()
            step(v.tensor_tensor(w2, w1, gap_e, ALU.mult))
            settle()
            for a in range(TH):
                step(v.tensor_scalar(wt1[:, a, :], hot1[:, a, :], w1[:, a:a + 1], None, ALU.mult))
                step(v.tensor_scalar(wt2[:, a, :], hot2[:, a, :], w2[:, a:a + 1], None, ALU.mult))
            settle()
            step(v.tensor_tensor(comb, wt1, wt2, ALU.add))
            step(v.memset(ones8, 1.0))
            n = JOB["ranks"]
            done(dve, n)
            step(v.tensor_scalar(rank1, bank(n)[:, 0:16].rearrange("p (a e) -> p a e", a=TH), 1.0, None, ALU.add))
            v.tensor_copy(count, bank(n)[:, 16:24]).then_inc(job_taken[n % 4], 1)
            settle()
            taken(dve, n)
            dve.wait_ge(chosen_ready, 1)
            step(v.tensor_tensor(rank1, rank1, chosen, ALU.mult))
            step(v.tensor_scalar(over1, count, float(CAP), None, ALU.is_gt))
            step(v.tensor_scalar(over2, count, 2.0 * CAP, None, ALU.is_gt))
            settle()
            step(v.tensor_scalar(rank1, rank1, -1.0, None, ALU.add))
            step(v.tensor_tensor(over, over1, over2, ALU.add))
            settle()
            step(v.tensor_tensor_scan(cum, ones8, over, 0.0, ALU.mult, ALU.add))
            settle()
            step(v.scalar_tensor_tensor(out=start, in0=cum, scalar=float(N_EXP), in1=over, op0=ALU.add,
                                        op1=ALU.subtract))
            step(v.tensor_scalar(n_f, cum[:, 7:8], float(N_EXP), None, ALU.add))
            settle()
            step(v.tensor_scalar(start1, start, 1.0, None, ALU.add))
            step(v.tensor_copy(n_items[:], n_f))

            def over_items(t):
                return t.unsqueeze(1).to_broadcast([P, COLS, N_EXP])

            settle()
            step(v.tensor_tensor(hot, iota_j[:], over_items(iota_e[:]), ALU.is_equal))
            step(v.tensor_tensor(one1, iota_j[:], over_items(start), ALU.is_equal))
            step(v.tensor_tensor(one2, iota_j[:], over_items(start1), ALU.is_equal))
            settle()
            step(v.tensor_tensor(one1, one1, over_items(over1), ALU.mult))
            step(v.tensor_tensor(one2, one2, over_items(over2), ALU.mult))
            settle()
            step(v.tensor_tensor(hot, hot, one1, ALU.add))
            step(v.tensor_reduce(base1, one1, AX_X, ALU.add))
            step(v.tensor_reduce(base2, one2, AX_X, ALU.add))
            settle()
            step(v.tensor_tensor(hot, hot, one2, ALU.add))
            step(v.scalar_tensor_tensor(out=base, in0=base2, scalar=2.0, in1=base1, op0=ALU.mult, op1=ALU.add))
            settle()
            step(v.tensor_scalar(base, base, float(CAP), None, ALU.mult))
            step(v.tensor_tensor(prod[:, 0], hot, over_items(iota_e[:]), ALU.mult))
            settle()
            step(v.tensor_reduce(e_f, prod[:, 0], AX_X, ALU.add))
            for a in range(TH):
                step(v.tensor_tensor(prod[:, 1 + a], hot, over_items(rank1[:, a, :]), ALU.mult))
            settle()
            step(v.tensor_copy(item_e[:], e_f))
            for a in range(TH):
                step(v.tensor_reduce(pos_item[:, a, :], prod[:, 1 + a], AX_X, ALU.add))
            settle()
            for a in range(TH):
                step(v.tensor_tensor(pos_item[:, a, :], pos_item[:, a, :], base, ALU.subtract))
                step(v.tensor_tensor(prod[:, 1 + a], hot, over_items(comb[:, a, :]), ALU.mult))
            settle()
            for a in range(TH):
                step(v.tensor_reduce(w_item[:, a, :], prod[:, 1 + a], AX_X, ALU.add))
            settle()
            v.memset(gap, 0.0).then_inc(tables_ready, 1)

            for a in range(TH):
                v.tensor_scalar(sel[:, a, :], iota_c[:], pos_item[:, a, 0:1], None, ALU.is_equal).then_inc(sel_ready, 1)

            def tokens_lo(first):
                for i in range(2):
                    dve.wait_ge(xe_hi_ready, first + (i + 1))
                    sl = (slice(None), slice(4 * i, 4 * i + 4), slice(None))
                    lo_of(xe_parts, job_bank[2 + i][:, 0:4 * CAP].rearrange("p (k c) -> p k c", k=4), sl
                          ).then_inc(xe_ready, 1)

            for c in range(SPLITS):
                lo_part(U_LOOP + c)
            v.memset(sel_wT[:, 0, :], 0.0).then_inc(pair_taken[0], 1)
            v.memset(sel_wT[:, 1, :], 0.0).then_inc(out_taken, 4)
            tokens_lo(0)
            dve.wait_ge(xe_ready, 2)
            v.memset(gap, 0.0).then_inc(pair_taken[1], 1)
            n_reg = dve.value_load(n_items[0:1, 0:1], min_val=N_EXP, max_val=ITEMS)
            with dve.Fori(0, n_reg) as it:
                feed_i = feeder_i(dve, it, n_reg, lambda c, i: lo_part(U_LOOP + c, i))
                dve.wait_ge(pair_done, it * (NG + 1) + 1)
                dve.wait_ge(sel_ready, it * 4 + 2)
                for a in range(TH):
                    v.tensor_scalar(sel[:, a, :], iota_c[:], pos_item[:, a, bass.ds(it + 1, 1)], None, ALU.is_equal
                                    ).then_inc(sel_ready, 1)
                    v.tensor_scalar(sel_w[:, a, :], iota_c[:], pos_item[:, a, bass.ds(it, 1)],
                                    w_item[:, a, bass.ds(it, 1)], ALU.is_equal, ALU.mult).then_inc(sel_ready, 1)

                def hidden_lo(i):
                    dve.wait_ge(hid_hi_ready, it * NG + (sum(DENSE) + i + 1))
                    sl = (slice(None), i % 2, slice(None), slice(None))
                    lo_of(he_parts, acc[2 + i % 2][:, 0:GT * CAP].rearrange("p (f c) -> p f c", f=GT), sl
                          ).then_inc(hid_ready, 1)

                for i in range(NG):
                    if i >= 1:
                        feed_i(MOE_UNIT["g", i, 1] + 1 + SPLITS)
                        hidden_lo(i - 1)
                    feed_i(MOE_UNIT["u", i, 1] + SPLITS)
                    dve.wait_ge(th_ready, it * NG + (TH_LOOP + i + 1))
                    v.scalar_tensor_tensor(out=th_e[:, i % 2, :], in0=th_e[:, i % 2, :], scalar=1.0,
                                           in1=job_bank[2 * (i % 2)][0:CAP, :], op0=ALU.add, op1=ALU.mult
                                           ).then_inc(silu_half, 1)
                    dve.wait_ge(silu_half, it * NG + (sum(DENSE) + i + 1))
                    v.scalar_tensor_tensor(out=th_e[:, i % 2, :], in0=th_e[:, i % 2, :], scalar=0.5,
                                           in1=job_bank[2 * (i % 2) + 1][0:CAP, :], op0=ALU.mult, op1=ALU.mult
                                           ).then_inc(pair_taken[i % 2], 1)
                feed_i(MOE_UNIT["d", NG - 2, 1] + 1 + SPLITS)
                hidden_lo(NG - 1)
                tokens_lo(it * 2 + 2)
                v.tensor_copy(sel_wT[:, 0, :], job_bank[2][0:CAP, 4 * CAP:4 * CAP + P]).then_inc(xe_ready, 1)
                v.tensor_copy(sel_wT[:, 1, :], job_bank[3][0:CAP, 4 * CAP:4 * CAP + P]).then_inc(pair_taken[1], 1)
                feed_i(ITEM_UNITS - 1 + SPLITS)
                dve.wait_ge(down_done, it * NG + (DN_LOOP + NG))
                v.tensor_copy(y_tok[:, 0:512], acc[0][0:CAP, :]).then_inc(y_dve, 1)
                feed_i(ITEM_UNITS + SPLITS)
                for q in range(4):
                    dve.wait_ge(out_done, it * 4 + (q + 1))
                    dve.wait_ge(out_taken, it * 4 + (q + 1))
                    dst = x_tok[:, q // 2, (q % 2) * 512:(q % 2) * 512 + 512]
                    v.tensor_tensor(dst, acc[(2 + q) % 4][:], dst, ALU.add).then_inc(out_taken, 1)

            dve.wait_ge(fin_rstd, 1)
            dve.wait_ge(fnw_landed, 16)
            for a in range(TH):
                v.scalar_tensor_tensor(out=h_tok[:, a, :], in0=x_tok[:, a, :], scalar=fin[:, 4 + a:5 + a],
                                       in1=qk_mem[:, 0:D], op0=ALU.mult, op1=ALU.mult).then_inc(fin_ready, 1)

        @block.tensor
        def _(pe):
            def bank(n):
                return job_bank[n % 4]

            def split(name, l, c, part):
                n = UNIT_OF[name, l, c, part]
                pe.wait_ge(lo_dve, n + 1)
                pe.wait_ge(lo_pool, n + 1)
                return n % SPLITS

            def three(out, ops, first, last, **kw):
                (s_hi, s_lo), (m_hi, m_lo) = ops
                nc.tensor.matmul(out, s_hi, m_hi, start=first, stop=False, **kw)
                nc.tensor.matmul(out, s_hi, m_lo, start=False, stop=False, **kw)
                return nc.tensor.matmul(out, s_lo, m_hi, start=False, stop=last, **kw)

            pe.wait_ge(consts, 1)
            n = JOB["params"]
            pe.wait_ge(params_landed, 16 * 6)
            nc.tensor.transpose(bank(n)[:, 0:C_ROWS], rows[:, :], ident[0:C_ROWS, 0:C_ROWS]).then_inc(job_done, 1)
            pe.wait_ge(x_landed, 16)
            for i in range(4):
                n = JOB["x_in", i]
                bank_free(pe, n)
                a, k0 = i // 2, 4 * (i % 2)
                for k in range(4):
                    mm = nc.tensor.transpose(bank(n)[:, k * P:(k + 1) * P],
                                             x_tok[:, a, (k0 + k) * P:(k0 + k + 1) * P], ident[:])
                mm.then_inc(job_done, 1)

            def norm(l, w):
                n = JOB["norm", l, w]
                bank_free(pe, n)
                for k in range(KT):
                    if k % 4 == 0:
                        pe.wait_ge(sq_ready, 2 * (2 * l + w) + k // 4 + 1)
                    mm = nc.tensor.matmul(bank(n)[:, 0:T], mean_d[:], sq[:, k, :], start=(k == 0), stop=(k == KT - 1))
                mm.then_inc(job_done, 1)

            def project(name, l, c, keys, src, width=GROUP, at=0, h_wait=None, free=True, kts=KT):
                per = UNIT // width
                parts = kts // per
                for part in range(parts):
                    b = split(name, l, c, part)
                    hi, lo = kf(w_hi, b, width), kf(w_lo, b, width)
                    for j, key in enumerate(keys):
                        n = JOB[key]
                        if part == 0 and free:
                            bank_free(pe, n)
                        for k in range(per):
                            kk = part * per + k
                            if h_wait and j == 0:
                                h_wait(kk)
                            fs = slice(j * P, (j + 1) * P)
                            mm = three(bank(n)[:, at:at + T], ((hi[:, k, fs], lo[:, k, fs]),
                                                               (src[0][:, kk, :], src[1][:, kk, :])),
                                       kk == 0, kk == kts - 1)
                        if part == parts - 1 and name != "dense_g":
                            mm.then_inc(job_done, 1)
                    if part < parts - 1 or name == "dense_g":
                        mm.then_inc(unit_done, 1)

            def project_up(name, l, key, src):
                for part in range(2):
                    b = split(name, l, 0, part)
                    hi, lo = fd(w_hi, b), fd(w_lo, b)
                    for i in range(4):
                        n = JOB[key, l, i]
                        if part == 0:
                            bank_free(pe, n)
                        for h in range(2):
                            ds = slice((2 * i + h) * P, (2 * i + h + 1) * P)
                            for k in range(2):
                                kk = 2 * part + k
                                mm = three(bank(n)[:, h * T:(h + 1) * T], ((hi[:, k, ds], lo[:, k, ds]),
                                                                           (src[0][:, kk, :], src[1][:, kk, :])),
                                           kk == 0 and h == 0, kk == 3, skip_group_check=True)
                        if part == 1:
                            mm.then_inc(job_done, 1)
                    if part == 0:
                        mm.then_inc(unit_done, 1)

            def level(l, lev):
                if lev >= 2:
                    pe.wait_ge(level_taken, 2 * (NL * l + lev - 1))
                if LEVELS[lev] != "diag":
                    pe.wait_ge(scaled_ready, 2 * ((NL - 1) * l + lev))
                e = e_mem[:, lev % 2, :].rearrange("p (h t) -> p h t", h=HEADS)
                pair = acc[2 * (lev % 2)], acc[2 * (lev % 2) + 1]
                for hd in range(HEADS):
                    for a in range(1 if LEVELS[lev] == "cross" else TH):
                        ts = slice(a * P, (a + 1) * P)
                        if LEVELS[lev] == "diag":
                            s_op, t_op = kT[:, hd, ts], qT[:, hd, ts]
                        elif LEVELS[lev] == "cross":
                            s_op, t_op = e[:, hd, 0:P], e[:, hd, P:T]
                        else:
                            s_op, t_op = e[:, hd, ts], e[:, hd, ts]
                        mm = nc.tensor.matmul(pair[a][:, hd * P:(hd + 1) * P], s_op, t_op, start=True, stop=True)
                mm.then_inc(level_done, 1)

            for l in range(DEPTH):
                norm(l, 0)

                def h_wait(k, l=l, w=0):
                    pe.wait_ge(h_ready, KT * (2 * l + w) + k + 1)

                for name in "fq":
                    project(name, l, 0, [(name, l, j) for j in range(4)], h_parts,
                            h_wait=h_wait if name == "f" else None)
                for part in range(2):
                    b = split("v", l, 0, part)
                    for a in range(TH):
                        n = JOB["v", l, a]
                        if part == 0:
                            bank_free(pe, n)
                        for k in range(4):
                            kk = 4 * part + k
                            ts = slice(a * P, (a + 1) * P)
                            mm = three(bank(n)[:], ((h_parts[0][:, kk, ts], h_parts[1][:, kk, ts]),
                                                    (kf(w_hi, b)[:, k, :], kf(w_lo, b)[:, k, :])), kk == 0, kk == KT - 1)
                        if part == 1:
                            mm.then_inc(job_done, 1)
                    if part == 0:
                        mm.then_inc(unit_done, 1)
                for name in "ug":
                    project(name, l, 0, [(name, l, j) for j in range(4)], h_parts)
                pe.wait_ge(pooled_ready, 5 * (l + 1))
                pe.wait_ge(poolw_landed, 16 * (l + 1))
                for g in range(POOL_TILES):
                    n = JOB["mix", l, g]
                    bank_free(pe, n)
                    nc.tensor.matmul(bank(n)[:, 0:T], poolw[:, g, :], pu[:, g, PAD:], start=True, stop=True
                                     ).then_inc(job_done, 1)
                for c in range(4):
                    project("gate", l, c, [("gate", l, 4 * c + j) for j in range(4)], h_parts)
                    if c == 0:
                        for q in range(HEADS):
                            taken(pe, JOB["q", l, q])
                        pe.wait_ge(key_ready, HEADS * (l + 1))
                    level(l, 2 * c)
                    level(l, 2 * c + 1)
                level(l, NL - 1)
                pe.wait_ge(mix_ready, POOL_TILES * (l + 1))
                project_up("pool_up", l, "y_pool", mix_parts)
                pe.wait_ge(level_taken, 2 * NL * (l + 1))
                for j in range(TH):
                    taken(pe, JOB["v", l, j])
                for hd in range(HEADS):
                    hs = slice(hd * P, (hd + 1) * P)
                    o_a = acc[hd // 2][:, (hd % 2) * T:(hd % 2) * T + P]
                    o_b = acc[hd // 2][:, (hd % 2) * T + P:(hd % 2) * T + T]
                    nc.tensor.matmul(o_a, v_tok[:, 0, hs], score[:, 0, hd, :], start=True, stop=True)
                    nc.tensor.matmul(o_b, v_tok[:, 0, hs], score_x[:, hd, :], start=True, stop=False)
                    mm = nc.tensor.matmul(o_b, v_tok[:, 1, hs], score[:, 1, hd, :], start=False, stop=True)
                    if hd % 2:
                        mm.then_inc(o_done, 1)
                for i in range(2):
                    pe.wait_ge(o_sq_ready, 2 * l + i + 1)
                    nc.tensor.matmul(acc[2 + i][:], mean_h[:], o_sq[:, i * 512:(i + 1) * 512], start=True, stop=True
                                     ).then_inc(o_mean_done, 1)
                pe.wait_ge(o_ready, 2 * (l + 1))
                project_up("hgrn_up", l, "y_hgrn", o_parts)
                for c in range(2):
                    project("w_out", l, c, [("w_out", l, 4 * c + j) for j in range(4)], merged_parts,
                            h_wait=(lambda k: pe.wait_ge(merged_ready, 4 * l + k // 2 + 1)) if c == 0 else None)
                norm(l, 1)
                if l == 0:
                    def down(i):
                        parts = 2 if DENSE[i] == GT else 1
                        for part in range(parts):
                            b = split("dense_d", 0, i, part)
                            for f in range(2):
                                ff = 2 * part + f
                                pe.wait_ge(hid_ready, sum(DENSE[:i]) + ff + 1)
                                for d in range(KT):
                                    ds = slice(d * P, (d + 1) * P)
                                    mm = three(acc[d // 2][:, (d % 2) * T:(d % 2) * T + T],
                                               ((fd(w_hi, b)[:, f, ds], fd(w_lo, b)[:, f, ds]),
                                                (hid_parts[0][:, i % 2, ff, :], hid_parts[1][:, i % 2, ff, :])),
                                               i == 0 and ff == 0 and d % 2 == 0,
                                               i == len(DENSE) - 1 and ff == DENSE[i] - 1, skip_group_check=True)
                            mm.then_inc(down_done if part == parts - 1 else unit_done, 1)

                    for i, tiles in enumerate(DENSE):
                        keys = [("ffn", sum(DENSE[:i]) + f) for f in range(tiles)]
                        project("dense_g", 0, i, keys, h_parts, width=tiles * P,
                                h_wait=(lambda k: h_wait(k, l, 1)) if i == 0 else None)
                        project("dense_u", 0, i, keys, h_parts, width=tiles * P, at=T, free=False)
                        if i >= 1:
                            down(i - 1)
                    down(len(DENSE) - 1)

            n = JOB["logits"]
            bank_free(pe, n)
            pe.wait_ge(router_landed, 16)
            for a in range(TH):
                for k in range(KT):
                    if a == 0:
                        pe.wait_ge(h_full_ready, KT * (2 * DEPTH - 1) + k + 1)
                    mm = nc.tensor.matmul(bank(n)[:, a * N_EXP:(a + 1) * N_EXP], h_full[:, k, a * P:(a + 1) * P],
                                          router[:, k, :], start=(k == 0), stop=(k == KT - 1))
            mm.then_inc(job_done, 1)
            for name, src in (("h_tok", h_full), ("x_tok", xT)):
                for i in range(4):
                    n = JOB[name, i]
                    bank_free(pe, n)
                    for k in range(4):
                        kk = (i % 2) * 4 + k
                        mm = nc.tensor.transpose(bank(n)[:, k * P:(k + 1) * P],
                                                 src[:, kk, (i // 2) * P:(i // 2 + 1) * P], ident[:])
                    mm.then_inc(job_done, 1)
            n = JOB["ranks"]
            bank_free(pe, n)
            pe.wait_ge(chosen_ready, 1)
            b = bank(n)
            nc.tensor.matmul(b[:, 0:8], before[:], chosen[:, 0, :], start=True, stop=True)
            nc.tensor.matmul(b[:, 8:16], ones[:], chosen[:, 0, :], start=True, stop=False)
            nc.tensor.matmul(b[:, 8:16], before[:], chosen[:, 1, :], start=False, stop=True)
            nc.tensor.matmul(b[:, 16:24], ones[:], chosen[:, 0, :], start=True, stop=False)
            nc.tensor.matmul(b[:, 16:24], ones[:], chosen[:, 1, :], start=False, stop=True).then_inc(job_done, 1)

            def gather():
                for k in range(KT):
                    for a in range(TH):
                        mm = nc.tensor.matmul(job_bank[2 + k // 4][:, (k % 4) * CAP:(k % 4 + 1) * CAP],
                                              h_tok[:, a, k * P:(k + 1) * P], sel[:, a, :],
                                              start=(a == 0), stop=(a == TH - 1))
                mm.then_inc(pair_done, 1)

            for i in range(4):
                taken(pe, JOB["h_tok", i])
            for n in range(len(JOB) - 4, len(JOB)):
                taken(pe, n)
            pe.wait_ge(sel_ready, TH)
            gather()
            pe.wait_ge(tables_ready, 1)
            n_reg = pe.value_load(n_items[0:1, 0:1], min_val=N_EXP, max_val=ITEMS)
            with pe.Fori(0, n_reg) as it:
                def split_i(kind, i, part):
                    n = U_LOOP + MOE_UNIT[kind, i, part]
                    pe.wait_ge(lo_dve, it * ITEM_UNITS + (n + 1))
                    pe.wait_ge(lo_pool, it * ITEM_UNITS + (n + 1))
                    return n % SPLITS

                def hidden(kind, i):
                    ps = job_bank[2 * (i % 2) + (kind == "u")][0:CAP, :]
                    for part in range(2):
                        b = split_i(kind, i, part)
                        for k in range(4):
                            kk = 4 * part + k
                            mm = three(ps, ((xe_parts[0][:, kk, :], xe_parts[1][:, kk, :]),
                                            (kf(w_hi, b)[:, k, :], kf(w_lo, b)[:, k, :])), kk == 0, kk == KT - 1)
                        mm.then_inc(pair_done if (kind, part) == ("u", 1) else unit_done, 1)

                def turn(i):
                    pe.wait_ge(pair_taken[i % 2], it * 4 + (i // 2 + 2))
                    if i < 2:
                        pe.wait_ge(out_taken, it * 4 + 4)
                    else:
                        pe.wait_ge(hid_ready, it * NG + (sum(DENSE) + i - 1))
                    for f in range(GT):
                        mm = nc.tensor.transpose(acc[2 + i % 2][:, f * CAP:(f + 1) * CAP],
                                                 th_e[:, i % 2, f * P:(f + 1) * P], ident[0:CAP, 0:CAP])
                    mm.then_inc(turned, 1)

                def down_i(i):
                    for part in range(2):
                        b = split_i("d", i, part)
                        if part == 0:
                            pe.wait_ge(hid_ready, it * NG + (sum(DENSE) + i + 1))
                        for f in range(2):
                            ff = 2 * part + f
                            for q in range(2):
                                qs = slice(q * 512, (q + 1) * 512)
                                mm = three(acc[q][0:CAP, :],
                                           ((he_parts[0][:, i % 2, ff, :], he_parts[1][:, i % 2, ff, :]),
                                            (fd(w_hi, b)[:, f, qs], fd(w_lo, b)[:, f, qs])),
                                           i == 0 and ff == 0, i == NG - 1 and ff == GT - 1)
                        mm.then_inc(unit_done if part == 0 else down_done, 1)

                pe.wait_ge(xe_ready, it * 3 + 2)
                for i in range(NG):
                    pe.wait_ge(pair_taken[i % 2], it * 4 + (i // 2 + 1))
                    hidden("g", i)
                    if i >= 1:
                        turn(i - 1)
                    hidden("u", i)
                    if i >= 1:
                        down_i(i - 1)
                turn(NG - 1)
                pe.wait_ge(pair_taken[1], it * 4 + (NG // 2 + 1))
                pe.wait_ge(sel_ready, it * 4 + 6)
                for a in range(TH):
                    nc.tensor.transpose(job_bank[2 + a][0:CAP, 4 * CAP:4 * CAP + P], sel_w[:, a, :], ident[:])
                gather()
                down_i(NG - 1)
                pe.wait_ge(xe_ready, it * 3 + 5)
                pe.wait_ge(pair_taken[1], it * 4 + (NG // 2 + 2))
                for q in range(4):
                    if q % 2:
                        pe.wait_ge(y_act, it + 1)
                    else:
                        pe.wait_ge(y_dve, it + 1)
                    nc.tensor.matmul(acc[(2 + q) % 4][:], sel_wT[:, q // 2, :],
                                     y_tok[:, (q % 2) * 512:(q % 2) * 512 + 512], start=True, stop=True
                                     ).then_inc(out_done, 1)


_INS = ["x", "attn_norm_w", "w_in", "gate_bias", "pool_w", "pool_scale", "pool_up", "hgrn_lower_bounds",
        "hgrn_norm_w", "hgrn_up", "w_out", "ffn_norm_w", "dense_w_gate", "dense_w_up", "dense_w_down",
        "moe_router", "moe_w_gate", "moe_w_up", "moe_w_down", "final_norm_w"]


def kernel(**inputs):
    import numpy as _np
    import concourse.bacc as _bacc
    from concourse import mybir as _mybir
    from concourse.bass_utils import run_bass_kernel_spmd as _run

    nc = _bacc.Bacc("TRN2", target_bir_lowering=False, num_devices=1)
    arrays, args = {}, []
    for name in _INS:
        a = _np.ascontiguousarray(inputs[name])
        arrays[f"in_{name}"] = a
        args.append(nc.dram_tensor(f"in_{name}", a.shape, _mybir.dt.from_np(a.dtype), kind="ExternalInput").ap())
    args.append(nc.dram_tensor("out_0", (1, T, D), F32, kind="ExternalOutput").ap())
    build(nc, *args)
    r = _run(nc, [arrays], core_ids=[0])
    return r.results[0]["out_0"]
```

```python
from contextlib import ExitStack

import concourse.bass as bass
from concourse import mybir

F32 = mybir.dt.float32
F32R = mybir.dt.float32r
I32 = mybir.dt.int32
U32 = mybir.dt.uint32
U8 = mybir.dt.uint8
ALU = mybir.AluOpType
ACT = mybir.ActivationFunctionType
AX_X = mybir.AxisListType.X

P = 128
T = 256
TH = T // P
D = 1024
KT = D // P
DEPTH = 2
HEADS = 4
POOL_TILES = 4
WINDOWS = (2, 4, 8, 16)
PAD = 16
F_DENSE = 2816
N_EXP = 8
F_EXP = 3584
EPS = 1e-6
LB_FLOOR = 1e-30
LB_CEIL = 1.0 - 1e-6
EXP_CEIL = 1e37

RING = 7
LN_EXP = "natural_log_exp_and_others"
UNIT = 2048
SPLITS = 3
POOL_QUARTERS = 2
POOL_QUARTERS_EXP = 1
GROUP = 512
GT = GROUP // P
CAP = 96
MAX_EXTRA = (2 * T) // (CAP + 1)
ITEMS = N_EXP + MAX_EXTRA
COLS = ITEMS + 1

LEVELS = ["diag", "cross"] + [64, 32, 16, 8, 4, 2, 1]
NL = len(LEVELS)

C_ATTN, C_FFN, C_BIAS, C_PSCALE, C_LB, C_HNORM, C_ROWS = 0, 16, 32, 64, 72, 80, 82


def dense_groups(width):
    out = []
    while width > 0:
        out.append(min(GT, width // P))
        width -= GROUP
    return out


DENSE = dense_groups(F_DENSE)
EXPERT = dense_groups(F_EXP)


def swiglu_order(groups):
    out = []
    for i in range(len(groups)):
        out += [("g", i), ("u", i)]
        if i >= 1:
            out.append(("d", i - 1))
    return out + [("d", len(groups) - 1)]


def plan():
    jobs, units, ahead = {}, [], {}
    a_units = [0]

    def job(*key):
        jobs[key if len(key) > 1 else key[0]] = len(jobs)
        event(*key)

    def event(*key):
        ahead[key if len(key) > 1 else key[0]] = len(units) + SPLITS

    def chunk(name, l, c, parts, keys, last="job", value=None):
        for key in keys:
            job(*key)
        for part in range(parts):
            if part < parts - 1:
                a_units[0] += 1
                units.append((name, l, c, part, "unit", a_units[0]))
            else:
                units.append((name, l, c, part, last, keys[-1] if last == "job" else value))
        for key in keys:
            ahead[key] = len(units) - 1 + SPLITS
        if last == "down":
            ahead["down", c] = len(units) - 1 + SPLITS

    for i in range(4):
        job("x_in", i)
    job("params")
    for l in range(DEPTH):
        for name, n in (("f", 4), ("q", 4), ("v", 2), ("u", 4)):
            chunk(name, l, 0, 2, [(name, l, j) for j in range(n)])
        for c in range(4):
            chunk("gate", l, c, 2, [("gate", l, 4 * c + j) for j in range(4)])
            if c == 0:
                for j in range(POOL_TILES):
                    job("mix", l, j)
        chunk("g", l, 0, 2, [("g", l, j) for j in range(4)])
        event("o", l)
        chunk("pool_up", l, 0, 2, [("y_pool", l, j) for j in range(4)])
        chunk("hgrn_up", l, 0, 2, [("y_hgrn", l, j) for j in range(4)])
        for c in range(2):
            chunk("w_out", l, c, 2, [("w_out", l, 4 * c + j) for j in range(4)])
        if l == 0:
            for kind, i in swiglu_order(DENSE):
                full = 2 if DENSE[i] == GT else 1
                first = sum(DENSE[:i])
                if kind == "g":
                    for part in range(full):
                        a_units[0] += 1
                        units.append(("dense_g", l, i, part, "unit", a_units[0]))
                elif kind == "u":
                    chunk("dense_u", l, i, full, [("ffn", first + j) for j in range(DENSE[i])])
                else:
                    chunk("dense_d", l, i, full, [], "down", i + 1)
    for k in range(2):
        for a in range(TH):
            job("h_tok", 2 * a + k)
    job("ranks")
    return jobs, units, ahead, a_units[0]


def build(nc, x, attn_norm_w, w_in, gate_bias, pool_w, pool_scale, pool_up, hgrn_lower_bounds,
          hgrn_norm_w, hgrn_up, w_out, ffn_norm_w, dense_w_gate, dense_w_up, dense_w_down,
          moe_router, moe_w_gate, moe_w_up, moe_w_down, final_norm_w, out):
    JOB, UNITS, AHEAD, A_LOOP = plan()
    U_LOOP = len(UNITS)
    UNIT_OF = {u[:4]: n for n, u in enumerate(UNITS)}
    MOE = [(kind, i, part) for kind, i in swiglu_order(EXPERT) for part in range(2)]
    ITEM_UNITS = len(MOE)
    MOE_UNIT = {c: n for n, c in enumerate(MOE)}
    NG = len(EXPERT)
    assert ITEM_UNITS % RING == 0 and ITEM_UNITS % SPLITS == 0 and set(EXPERT) == {GT} and NG % 2 == 1
    MOE_FREED, a_item = [], 0
    for kind, i, part in MOE:
        if part == 1 and kind == "u":
            MOE_FREED.append(("pair", i + 1 + (i == NG - 1)))
        elif part == 1 and kind == "d":
            MOE_FREED.append(("down", i + 1))
        else:
            a_item += 1
            MOE_FREED.append(("unit", a_item))
    DN_LOOP = len(DENSE)
    TH_LOOP = DEPTH * 8 + sum(DENSE)
    TH_OF = {}
    for l in range(DEPTH):
        for name in "qg":
            for j in range(4):
                TH_OF[name, l, j] = len(TH_OF)
        if l == 0:
            for j in range(sum(DENSE)):
                TH_OF["ffn", j] = len(TH_OF)

    with ExitStack() as ctx:
        def sb(name, shape, dt=F32):
            return ctx.enter_context(nc.sbuf_tensor(name, shape, dt))

        def sem(name):
            return ctx.enter_context(nc.semaphore(name))

        ring = sb("ring", [P, RING, UNIT])
        w_hi = sb("w_hi", [P, SPLITS, UNIT], F32R)
        w_lo = sb("w_lo", [P, SPLITS, UNIT], F32R)
        xT = sb("xT", [P, KT, T])
        a_hi = sb("a_hi", [P, KT * T], F32R)
        a_lo = sb("a_lo", [P, KT * T], F32R)
        b_hi = sb("b_hi", [P, KT * T], F32R)
        b_lo = sb("b_lo", [P, KT * T], F32R)
        qk_mem = sb("qk_mem", [P, KT * T])
        gates_mem = sb("gates_mem", [P, 16 * T])
        G = sb("G", [P, HEADS, T])
        og_mem = sb("og_mem", [P, HEADS * T])
        v_tok = sb("v_tok", [P, TH, HEADS * P])
        e_mem = sb("e_mem", [P, 2, HEADS * T])
        score_mem = sb("score_mem", [P, 3 * 512])
        th_mem = sb("th_mem", [P, 4 * T])
        masks = sb("masks", [P, NL - 2, P], U8)
        ident = sb("ident", [P, P])
        mean_d = sb("mean_d", [P, P])
        mean_h = sb("mean_h", [P, P])
        ones = sb("ones", [P, P])
        before = sb("before", [P, P])
        cols = sb("cols", [P, C_ROWS])
        half_bias = sb("half_bias", [P, 32])
        half_hnorm = sb("half_hnorm", [P, DEPTH])
        lb = sb("lb", [P, DEPTH, HEADS])
        lb_floor = sb("lb_floor", [P, DEPTH, HEADS])
        one_lb = sb("one_lb", [P, DEPTH, HEADS])
        half_one_lb = sb("half_one_lb", [P, DEPTH, HEADS])
        lb_tmp = sb("lb_tmp", [P, 4, HEADS])
        eps = sb("eps", [P, 1])
        poolw = sb("poolw", [P, POOL_TILES, P])
        rstd = sb("rstd", [P, T])
        inv_pos = sb("inv_pos", [P, POOL_TILES, PAD])
        pool_head = sb("pool_head", [P, POOL_TILES, PAD])
        router = sb("router", [P, KT, N_EXP])
        iota_e = sb("iota_e", [P, N_EXP])
        iota_c = sb("iota_c", [P, CAP])
        iota_j = sb("iota_j", [P, COLS, N_EXP])
        top_i = sb("top_i", [P, TH, 8], U32)
        pos_item = sb("pos_item", [P, TH, COLS])
        w_item = sb("w_item", [P, TH, COLS])
        item_e = sb("item_e", [P, COLS], I32)
        n_items = sb("n_items", [P, 1], I32)
        fin = sb("fin", [P, 6])
        one_more = sb("one_more", [P, 1])

        h_full = qk_mem[:, :].rearrange("p (k t) -> p k t", k=KT)
        sq = e_mem[:, :, :].rearrange("p a (k t) -> p (a k) t", t=T)
        qT = qk_mem[:, 0:HEADS * T].rearrange("p (h t) -> p h t", h=HEADS)
        kT = qk_mem[:, HEADS * T:].rearrange("p (h t) -> p h t", h=HEADS)
        gates = gates_mem[:, :].rearrange("p (k t) -> p k t", k=16)
        og = og_mem[:, :].rearrange("p (h t) -> p h t", h=HEADS)
        expf = e_mem[:, 0, :].rearrange("p (h t) -> p h t", h=HEADS)
        sig = e_mem[:, 1, :].rearrange("p (h t) -> p h t", h=HEADS)
        PW = POOL_TILES * (PAD + T)
        pu, pb, pc = (m.rearrange("p (g t) -> p g t", g=POOL_TILES) for m in
                      (gates_mem[:, 16 * T - PW:], score_mem[:, 0:PW], gates_mem[:, 16 * T - 2 * PW:16 * T - PW]))
        th = th_mem[:, :].rearrange("p (b t) -> p b t", b=4)
        score = score_mem[:, 0:TH * HEADS * P].rearrange("p (a h t) -> p a h t", a=TH, h=HEADS)
        score_x = score_mem[:, 1024:1536].rearrange("p (h t) -> p h t", h=HEADS)
        mixed = og_mem[:, :].rearrange("p (g t) -> p g t", g=POOL_TILES)
        o_sq = th_mem
        rows = th_mem[0:C_ROWS, 0:P]
        mask_f = score_mem[:, 0:(NL - 2) * P].rearrange("p (m t) -> p m t", m=NL - 2)
        o_full = e_mem[:, 1, :]
        h_tok = gates_mem[:, 0:TH * D].rearrange("p (a d) -> p a d", a=TH)
        x_tok = gates_mem[:, TH * D:].rearrange("p (a d) -> p a d", a=TH)

        def tiles_of(mem, n=KT, at=0):
            return mem[:, at:at + n * T].rearrange("p (k t) -> p k t", k=n)

        h_parts = tiles_of(a_hi), tiles_of(a_lo)
        mix_parts = tiles_of(b_hi, 4), tiles_of(b_lo, 4)
        o_parts = tiles_of(b_hi, 4, 4 * T), tiles_of(b_lo, 4, 4 * T)
        merged_parts = h_parts
        hid_parts = tuple(m[:, :].rearrange("p (b f t) -> p b f t", b=2, f=GT) for m in (b_hi, b_lo))
        xe_parts = tuple(m[:, 0:KT * CAP].rearrange("p (k c) -> p k c", k=KT) for m in (a_hi, a_lo))
        he_parts = tuple(m[:, 0:2 * GT * CAP].rearrange("p (b f c) -> p b f c", b=2, f=GT) for m in (b_hi, b_lo))
        th_e = th_mem[0:CAP, :].rearrange("p (b f) -> p b f", b=2)
        y_tok = G[0:CAP, :, :].rearrange("p h t -> p (h t)")
        sel = og_mem[:, 0:TH * CAP].rearrange("p (a c) -> p a c", a=TH)
        sel_w = og_mem[:, TH * CAP:2 * TH * CAP].rearrange("p (a c) -> p a c", a=TH)
        sel_wT = og_mem[0:CAP, 2 * TH * CAP:2 * TH * CAP + T].rearrange("p (a c) -> p a c", a=TH)
        at = [0]

        def scratch(*shape):
            n = 1
            for s in shape:
                n *= s
            v = score_mem[:, at[0]:at[0] + n]
            at[0] += n
            return v

        lg = scratch(TH, 8).rearrange("p (a e) -> p a e", a=TH)
        top_v = scratch(TH, 8).rearrange("p (a e) -> p a e", a=TH)
        top_f = scratch(TH, 8).rearrange("p (a e) -> p a e", a=TH)
        gap = scratch(TH)
        gap_e = scratch(TH)
        gap_1 = scratch(TH)
        w1 = scratch(TH)
        w2 = scratch(TH)
        hot1 = scratch(TH, 8).rearrange("p (a e) -> p a e", a=TH)
        hot2 = scratch(TH, 8).rearrange("p (a e) -> p a e", a=TH)
        wt1 = scratch(TH, 8).rearrange("p (a e) -> p a e", a=TH)
        wt2 = scratch(TH, 8).rearrange("p (a e) -> p a e", a=TH)
        chosen = scratch(TH, 8).rearrange("p (a e) -> p a e", a=TH)
        comb = scratch(TH, 8).rearrange("p (a e) -> p a e", a=TH)
        rank1 = scratch(TH, 8).rearrange("p (a e) -> p a e", a=TH)
        count = scratch(8)
        over1 = scratch(8)
        over2 = scratch(8)
        over = scratch(8)
        cum = scratch(8)
        start = scratch(8)
        start1 = scratch(8)
        ones8 = scratch(8)
        one1 = scratch(COLS, 8).rearrange("p (j e) -> p j e", e=8)
        one2 = scratch(COLS, 8).rearrange("p (j e) -> p j e", e=8)
        hot = scratch(COLS, 8).rearrange("p (j e) -> p j e", e=8)
        prod = scratch(3, COLS, 8).rearrange("p (a j e) -> p a j e", a=3, e=8)
        base1 = scratch(COLS)
        base2 = scratch(COLS)
        base = scratch(COLS)
        e_f = scratch(COLS)
        n_f = scratch(1)

        job_bank = [ctx.enter_context(nc.psum_tensor(f"job_bank{i}", [P, 512], F32)) for i in range(4)]
        acc = [ctx.enter_context(nc.psum_tensor(f"acc{i}", [P, 512], F32)) for i in range(4)]

        landed = [sem(f"landed{i}") for i in range(RING)]
        hi_done = sem("hi_done")
        lo_dve = sem("lo_dve")
        lo_pool = sem("lo_pool")
        unit_done = sem("unit_done")
        pair_done = sem("pair_done")
        pair_taken = [sem("pair_taken0"), sem("pair_taken1")]
        h_full_ready = sem("h_full_ready")
        h_hi_ready = sem("h_hi_ready")
        mix_hi_ready = sem("mix_hi_ready")
        mix_ready = sem("mix_ready")
        o_full_ready = sem("o_full_ready")
        o_hi_ready = sem("o_hi_ready")
        merged_full_ready = sem("merged_full_ready")
        merged_hi_ready = sem("merged_hi_ready")
        hid_hi_ready = sem("hid_hi_ready")
        hid_ready = sem("hid_ready")
        logits_done = sem("logits_done")
        x_tok_done = sem("x_tok_done")
        x_tok_taken = sem("x_tok_taken")
        turned = sem("turned")
        xe_hi_ready = sem("xe_hi_ready")
        xe_ready = sem("xe_ready")
        out_taken = sem("out_taken")
        out_done = sem("out_done")
        x_landed = [sem("x_landed0"), sem("x_landed1")]
        params_landed = sem("params_landed")
        poolw_landed = sem("poolw_landed")
        router_landed = sem("router_landed")
        fnw_landed = sem("fnw_landed")
        consts = sem("consts")
        job_done = sem("job_done")
        job_taken = [sem(f"job_taken{i}") for i in range(4)]
        down_done = sem("down_done")
        lb_max_ready = sem("lb_max_ready")
        lb_exp_ready = sem("lb_exp_ready")
        params_ready = sem("params_ready")
        sq_ready = sem("sq_ready")
        norm_done = sem("norm_done")
        rms_ln_ready = sem("rms_ln_ready")
        rstd_ready = sem("rstd_ready")
        h_ready = sem("h_ready")
        x_ready = sem("x_ready")
        forget_ready = sem("forget_ready")
        key_ready = sem("key_ready")
        logf_ready = sem("logf_ready")
        gsum_ready = sem("gsum_ready")
        th_ready = sem("th_ready")
        win_ready = sem("win_ready")
        pooled_ready = sem("pooled_ready")
        arg_ready = sem("arg_ready")
        exp_ready = sem("exp_ready")
        scaled_ready = sem("scaled_ready")
        level_done = sem("level_done")
        level_taken = sem("level_taken")
        o_done = sem("o_done")
        o_sq_ready = sem("o_sq_ready")
        o_mean_done = sem("o_mean_done")
        o_ln = sem("o_ln")
        o_rstd_ready = sem("o_rstd_ready")
        o_ready = sem("o_ready")
        merged_ready = sem("merged_ready")
        gap_ready = sem("gap_ready")
        gap_exp_ready = sem("gap_exp_ready")
        chosen_ready = sem("chosen_ready")
        tables_ready = sem("tables_ready")
        count_ready = sem("count_ready")
        sel_ready = sem("sel_ready")
        y_half_done = sem("y_half_done")
        y_dve = sem("y_dve")
        y_act = sem("y_act")
        silu_half = sem("silu_half")
        fin_sq = sem("fin_sq")
        fin_ln = sem("fin_ln")
        fin_rstd = sem("fin_rstd")
        fin_ready = sem("fin_ready")
        stored = sem("stored")
        pool_step = sem("pool_step")
        dve_step = sem("dve_step")

        def done(eng, n):
            eng.wait_ge(job_done, n + 1)

        def taken(eng, n):
            eng.wait_ge(job_taken[n % 4], n // 4 + 1)

        def bank_free(eng, n):
            if n >= 4:
                taken(eng, n - 4)

        def unit_freed(eng, n):
            kind, key = UNITS[n][4:]
            if kind == "unit":
                eng.wait_ge(unit_done, key)
            elif kind == "down":
                eng.wait_ge(down_done, key)
            else:
                done(eng, JOB[key])

        def unit_freed_i(eng, c, it):
            back = 1 if c < 0 else 0
            kind, value = MOE_FREED[c % ITEM_UNITS]
            if kind == "unit":
                eng.wait_ge(unit_done, it * a_item + (A_LOOP + value - back * a_item))
            elif kind == "down":
                eng.wait_ge(down_done, it * NG + (DN_LOOP + value - back * NG))
            else:
                eng.wait_ge(pair_done, it * (NG + 1) + (1 + value - back * (NG + 1)))

        def landed_wait(eng, n, it=None):
            if it is None:
                eng.wait_ge(landed[n % RING], 16 * (n // RING + 1))
            else:
                eng.wait_ge(landed[n % RING], it * (16 * ITEM_UNITS // RING) + 16 * (n // RING + 1))

        def feeder(eng, split_one):
            fed = [0]

            def feed(limit):
                while fed[0] < min(limit, U_LOOP):
                    split_one(fed[0])
                    fed[0] += 1
            return feed

        def feeder_i(eng, it, n_reg, split_item):
            fed = [SPLITS]

            def feed(limit):
                while fed[0] < limit:
                    c = fed[0]
                    if c < ITEM_UNITS:
                        split_item(c, it)
                    else:
                        with eng.If(n_reg > it + 1):
                            split_item(c - ITEM_UNITS, it + 1)
                    fed[0] += 1
            return feed

        w_in_v = w_in.rearrange("l (k p) f -> l p k f", p=P)
        column = {"u": 0, "q": 512, "f": 1024, "v": 1536, "g": 2048, "gate": 2560}
        ups = {"pool_up": pool_up.rearrange("l (k p) d -> l p k d", p=P),
               "hgrn_up": hgrn_up.rearrange("l (k p) d -> l p k d", p=P)}
        w_out_v = w_out.rearrange("l (k p) d -> l p k d", p=P)

        def kf(mem, s, width=GROUP):
            return mem[:, s, :].rearrange("p (k f) -> p k f", f=width)

        def fd(mem, s):
            return mem[:, s, :].rearrange("p (f d) -> p f d", d=D)

        block = ctx.enter_context(nc.Block())

        @block.sync
        def _(sp):
            def slot_free(n):
                sp.wait_ge(lo_dve, n - RING + 1)
                sp.wait_ge(lo_pool, n - RING + 1)

            for a in range(TH):
                sp.dma_start(x_tok[:, a, :], x[0, a * P:(a + 1) * P, :]).then_inc(x_landed[a], 16)
            for src, a, n in ((attn_norm_w.rearrange("l (k p) -> (l k) p", p=P), C_ATTN, 16),
                              (ffn_norm_w.rearrange("l (k p) -> (l k) p", p=P), C_FFN, 16),
                              (gate_bias.rearrange("l (k p) -> (l k) p", p=P), C_BIAS, 32),
                              (pool_scale.rearrange("l (k p) -> (l k) p", p=P), C_PSCALE, 8),
                              (hgrn_lower_bounds.rearrange("l (k p) -> (l k) p", p=P), C_LB, 8),
                              (hgrn_norm_w, C_HNORM, 2)):
                sp.dma_start(rows[a:a + n, :], src).then_inc(params_landed, 16)
            for n, (name, l, c, part, _, _) in enumerate(UNITS):
                if n >= RING:
                    slot_free(n)
                s = n % RING
                ks = slice(4 * part, 4 * part + 4)
                if name in column:
                    a = column[name] + c * GROUP
                    sp.dma_start(kf(ring, s), w_in_v[l, :, ks, a:a + GROUP]).then_inc(landed[s], 16)
                elif name in ups:
                    sp.dma_start(fd(ring, s), ups[name][l, :, 2 * part:2 * part + 2, :]).then_inc(landed[s], 16)
                elif name == "w_out":
                    sp.dma_start(kf(ring, s), w_out_v[l, :, ks, c * GROUP:(c + 1) * GROUP]).then_inc(landed[s], 16)
                elif name == "dense_d":
                    a = c * GROUP + part * 2 * P
                    sp.dma_start(fd(ring, s), dense_w_down[0, a:a + 2 * P, :].rearrange("(f p) d -> p f d", p=P)
                                 ).then_inc(landed[s], 16)
                else:
                    w = dense_w_gate if name == "dense_g" else dense_w_up
                    a, width = c * GROUP, DENSE[c] * P
                    if width < GROUP:
                        ks = slice(0, KT)
                    sp.dma_start(kf(ring, s, width),
                                 w[0, :, a:a + width].rearrange("(k p) f -> p k f", p=P)[:, ks, :]
                                 ).then_inc(landed[s], 16)

            def load_item(it, e):
                for c, (kind, i, part) in enumerate(MOE):
                    n = U_LOOP + c
                    s = n % RING
                    sp.wait_ge(lo_dve, it * ITEM_UNITS + (n - RING + 1))
                    sp.wait_ge(lo_pool, it * ITEM_UNITS + (n - RING + 1))
                    a = i * GROUP
                    if kind == "d":
                        a += part * 2 * P
                        src = moe_w_down[0, bass.ds(e, 1), a:a + 2 * P, :].rearrange("o (f p) d -> p (o f) d", p=P)
                        sp.dma_start(fd(ring, s), src).then_inc(landed[s], 16)
                    else:
                        w = moe_w_gate if kind == "g" else moe_w_up
                        r = part * 4 * P
                        src = w[0, bass.ds(e, 1), r:r + 4 * P, a:a + GROUP].rearrange("o (k p) f -> p (o k) f", p=P)
                        sp.dma_start(kf(ring, s), src).then_inc(landed[s], 16)

            with sp.Fori(0, N_EXP) as it:
                load_item(it, it)
            sp.wait_ge(tables_ready, 1)
            n = sp.value_load(n_items[0:1, 0:1], min_val=N_EXP, max_val=ITEMS)
            with sp.If(n > N_EXP):
                with sp.Fori(N_EXP, n) as it:
                    e = sp.value_load(item_e[0:1, bass.ds(it, 1)], min_val=0, max_val=N_EXP - 1)
                    load_item(it, e)
            for a in range(TH):
                for c in range(2):
                    ds = slice(c * 512, (c + 1) * 512)
                    sp.wait_ge(fin_ready, 2 * a + c + 1)
                    sp.dma_start(out[0, a * P:(a + 1) * P, ds], h_tok[:, a, ds]).then_inc(stored, 16)
            sp.wait_ge(stored, 16 * TH * 2)

        @block.gpsimd
        def _(pool):
            steps = [0]

            def step(ins):
                steps[0] += 1
                ins.then_inc(pool_step, 1)

            def settle():
                pool.wait_ge(pool_step, steps[0])

            g = nc.gpsimd
            step(g.memset(ident[:], 0.0))
            step(g.memset(mean_d[:], 1.0 / D))
            step(g.memset(mean_h[:], 1.0 / P))
            step(g.memset(eps[:], EPS))
            step(g.iota(inv_pos[:], pattern=[[0, POOL_TILES], [1, PAD]], base=1, channel_multiplier=0,
                        allow_small_or_imprecise_dtypes=True))
            settle()
            step(g.affine_select(out=ident[:], in_=ident[:], compare_op=ALU.not_equal, fill=1.0, base=0,
                                 pattern=[[-1, P]], channel_multiplier=1))
            settle()
            g.memset(fin[:], 0.0).then_inc(consts, 1)
            step(g.memset(ones[:], 1.0))
            step(g.memset(before[:], 1.0))
            step(g.memset(mask_f, 0.0))
            step(g.iota(iota_e[:], pattern=[[1, N_EXP]], base=0, channel_multiplier=0,
                        allow_small_or_imprecise_dtypes=True))
            step(g.iota(iota_c[:], pattern=[[1, CAP]], base=0, channel_multiplier=0,
                        allow_small_or_imprecise_dtypes=True))
            step(g.iota(iota_j[:], pattern=[[1, COLS], [0, N_EXP]], base=0, channel_multiplier=0,
                        allow_small_or_imprecise_dtypes=True))
            settle()
            step(g.affine_select(out=before[:], in_=before[:], compare_op=ALU.is_gt, fill=0.0, base=0,
                                 pattern=[[1, P]], channel_multiplier=-1))
            for m, h in enumerate(LEVELS[2:]):
                step(g.memset(mask_f[:, m, :].rearrange("p (b r) -> p b r", r=2 * h)[:, :, h:], 1.0))
            settle()
            for m, h in enumerate(LEVELS[2:]):
                v = mask_f[:, m, :].rearrange("p (b r) -> p b r", r=2 * h)
                step(g.affine_select(out=v, in_=v, compare_op=ALU.is_ge, fill=0.0, base=0,
                                     pattern=[[-2 * h, P // (2 * h)], [0, 2 * h]], channel_multiplier=1))
            settle()
            for m, h in enumerate(LEVELS[2:]):
                v = mask_f[:, m, :].rearrange("p (b r) -> p b r", r=2 * h)
                step(g.affine_select(out=v, in_=v, compare_op=ALU.is_ge, fill=0.0, base=h - 1,
                                     pattern=[[2 * h, P // (2 * h)], [0, 2 * h]], channel_multiplier=-1))
            settle()
            g.tensor_copy(masks[:], mask_f).then_inc(consts, 1)

            def lo_part(n, it=None):
                m = n if it is None else it * ITEM_UNITS + n
                q = UNIT // 4 * (4 - (POOL_QUARTERS if it is None else POOL_QUARTERS_EXP))
                s, b = n % RING, n % SPLITS
                pool.wait_ge(hi_done, m + 1)
                g.tensor_tensor(w_lo[:, b, q:], ring[:, s, q:], w_hi[:, b, q:].bitcast(F32), ALU.subtract
                                ).then_inc(lo_pool, 1)

            feed = feeder(pool, lo_part)
            for l in range(DEPTH):
                feed(AHEAD["u", l, 3])
                for j in range(4):
                    taken(pool, JOB["u", l, j])
                for buf in (pu, pb, pc):
                    step(g.memset(buf[:, :, 0:PAD], 0.0))
                settle()
                span = {1: (pu, pb, 0), 2: (pb, pc, 1), 4: (pc, pb, 2), 8: (pb, pc, 3)}
                for shift, (src, dst, first) in span.items():
                    a = src[:, first:, PAD:]
                    b = src[:, first:, PAD - shift:PAD - shift + T]
                    ins = g.tensor_tensor(dst[:, first:, PAD:], a, b, ALU.add)
                    if shift == 8:
                        ins.then_inc(win_ready, 1)
                    else:
                        step(ins)
                        settle()
            feed(U_LOOP)
            for c in range(SPLITS):
                lo_part(U_LOOP + c)
            pool.wait_ge(count_ready, 1)
            n_reg = pool.value_load(n_items[0:1, 0:1], min_val=N_EXP, max_val=ITEMS)
            with pool.Fori(0, n_reg) as it:
                feeder_i(pool, it, n_reg, lambda c, i: lo_part(U_LOOP + c, i))(ITEM_UNITS + SPLITS)

        @block.scalar
        def _(act):
            nc.scalar.preload_act_table_set(LN_EXP)
            act.dma_start(poolw[:], pool_w[0].rearrange("g c d -> c g d")).then_inc(poolw_landed, 16)
            act.dma_start(router[:], moe_router[0].rearrange("(k p) e -> p k e", p=P)).then_inc(router_landed, 16)
            act.wait_ge(consts, 1)

            def bank(n):
                return job_bank[n % 4]

            def hi_part(n, it=None, freed=None):
                if it is None:
                    landed_wait(act, n)
                    if n >= SPLITS:
                        unit_freed(act, n - SPLITS) if freed is None else freed()
                else:
                    landed_wait(act, n, it)
                    unit_freed_i(act, n - U_LOOP - SPLITS, it)
                nc.scalar.activation(w_hi[:, n % SPLITS, :], ring[:, n % RING, :], ACT.Copy).then_inc(hi_done, 1)

            feed = feeder(act, hi_part)
            for a in range(TH):
                n = JOB["x_in", 2 * a]
                done(act, n)
                nc.scalar.activation(xT[:, 0:4, a * P:(a + 1) * P],
                                     bank(n)[:].rearrange("p (k t) -> p k t", k=4), ACT.Copy
                                     ).then_inc(job_taken[n % 4], 1)
            def norm(l, w):
                if (l, w) == (1, 0):
                    nc.scalar.preload_act_table_set(LN_EXP)
                for i in range(KT // 2):
                    ks = slice(2 * i, 2 * i + 2)
                    if w == 1:
                        feed(AHEAD["w_out", l, 2 * i])
                        for j in range(2):
                            taken(act, JOB["w_out", l, 2 * i + j])
                    elif l == 0:
                        for j in (i // 2, 2 + i // 2):
                            taken(act, JOB["x_in", j])
                    else:
                        act.wait_ge(x_ready, i + 1)
                    nc.scalar.activation(sq[:, ks, :], xT[:, ks, :], ACT.Square).then_inc(sq_ready, 1)
                if (l, w) == (0, 0):
                    act.wait_ge(lb_max_ready, 1)
                    nc.scalar.activation(lb_tmp[:, 0:2, :], lb[:, :, :], ACT.Exp).then_inc(lb_exp_ready, 1)
                    feed(1)
                act.wait_ge(norm_done, 2 * l + w + 1)
                nc.scalar.activation(rstd[:], acc[0][:, 0:T], ACT.Ln, bias=eps[:, 0:1]).then_inc(rms_ln_ready, 1)
                act.wait_ge(rms_ln_ready, 2 * l + w + 1)
                nc.scalar.activation(rstd[:], rstd[:], ACT.Exp, scale=-0.5).then_inc(rstd_ready, 1)
                if (l, w) != (DEPTH - 1, 1):
                    for k in range(KT):
                        act.wait_ge(h_full_ready, KT * (2 * l + w) + k + 1)
                        nc.scalar.activation(h_parts[0][:, k, :], h_full[:, k, :], ACT.Copy).then_inc(h_hi_ready, 1)
                        if (l, w, k) == (0, 0, 3):
                            feed(2)

            def tanh_half(*key):
                n = JOB[key]
                feed(AHEAD[key])
                done(act, n)
                nc.scalar.activation(th[:, n % 4, :], bank(n)[:, 0:T], ACT.Tanh, scale=0.5).then_inc(th_ready, 1)

            for l in range(DEPTH):
                norm(l, 0)
                for j in range(HEADS):
                    n = JOB["f", l, j]
                    feed(AHEAD["f", l, j])
                    done(act, n)
                    nc.scalar.activation(expf[:, j, :], bank(n)[:, 0:T], ACT.Exp, scale=-1.0
                                         ).then_inc(job_taken[n % 4], 1)
                for j in range(HEADS):
                    tanh_half("q", l, j)
                feed(AHEAD["q", l, 3] + 1)
                act.wait_ge(forget_ready, HEADS * (l + 1))
                nc.scalar.activation(sig, sig, ACT.Ln).then_inc(logf_ready, 1)
                for a in range(TH):
                    n = JOB["v", l, a]
                    feed(AHEAD["v", l, a])
                    done(act, n)
                    nc.scalar.activation(v_tok[:, a, :], bank(n)[:], ACT.Copy).then_inc(job_taken[n % 4], 1)
                for j in range(POOL_TILES):
                    n = JOB["u", l, j]
                    feed(AHEAD["u", l, j])
                    done(act, n)
                    nc.scalar.activation(pu[:, j, PAD:], bank(n)[:, 0:T], ACT.Copy).then_inc(job_taken[n % 4], 1)
                def level_exp(lev):
                    act.wait_ge(arg_ready, 2 * ((NL - 1) * l + lev))
                    nc.scalar.activation(e_mem[:, lev % 2, :], e_mem[:, lev % 2, :], ACT.Exp).then_inc(exp_ready, 1)

                for c in range(4):
                    feed(UNIT_OF["gate", l, c, 0] + SPLITS)
                    if c > 0:
                        level_exp(2 * c)
                    level_exp(2 * c + 1)
                    for j in range(4 * c, 4 * c + 4):
                        n = JOB["gate", l, j]
                        feed(AHEAD["gate", l, j])
                        done(act, n)
                        nc.scalar.activation(gates[:, j, :], bank(n)[:, 0:T], ACT.Tanh, scale=0.5,
                                             bias=half_bias[:, 16 * l + j:16 * l + j + 1]
                                             ).then_inc(job_taken[n % 4], 1)
                    if c == 0:
                        for j in range(POOL_TILES):
                            n = JOB["mix", l, j]
                            c = C_PSCALE + POOL_TILES * l + j
                            done(act, n)
                            nc.scalar.activation(mixed[:, j, :], bank(n)[:, 0:T], ACT.Copy, scale=cols[:, c:c + 1]
                                                 ).then_inc(job_taken[n % 4], 1)
                        if l + 1 < DEPTH:
                            act.dma_start(poolw[:], pool_w[l + 1].rearrange("g c d -> c g d")).then_inc(poolw_landed, 16)
                        for j in range(POOL_TILES):
                            taken(act, JOB["mix", l, j])
                            nc.scalar.activation(mix_parts[0][:, j, :], mixed[:, j, :], ACT.Copy).then_inc(mix_hi_ready, 1)
                feed(UNIT_OF["g", l, 0, 0] + SPLITS)
                level_exp(NL - 1)
                for j in range(HEADS):
                    tanh_half("g", l, j)
                nc.scalar.preload_act_table_set(LN_EXP)
                feed(AHEAD["o", l])
                for j in range(HEADS):
                    taken(act, JOB["g", l, j])
                for i in range(2):
                    act.wait_ge(o_done, 2 * l + i + 1)
                    nc.scalar.activation(o_sq[:, i * 512:(i + 1) * 512], acc[i][:], ACT.Square
                                         ).then_inc(o_sq_ready, 1)
                for i in range(2):
                    act.wait_ge(o_mean_done, 2 * l + i + 1)
                    nc.scalar.activation(e_mem[:, 0, i * 512:(i + 1) * 512], acc[2 + i][:], ACT.Ln,
                                         bias=eps[:, 0:1]).then_inc(o_ln, 1)
                for i in range(2):
                    act.wait_ge(o_ln, 2 * l + i + 1)
                    nc.scalar.activation(e_mem[:, 0, i * 512:(i + 1) * 512], e_mem[:, 0, i * 512:(i + 1) * 512],
                                         ACT.Exp, scale=-0.5).then_inc(o_rstd_ready, 1)
                for i in range(2):
                    act.wait_ge(o_full_ready, 2 * l + i + 1)
                    nc.scalar.activation(o_parts[0][:, 2 * i:2 * i + 2, :],
                                         o_full[:, i * 512:(i + 1) * 512].rearrange("p (h t) -> p h t", h=2), ACT.Copy
                                         ).then_inc(o_hi_ready, 1)
                feed(AHEAD["y_hgrn", l, 0] - 1)
                for i in range(4):
                    if i == 2:
                        feed(AHEAD["y_hgrn", l, 0])
                    act.wait_ge(merged_full_ready, 4 * l + i + 1)
                    nc.scalar.activation(merged_parts[0][:, 2 * i:2 * i + 2, :], gates[:, 2 * i:2 * i + 2, :], ACT.Copy
                                         ).then_inc(merged_hi_ready, 1)
                norm(l, 1)
                if l == 0:
                    def hid_hi(tile):
                        n = JOB["ffn", tile]
                        i = tile // GT
                        taken(act, n)
                        nc.scalar.activation(hid_parts[0][:, i % 2, tile % GT, :], th[:, n % 4, :], ACT.Copy
                                             ).then_inc(hid_hi_ready, 1)

                    for j in range(sum(DENSE)):
                        if j >= 4:
                            act.wait_ge(hid_ready, j - 3)
                        tanh_half("ffn", j)
                        if j >= 1:
                            hid_hi(j - 1)
                    hid_hi(sum(DENSE) - 1)
                    feed(AHEAD["down", len(DENSE) - 1])

            for c in range(SPLITS):
                hi_part(U_LOOP + c)
            for i in (0, 2, 1, 3):
                n = JOB["h_tok", i]
                done(act, n)
                nc.scalar.activation(h_tok[:, i // 2, (i % 2) * 512:(i % 2) * 512 + 512], bank(n)[:], ACT.Copy
                                     ).then_inc(job_taken[n % 4], 1)
            act.wait_ge(gap_ready, 1)
            nc.scalar.activation(gap_e, gap, ACT.Exp).then_inc(gap_exp_ready, 1)
            nc.scalar.preload_act_table(ACT.Tanh)
            act.dma_start(qk_mem[:, 0:D], final_norm_w.rearrange("(o d) -> o d", o=1).to_broadcast([P, D])
                          ).then_inc(fnw_landed, 16)

            def tokens_hi():
                for i in range(2):
                    nc.scalar.activation(xe_parts[0][:, 4 * i:4 * i + 4, :],
                                         job_bank[2 + i][:, 0:4 * CAP].rearrange("p (k c) -> p k c", k=4), ACT.Copy
                                         ).then_inc(xe_hi_ready, 1)

            act.wait_ge(pair_done, 1)
            tokens_hi()
            for i in range(4):
                act.wait_ge(x_tok_done, i + 1)
                nc.scalar.activation(x_tok[:, i // 2, (i % 2) * 512:(i % 2) * 512 + 512], acc[i][:], ACT.Copy
                                     ).then_inc(x_tok_taken, 1)
            act.wait_ge(count_ready, 1)
            n_reg = act.value_load(n_items[0:1, 0:1], min_val=N_EXP, max_val=ITEMS)
            with act.Fori(0, n_reg) as it:
                feed_i = feeder_i(act, it, n_reg, lambda c, i: hi_part(U_LOOP + c, i))

                def hidden_hi(i):
                    act.wait_ge(turned, it * NG + (i + 1))
                    nc.scalar.activation(he_parts[0][:, i % 2, :, :],
                                         acc[2 + i % 2][:, 0:GT * CAP].rearrange("p (f c) -> p f c", f=GT), ACT.Copy
                                         ).then_inc(hid_hi_ready, 1)

                for i in range(NG):
                    if i >= 1:
                        feed_i(MOE_UNIT["g", i, 1] + 1 + SPLITS)
                        hidden_hi(i - 1)
                    feed_i(MOE_UNIT["u", i, 1] + SPLITS)
                    act.wait_ge(pair_done, it * (NG + 1) + (i + 2 + (i == NG - 1)))
                    nc.scalar.activation(th_e[:, i % 2, :], job_bank[2 * (i % 2)][0:CAP, :], ACT.Tanh, scale=0.5
                                         ).then_inc(th_ready, 1)
                feed_i(MOE_UNIT["d", NG - 2, 0] + SPLITS)
                hidden_hi(NG - 1)
                tokens_hi()
                feed_i(ITEM_UNITS - 1 + SPLITS)
                act.wait_ge(down_done, it * NG + (DN_LOOP + NG))
                nc.scalar.activation(y_tok[:, 512:1024], acc[1][0:CAP, :], ACT.Copy).then_inc(y_act, 1)
                feed_i(ITEM_UNITS + SPLITS)

            nc.scalar.preload_act_table_set(LN_EXP)
            for a in range(TH):
                act.wait_ge(out_taken, n_reg * 4 + (4 - 2 * (TH - 1 - a)))
                nc.scalar.activation(qk_mem[:, D:2 * D], x_tok[:, a, :], ACT.Square,
                                     accum_out=fin[:, a:a + 1]).then_inc(fin_sq, 1)
                act.wait_ge(fin_sq, a + 1)
                nc.scalar.activation(fin[:, 2 + a:3 + a], fin[:, a:a + 1], ACT.Ln, scale=1.0 / D, bias=eps[:, 0:1]
                                     ).then_inc(fin_ln, 1)
                act.wait_ge(fin_ln, a + 1)
                nc.scalar.activation(fin[:, 4 + a:5 + a], fin[:, 2 + a:3 + a], ACT.Exp, scale=-0.5).then_inc(fin_rstd, 1)

        @block.vector
        def _(dve):
            v = nc.vector
            steps = [0]

            def step(ins):
                steps[0] += 1
                ins.then_inc(dve_step, 1)

            def settle():
                dve.wait_ge(dve_step, steps[0])

            def bank(n):
                return job_bank[n % 4]

            def lo_part(n, it=None):
                m = n if it is None else it * ITEM_UNITS + n
                q = UNIT // 4 * (4 - (POOL_QUARTERS if it is None else POOL_QUARTERS_EXP))
                s, b = n % RING, n % SPLITS
                dve.wait_ge(hi_done, m + 1)
                v.tensor_tensor(w_lo[:, b, 0:q], ring[:, s, 0:q], w_hi[:, b, 0:q].bitcast(F32), ALU.subtract
                                ).then_inc(lo_dve, 1)

            def lo_of(parts, full, at):
                return v.tensor_tensor(parts[1][at], full, parts[0][at].bitcast(F32), ALU.subtract)

            feed = feeder(dve, lo_part)
            dve.wait_ge(consts, 1)
            for g, w in enumerate(WINDOWS):
                step(v.tensor_scalar(inv_pos[:, g, :], inv_pos[:, g, :], float(w), None, ALU.min))
            settle()
            step(v.reciprocal(inv_pos[:], inv_pos[:]))
            for a in range(TH):
                n = JOB["x_in", 2 * a + 1]
                done(dve, n)
                v.tensor_copy(xT[:, 4:8, a * P:(a + 1) * P], bank(n)[:].rearrange("p (k t) -> p k t", k=4)
                              ).then_inc(job_taken[n % 4], 1)
            n = JOB["params"]
            done(dve, n)
            v.tensor_copy(cols[:], bank(n)[:, 0:C_ROWS]).then_inc(job_taken[n % 4], 1)
            taken(dve, n)
            step(v.tensor_scalar(half_bias[:], cols[:, C_BIAS:C_BIAS + 32], 0.5, None, ALU.mult))
            step(v.tensor_scalar(half_hnorm[:], cols[:, C_HNORM:C_HNORM + DEPTH], 0.5, None, ALU.mult))
            l0, l1 = cols[:, C_LB:C_LB + HEADS], cols[:, C_LB + HEADS:C_LB + 2 * HEADS]
            step(v.tensor_tensor(lb_tmp[:, 2, :], l0, l1, ALU.max))
            settle()
            step(v.tensor_tensor(lb[:, 0, :], l0, lb_tmp[:, 2, :], ALU.subtract))
            v.tensor_tensor(lb[:, 1, :], l1, lb_tmp[:, 2, :], ALU.subtract).then_inc(lb_max_ready, 1)
            dve.wait_ge(lb_exp_ready, 1)
            step(v.tensor_tensor(lb_tmp[:, 2, :], lb_tmp[:, 0, :], lb_tmp[:, 1, :], ALU.add))
            settle()
            step(v.reciprocal(lb_tmp[:, 3, :], lb_tmp[:, 2, :]))
            settle()
            step(v.tensor_tensor(lb_tmp[:, 0, :], lb_tmp[:, 0, :], lb_tmp[:, 3, :], ALU.mult))
            step(v.tensor_tensor(lb_tmp[:, 1, :], lb_tmp[:, 1, :], lb_tmp[:, 3, :], ALU.mult))
            settle()
            step(v.tensor_tensor(lb[:, 0, :], lb_tmp[:, 0, :], lb_tmp[:, 0, :], ALU.subtract))
            step(v.tensor_tensor(lb[:, 1, :], lb_tmp[:, 0, :], lb_tmp[:, 1, :], ALU.add))
            settle()
            step(v.tensor_tensor(lb[:, 1, :], lb[:, 1, :], lb_tmp[:, 0, :], ALU.subtract))
            settle()
            step(v.tensor_scalar(lb[:], lb[:], 0.0, LB_CEIL, ALU.max, ALU.min))
            settle()
            step(v.tensor_scalar(lb_floor[:], lb[:], LB_FLOOR, None, ALU.max))
            step(v.tensor_scalar(one_lb[:], lb[:], -1.0, 1.0, ALU.mult, ALU.add))
            settle()
            v.tensor_scalar(half_one_lb[:], one_lb[:], 0.5, None, ALU.mult).then_inc(params_ready, 1)

            def norm(l, w):
                if (l, w) == (0, 0):
                    feed(1)
                dve.wait_ge(rstd_ready, 2 * l + w + 1)
                last = (l, w) == (DEPTH - 1, 1)
                at = KT * (2 * l + w)

                def lo(k):
                    dve.wait_ge(h_hi_ready, at + k + 1)
                    sl = (slice(None), k, slice(None))
                    lo_of(h_parts, h_full[sl], sl).then_inc(h_ready, 1)

                for k in range(KT):
                    c = (C_FFN if w else C_ATTN) + KT * l + k
                    v.scalar_tensor_tensor(out=h_full[:, k, :], in0=xT[:, k, :], scalar=cols[:, c:c + 1], in1=rstd[:],
                                           op0=ALU.mult, op1=ALU.mult).then_inc(h_full_ready, 1)
                    if k >= 1 and not last:
                        lo(k - 1)
                    if (l, w, k) == (0, 0, 6):
                        feed(2)
                if not last:
                    lo(KT - 1)

            def twice_silu(dst, name, l, j, ahead=0):
                n = JOB[name, l, j]
                feed(AHEAD[name, l, j] - ahead)
                dve.wait_ge(th_ready, TH_OF[name, l, j] + 1)
                v.scalar_tensor_tensor(out=dst, in0=th[:, n % 4, :], scalar=1.0, in1=bank(n)[:, 0:T],
                                       op0=ALU.add, op1=ALU.mult).then_inc(job_taken[n % 4], 1)

            for l in range(DEPTH):
                norm(l, 0)
                if l == 0:
                    dve.wait_ge(params_ready, 1)
                    dve.wait_ge(consts, 2)
                def forget(j):
                    feed(AHEAD["f", l, j])
                    taken(dve, JOB["f", l, j])
                    step(v.tensor_scalar(expf[:, j, :], expf[:, j, :], EXP_CEIL, None, ALU.min))
                    settle()
                    step(v.tensor_scalar(sig[:, j, :], expf[:, j, :], 1.0, None, ALU.add))
                    settle()
                    step(v.reciprocal(sig[:, j, :], sig[:, j, :]))
                    settle()
                    v.scalar_tensor_tensor(out=kT[:, j, :], in0=expf[:, j, :], scalar=half_one_lb[:, l, j:j + 1],
                                           in1=sig[:, j, :], op0=ALU.mult, op1=ALU.mult).then_inc(key_ready, 1)
                    v.tensor_scalar(sig[:, j, :], sig[:, j, :], one_lb[:, l, j:j + 1], lb_floor[:, l, j:j + 1],
                                    ALU.mult, ALU.add).then_inc(forget_ready, 1)

                for k in range(KT):
                    dve.wait_ge(h_ready, KT * 2 * l + k + 1)
                for j in range(HEADS - 1):
                    forget(j)
                feed(AHEAD["q", l, 0] - 1)
                for j in range(HEADS):
                    twice_silu(qT[:, j, :], "q", l, j, ahead=1)
                forget(HEADS - 1)
                feed(AHEAD["q", l, 3] + 1)
                dve.wait_ge(logf_ready, l + 1)
                for j in range(HEADS):
                    for a in range(TH):
                        ts = slice(a * P, (a + 1) * P)
                        v.tensor_tensor_scan(G[:, j, ts], ones[:], sig[:, j, ts], 0.0, ALU.mult, ALU.add
                                             ).then_inc(gsum_ready, 1)
                dve.wait_ge(gsum_ready, TH * HEADS * (l + 1))
                dve.wait_ge(key_ready, HEADS * (l + 1))

                def blocks(t, h):
                    return t.rearrange("p h t -> p (h t)").rearrange("p (b s r) -> p b s r", s=2, r=h)

                def scaled(lev):
                    return e_mem[:, lev % 2, :].rearrange("p (h t) -> p h t", h=HEADS)

                def arguments(lev):
                    if lev >= 3:
                        dve.wait_ge(level_done, NL * l + lev - 1)
                    h = P if LEVELS[lev] == "cross" else LEVELS[lev]
                    gb, eb = blocks(G[:], h), blocks(scaled(lev), h)
                    ref = gb[:, :, 0, h - 1:h].to_broadcast([P, HEADS * T // (2 * h), h])
                    v.tensor_tensor(eb[:, :, 0, :], ref, gb[:, :, 0, :], ALU.subtract).then_inc(arg_ready, 1)
                    if LEVELS[lev] == "cross":
                        v.tensor_copy(eb[:, :, 1, :], gb[:, :, 1, :]).then_inc(arg_ready, 1)
                    else:
                        v.tensor_tensor(eb[:, :, 1, :], gb[:, :, 1, :], ref, ALU.subtract).then_inc(arg_ready, 1)

                def scale_qk(lev):
                    dve.wait_ge(exp_ready, (NL - 1) * l + lev)
                    h = P if LEVELS[lev] == "cross" else LEVELS[lev]
                    eb, kb, qb = blocks(scaled(lev), h), blocks(kT, h), blocks(qT, h)
                    v.tensor_tensor(eb[:, :, 0, :], eb[:, :, 0, :], kb[:, :, 0, :], ALU.mult).then_inc(scaled_ready, 1)
                    v.tensor_tensor(eb[:, :, 1, :], eb[:, :, 1, :], qb[:, :, 1, :], ALU.mult).then_inc(scaled_ready, 1)

                def take(lev):
                    dve.wait_ge(level_done, NL * l + lev + 1)
                    pair = acc[2 * (lev % 2)], acc[2 * (lev % 2) + 1]
                    if LEVELS[lev] == "cross":
                        v.tensor_copy(score_x.rearrange("p h t -> p (h t)"), pair[0][:]).then_inc(level_taken, 2)
                        return
                    if LEVELS[lev] == "diag":
                        m = ident[:, :].unsqueeze(1).to_broadcast([P, HEADS, P])
                    else:
                        m = masks[:, lev - 2, :].unsqueeze(1).to_broadcast([P, HEADS, P])
                        dve.wait_ge(level_taken, 2 * (NL * l + lev))
                    for a in range(TH):
                        ps = pair[a][:].rearrange("p (h t) -> p h t", h=HEADS)
                        if LEVELS[lev] == "diag":
                            ins = v.tensor_tensor(score[:, a], ps, m, ALU.mult)
                        else:
                            ins = v.copy_predicated(score[:, a], m, ps)
                        ins.then_inc(level_taken, 1)

                arguments(1)
                feed(AHEAD["u", l, 3])
                def pooled():
                    dve.wait_ge(win_ready, l + 1)
                    step(v.tensor_tensor(pool_head[:, 0::2, :], pb[:, 0::2, PAD:2 * PAD], inv_pos[:, 0::2, :], ALU.mult))
                    step(v.tensor_tensor(pool_head[:, 1::2, :], pc[:, 1::2, PAD:2 * PAD], inv_pos[:, 1::2, :], ALU.mult))
                    settle()
                    v.tensor_tensor(pu[:, :, PAD:2 * PAD], pool_head[:], pu[:, :, PAD:2 * PAD], ALU.subtract
                                    ).then_inc(pooled_ready, 1)
                    for g, w in enumerate(WINDOWS):
                        src = (pb, pc)[g % 2]
                        v.scalar_tensor_tensor(out=pu[:, g, 2 * PAD:], in0=src[:, g, 2 * PAD:], scalar=1.0 / w,
                                               in1=pu[:, g, 2 * PAD:], op0=ALU.mult, op1=ALU.subtract
                                               ).then_inc(pooled_ready, 1)

                for j in range(HEADS):
                    taken(dve, JOB["q", l, j])
                for c in range(5):
                    first = UNIT_OF["gate", l, c, 0] if c < 4 else UNIT_OF["g", l, 0, 0]
                    if c > 0:
                        arguments(2 * c)
                        if 2 * c + 1 < NL:
                            arguments(2 * c + 1)
                        feed(first + SPLITS)
                        take(2 * c - 2)
                        scale_qk(2 * c)
                        take(2 * c - 1)
                    if 2 * c + 1 < NL:
                        scale_qk(2 * c + 1)
                        feed(first + 1 + SPLITS)
                    if c == 0:
                        pooled()
                    if c == 2:
                        for j in range(POOL_TILES):
                            dve.wait_ge(mix_hi_ready, POOL_TILES * l + j + 1)
                            sl = (slice(None), j, slice(None))
                            lo_of(mix_parts, mixed[sl], sl).then_inc(mix_ready, 1)
                take(NL - 1)
                dve.wait_ge(mix_ready, POOL_TILES * (l + 1))
                for j in range(HEADS):
                    twice_silu(og[:, j, :], "g", l, j)
                for j in range(HEADS):
                    taken(dve, JOB["g", l, j])
                feed(AHEAD["o", l])

                def twice_gated(name, first):
                    for i in range(4):
                        n = JOB[name, l, i]
                        feed(AHEAD[name, l, i] - (i < 3))
                        done(dve, n)
                        g = gates_mem[:, first * T + i * 512:first * T + (i + 1) * 512]
                        v.scalar_tensor_tensor(out=g, in0=g, scalar=1.0, in1=bank(n)[:], op0=ALU.add, op1=ALU.mult
                                               ).then_inc(job_taken[n % 4], 1)
                        yield i

                for i in range(2):
                    dve.wait_ge(o_sq_ready, 2 * l + i + 1)
                    dve.wait_ge(o_rstd_ready, 2 * l + i + 1)
                    step(v.scalar_tensor_tensor(out=o_full[:, i * 512:(i + 1) * 512], in0=acc[i][:],
                                                scalar=half_hnorm[:, l:l + 1], in1=e_mem[:, 0, i * 512:(i + 1) * 512],
                                                op0=ALU.mult, op1=ALU.mult))
                settle()
                for i in range(2):
                    part = o_full[:, i * 512:(i + 1) * 512]
                    v.tensor_tensor(part, part, og_mem[:, i * 512:(i + 1) * 512], ALU.mult).then_inc(o_full_ready, 1)
                for i in range(2):
                    dve.wait_ge(o_hi_ready, 2 * l + i + 1)
                    sl = (slice(None), slice(2 * i, 2 * i + 2), slice(None))
                    lo_of(o_parts, o_full[:, i * 512:(i + 1) * 512].rearrange("p (h t) -> p h t", h=2), sl
                          ).then_inc(o_ready, 1)

                for _ in twice_gated("y_pool", 0):
                    pass

                def merged_lo(i):
                    dve.wait_ge(merged_hi_ready, 4 * l + i + 1)
                    sl = (slice(None), slice(2 * i, 2 * i + 2), slice(None))
                    lo_of(merged_parts, gates[sl], sl).then_inc(merged_ready, 1)

                for i in twice_gated("y_hgrn", KT):
                    taken(dve, JOB["y_hgrn", l, i])
                    taken(dve, JOB["y_pool", l, i])
                    g = gates_mem[:, i * 512:(i + 1) * 512]
                    v.tensor_tensor(g, g, gates_mem[:, KT * T + i * 512:KT * T + (i + 1) * 512], ALU.add
                                    ).then_inc(merged_full_ready, 1)
                    if i >= 1:
                        merged_lo(i - 1)
                merged_lo(3)
                for d in range(KT):
                    n = JOB["w_out", l, d]
                    feed(AHEAD["w_out", l, d])
                    done(dve, n)
                    v.scalar_tensor_tensor(out=xT[:, d, :], in0=bank(n)[:, 0:T], scalar=0.5, in1=xT[:, d, :],
                                           op0=ALU.mult, op1=ALU.add).then_inc(job_taken[n % 4], 1)
                for d in range(KT):
                    taken(dve, JOB["w_out", l, d])
                norm(l, 1)
                if l == 0:
                    def hid_lo(tile):
                        n = JOB["ffn", tile]
                        dve.wait_ge(hid_hi_ready, tile + 1)
                        sl = (slice(None), tile // GT % 2, tile % GT, slice(None))
                        lo_of(hid_parts, th[:, n % 4, :], sl).then_inc(hid_ready, 1)

                    for tile in range(sum(DENSE)):
                        n = JOB["ffn", tile]
                        feed(AHEAD["ffn", tile])
                        dve.wait_ge(th_ready, TH_OF["ffn", tile] + 1)
                        v.scalar_tensor_tensor(out=th[:, n % 4, :], in0=th[:, n % 4, :], scalar=1.0,
                                               in1=bank(n)[:, 0:T], op0=ALU.add, op1=ALU.mult).then_inc(silu_half, 1)
                        dve.wait_ge(silu_half, tile + 1)
                        v.scalar_tensor_tensor(out=th[:, n % 4, :], in0=th[:, n % 4, :], scalar=0.5,
                                               in1=bank(n)[:, T:2 * T], op0=ALU.mult, op1=ALU.mult
                                               ).then_inc(job_taken[n % 4], 1)
                        if tile >= 1:
                            hid_lo(tile - 1)
                    hid_lo(sum(DENSE) - 1)
                    feed(AHEAD["down", len(DENSE) - 1])
                    dve.wait_ge(down_done, len(DENSE))
                    for i in range(4):
                        v.tensor_tensor(xT[:, 2 * i:2 * i + 2, :], acc[i][:].rearrange("p (d t) -> p d t", d=2),
                                        xT[:, 2 * i:2 * i + 2, :], ALU.add).then_inc(x_ready, 1)
                    dve.wait_ge(x_ready, 4)

            lo_part(U_LOOP)
            lo_part(U_LOOP + 1)
            dve.wait_ge(logits_done, 1)
            step(v.tensor_copy(lg, acc[2][:, 0:16].rearrange("p (a e) -> p a e", a=TH)))
            settle()
            for a in range(TH):
                step(v.max(top_v[:, a, :], lg[:, a, :]))
            settle()
            for a in range(TH):
                step(v.max_index(top_i[:, a, :], top_v[:, a, :], lg[:, a, :]))
            v.tensor_tensor(gap, top_v[:, :, 1], top_v[:, :, 0], ALU.subtract).then_inc(gap_ready, 1)
            settle()
            step(v.tensor_copy(top_f, top_i[:]))
            settle()
            for a in range(TH):
                step(v.tensor_scalar(hot1[:, a, :], iota_e[:], top_f[:, a, 0:1], None, ALU.is_equal))
                step(v.tensor_scalar(hot2[:, a, :], iota_e[:], top_f[:, a, 1:2], None, ALU.is_equal))
            settle()
            v.tensor_tensor(chosen, hot1, hot2, ALU.add).then_inc(chosen_ready, 1)
            lo_part(U_LOOP + 2)
            step(v.memset(ones8, 1.0))
            n = JOB["ranks"]
            done(dve, n)
            step(v.tensor_scalar(rank1, bank(n)[:, 0:16].rearrange("p (a e) -> p a e", a=TH), 1.0, None, ALU.add))
            v.tensor_copy(count, bank(n)[:, 16:24]).then_inc(job_taken[n % 4], 1)
            settle()
            taken(dve, n)
            dve.wait_ge(chosen_ready, 1)
            step(v.tensor_tensor(rank1, rank1, chosen, ALU.mult))
            step(v.tensor_scalar(over1, count, float(CAP), None, ALU.is_gt))
            step(v.tensor_scalar(over2, count, 2.0 * CAP, None, ALU.is_gt))
            settle()
            step(v.tensor_scalar(rank1, rank1, -1.0, None, ALU.add))
            step(v.tensor_tensor(over, over1, over2, ALU.add))
            settle()
            for a in range(TH):
                v.tensor_scalar(sel[:, a, :], iota_c[:], rank1[:, a, 0:1], None, ALU.is_equal).then_inc(sel_ready, 1)
            step(v.tensor_tensor_scan(cum, ones8, over, 0.0, ALU.mult, ALU.add))
            settle()
            step(v.scalar_tensor_tensor(out=start, in0=cum, scalar=float(N_EXP), in1=over, op0=ALU.add,
                                        op1=ALU.subtract))
            step(v.tensor_scalar(n_f, cum[:, 7:8], float(N_EXP), None, ALU.add))
            settle()
            step(v.tensor_scalar(start1, start, 1.0, None, ALU.add))
            v.tensor_copy(n_items[:], n_f).then_inc(count_ready, 1)
            v.memset(sel_wT[:, 0, :], 0.0).then_inc(pair_taken[0], 1)
            v.memset(sel_wT[:, 1, :], 0.0).then_inc(out_taken, 4)

            def tokens_lo(first):
                for i in range(2):
                    dve.wait_ge(xe_hi_ready, first + (i + 1))
                    sl = (slice(None), slice(4 * i, 4 * i + 4), slice(None))
                    lo_of(xe_parts, job_bank[2 + i][:, 0:4 * CAP].rearrange("p (k c) -> p k c", k=4), sl
                          ).then_inc(xe_ready, 1)

            dve.wait_ge(gap_exp_ready, 1)
            step(v.tensor_scalar(gap_1, gap_e, 1.0, None, ALU.add))
            settle()
            step(v.reciprocal(w1, gap_1))
            settle()
            step(v.tensor_tensor(w2, w1, gap_e, ALU.mult))
            settle()
            for a in range(TH):
                step(v.tensor_scalar(wt1[:, a, :], hot1[:, a, :], w1[:, a:a + 1], None, ALU.mult))
                step(v.tensor_scalar(wt2[:, a, :], hot2[:, a, :], w2[:, a:a + 1], None, ALU.mult))
            settle()
            step(v.tensor_tensor(comb, wt1, wt2, ALU.add))
            tokens_lo(0)
            dve.wait_ge(xe_ready, 2)
            v.memset(one_more[:], 0.0).then_inc(pair_taken[1], 1)

            def over_items(t):
                return t.unsqueeze(1).to_broadcast([P, COLS, N_EXP])

            settle()
            step(v.tensor_tensor(hot, iota_j[:], over_items(iota_e[:]), ALU.is_equal))
            step(v.tensor_tensor(one1, iota_j[:], over_items(start), ALU.is_equal))
            step(v.tensor_tensor(one2, iota_j[:], over_items(start1), ALU.is_equal))
            settle()
            step(v.tensor_tensor(one1, one1, over_items(over1), ALU.mult))
            step(v.tensor_tensor(one2, one2, over_items(over2), ALU.mult))
            settle()
            step(v.tensor_tensor(hot, hot, one1, ALU.add))
            step(v.tensor_reduce(base1, one1, AX_X, ALU.add))
            step(v.tensor_reduce(base2, one2, AX_X, ALU.add))
            settle()
            step(v.tensor_tensor(hot, hot, one2, ALU.add))
            step(v.scalar_tensor_tensor(out=base, in0=base2, scalar=2.0, in1=base1, op0=ALU.mult, op1=ALU.add))
            settle()
            step(v.tensor_scalar(base, base, float(CAP), None, ALU.mult))
            step(v.tensor_tensor(prod[:, 0], hot, over_items(iota_e[:]), ALU.mult))
            settle()
            step(v.tensor_reduce(e_f, prod[:, 0], AX_X, ALU.add))
            for a in range(TH):
                step(v.tensor_tensor(prod[:, 1 + a], hot, over_items(rank1[:, a, :]), ALU.mult))
            settle()
            step(v.tensor_copy(item_e[:], e_f))
            for a in range(TH):
                step(v.tensor_reduce(pos_item[:, a, :], prod[:, 1 + a], AX_X, ALU.add))
            settle()
            for a in range(TH):
                step(v.tensor_tensor(pos_item[:, a, :], pos_item[:, a, :], base, ALU.subtract))
                step(v.tensor_tensor(prod[:, 1 + a], hot, over_items(comb[:, a, :]), ALU.mult))
            settle()
            for a in range(TH):
                step(v.tensor_reduce(w_item[:, a, :], prod[:, 1 + a], AX_X, ALU.add))
            settle()
            v.memset(gap, 0.0).then_inc(tables_ready, 1)


            dve.wait_ge(count_ready, 1)
            dve.wait_ge(tables_ready, 1)
            n_reg = dve.value_load(n_items[0:1, 0:1], min_val=N_EXP, max_val=ITEMS)
            with dve.Fori(0, n_reg) as it:
                feed_i = feeder_i(dve, it, n_reg, lambda c, i: lo_part(U_LOOP + c, i))
                def hidden_lo(i):
                    dve.wait_ge(hid_hi_ready, it * NG + (sum(DENSE) + i + 1))
                    sl = (slice(None), i % 2, slice(None), slice(None))
                    lo_of(he_parts, acc[2 + i % 2][:, 0:GT * CAP].rearrange("p (f c) -> p f c", f=GT), sl
                          ).then_inc(hid_ready, 1)

                for i in range(NG):
                    if i >= 1:
                        feed_i(MOE_UNIT["g", i, 1] + 1 + SPLITS)
                        hidden_lo(i - 1)
                    feed_i(MOE_UNIT["u", i, 1] + SPLITS)
                    dve.wait_ge(th_ready, it * NG + (TH_LOOP + i + 1))
                    v.scalar_tensor_tensor(out=th_e[:, i % 2, :], in0=th_e[:, i % 2, :], scalar=1.0,
                                           in1=job_bank[2 * (i % 2)][0:CAP, :], op0=ALU.add, op1=ALU.mult
                                           ).then_inc(silu_half, 1)
                    dve.wait_ge(silu_half, it * NG + (sum(DENSE) + i + 1))
                    v.scalar_tensor_tensor(out=th_e[:, i % 2, :], in0=th_e[:, i % 2, :], scalar=0.5,
                                           in1=job_bank[2 * (i % 2) + 1][0:CAP, :], op0=ALU.mult, op1=ALU.mult
                                           ).then_inc(pair_taken[i % 2], 1)
                    if i == 0:
                        dve.wait_ge(pair_done, it * (NG + 1) + 1)
                        dve.wait_ge(sel_ready, it * 4 + 2)
                        for a in range(TH):
                            v.tensor_scalar(sel[:, a, :], iota_c[:], pos_item[:, a, bass.ds(it + 1, 1)], None, ALU.is_equal
                                            ).then_inc(sel_ready, 1)
                            v.tensor_scalar(sel_w[:, a, :], iota_c[:], pos_item[:, a, bass.ds(it, 1)],
                                            w_item[:, a, bass.ds(it, 1)], ALU.is_equal, ALU.mult).then_inc(sel_ready, 1)
                feed_i(MOE_UNIT["d", NG - 2, 0] + SPLITS)
                hidden_lo(NG - 1)
                tokens_lo(it * 2 + 2)
                v.tensor_copy(sel_wT[:, 0, :], job_bank[2][0:CAP, 4 * CAP:4 * CAP + P]).then_inc(xe_ready, 1)
                v.tensor_copy(sel_wT[:, 1, :], job_bank[3][0:CAP, 4 * CAP:4 * CAP + P]).then_inc(pair_taken[1], 1)
                feed_i(ITEM_UNITS - 2 + SPLITS)
                dve.wait_ge(y_half_done, it + 1)
                v.tensor_copy(y_tok[:, 0:512], acc[0][0:CAP, :]).then_inc(y_dve, 1)
                feed_i(ITEM_UNITS + SPLITS)
                for q in range(4):
                    dve.wait_ge(out_done, it * 4 + (q + 1))
                    dve.wait_ge(out_taken, it * 4 + (q + 1))
                    dst = x_tok[:, q // 2, (q % 2) * 512:(q % 2) * 512 + 512]
                    v.tensor_tensor(dst, acc[(2 + q) % 4][:], dst, ALU.add).then_inc(out_taken, 1)

            dve.wait_ge(fnw_landed, 16)
            for a in range(TH):
                dve.wait_ge(fin_rstd, a + 1)
                for c in range(2):
                    ds = slice(c * 512, (c + 1) * 512)
                    v.scalar_tensor_tensor(out=h_tok[:, a, ds], in0=x_tok[:, a, ds], scalar=fin[:, 4 + a:5 + a],
                                           in1=qk_mem[:, ds], op0=ALU.mult, op1=ALU.mult).then_inc(fin_ready, 1)

        @block.tensor
        def _(pe):
            def bank(n):
                return job_bank[n % 4]

            def split(name, l, c, part):
                n = UNIT_OF[name, l, c, part]
                pe.wait_ge(lo_dve, n + 1)
                pe.wait_ge(lo_pool, n + 1)
                return n % SPLITS

            def three(out, ops, first, last, **kw):
                (s_hi, s_lo), (m_hi, m_lo) = ops
                nc.tensor.matmul(out, s_hi, m_hi, start=first, stop=False, **kw)
                nc.tensor.matmul(out, s_hi, m_lo, start=False, stop=False, **kw)
                return nc.tensor.matmul(out, s_lo, m_hi, start=False, stop=last, **kw)

            def keep_warm(n):
                for _ in range(n):
                    nc.tensor.matmul(acc[3][:, 0:P], mean_d[:], mean_h[:], start=True, stop=True)

            pe.wait_ge(consts, 1)
            keep_warm(11)
            for i in range(4):
                n = JOB["x_in", i]
                bank_free(pe, n)
                if i % 2 == 0:
                    pe.wait_ge(x_landed[i // 2], 16)
                a, k0 = i // 2, 4 * (i % 2)
                for k in range(4):
                    mm = nc.tensor.transpose(bank(n)[:, k * P:(k + 1) * P],
                                             x_tok[:, a, (k0 + k) * P:(k0 + k + 1) * P], ident[:])
                mm.then_inc(job_done, 1)

            n = JOB["params"]
            bank_free(pe, n)
            pe.wait_ge(params_landed, 16 * 6)
            nc.tensor.transpose(bank(n)[:, 0:C_ROWS], rows[:, :], ident[0:C_ROWS, 0:C_ROWS]).then_inc(job_done, 1)
            keep_warm(2)

            def norm_sum(l, w, first):
                for k in range(first, first + 4):
                    if k % 2 == 0:
                        pe.wait_ge(sq_ready, KT // 2 * (2 * l + w) + k // 2 + 1)
                    mm = nc.tensor.matmul(acc[0][:, 0:T], mean_d[:], sq[:, k, :], start=(k == 0), stop=(k == KT - 1))
                return mm

            def norm(l, w):
                if w == 0:
                    norm_sum(l, w, 0)
                norm_sum(l, w, 4).then_inc(norm_done, 1)
                keep_warm(8)

            def project(name, l, c, keys, src, width=GROUP, at=0, h_wait=None, free=True, kts=KT, between={}):
                per = UNIT // width
                parts = kts // per
                for part in range(parts):
                    b = split(name, l, c, part)
                    hi, lo = kf(w_hi, b, width), kf(w_lo, b, width)
                    for j, key in enumerate(keys):
                        n = JOB[key]
                        if (part, j) in between:
                            between[part, j]()
                        if part == 0 and free:
                            bank_free(pe, n)
                        for k in range(per):
                            kk = part * per + k
                            if h_wait and j == 0:
                                h_wait(kk)
                            fs = slice(j * P, (j + 1) * P)
                            mm = three(bank(n)[:, at:at + T], ((hi[:, k, fs], lo[:, k, fs]),
                                                               (src[0][:, kk, :], src[1][:, kk, :])),
                                       kk == 0, kk == kts - 1)
                        if part == parts - 1 and name != "dense_g":
                            mm.then_inc(job_done, 1)
                    if part < parts - 1 or name == "dense_g":
                        mm.then_inc(unit_done, 1)

            def project_up(name, l, key, src, between={}):
                for part in range(2):
                    b = split(name, l, 0, part)
                    hi, lo = fd(w_hi, b), fd(w_lo, b)
                    for i in range(4):
                        n = JOB[key, l, i]
                        if (part, i) in between:
                            between[part, i]()
                        if part == 0:
                            bank_free(pe, n)
                        for h in range(2):
                            ds = slice((2 * i + h) * P, (2 * i + h + 1) * P)
                            for k in range(2):
                                kk = 2 * part + k
                                mm = three(bank(n)[:, h * T:(h + 1) * T], ((hi[:, k, ds], lo[:, k, ds]),
                                                                           (src[0][:, kk, :], src[1][:, kk, :])),
                                           kk == 0 and h == 0, kk == 3, skip_group_check=True)
                        if part == 1:
                            mm.then_inc(job_done, 1)
                    if part == 0:
                        mm.then_inc(unit_done, 1)

            def level(l, lev):
                if lev >= 2:
                    pe.wait_ge(level_taken, 2 * (NL * l + lev - 1))
                if LEVELS[lev] != "diag":
                    pe.wait_ge(scaled_ready, 2 * ((NL - 1) * l + lev))
                e = e_mem[:, lev % 2, :].rearrange("p (h t) -> p h t", h=HEADS)
                pair = acc[2 * (lev % 2)], acc[2 * (lev % 2) + 1]
                for hd in range(HEADS):
                    for a in range(1 if LEVELS[lev] == "cross" else TH):
                        ts = slice(a * P, (a + 1) * P)
                        if LEVELS[lev] == "diag":
                            s_op, t_op = kT[:, hd, ts], qT[:, hd, ts]
                        elif LEVELS[lev] == "cross":
                            s_op, t_op = e[:, hd, 0:P], e[:, hd, P:T]
                        else:
                            s_op, t_op = e[:, hd, ts], e[:, hd, ts]
                        mm = nc.tensor.matmul(pair[a][:, hd * P:(hd + 1) * P], s_op, t_op, start=True, stop=True)
                mm.then_inc(level_done, 1)

            for l in range(DEPTH):
                norm(l, 0)

                def h_wait(k, l=l, w=0):
                    pe.wait_ge(h_ready, KT * (2 * l + w) + k + 1)

                for name in "fq":
                    project(name, l, 0, [(name, l, j) for j in range(4)], h_parts,
                            h_wait=h_wait if name == "f" else None)
                for part in range(2):
                    b = split("v", l, 0, part)
                    for a in range(TH):
                        n = JOB["v", l, a]
                        if part == 0:
                            bank_free(pe, n)
                        for k in range(4):
                            kk = 4 * part + k
                            ts = slice(a * P, (a + 1) * P)
                            mm = three(bank(n)[:], ((h_parts[0][:, kk, ts], h_parts[1][:, kk, ts]),
                                                    (kf(w_hi, b)[:, k, :], kf(w_lo, b)[:, k, :])), kk == 0, kk == KT - 1)
                        if part == 1:
                            mm.then_inc(job_done, 1)
                    if part == 0:
                        mm.then_inc(unit_done, 1)
                project("u", l, 0, [("u", l, j) for j in range(4)], h_parts)
                for c in range(4):
                    project("gate", l, c, [("gate", l, 4 * c + j) for j in range(4)], h_parts)
                    if c == 0:
                        for q in range(HEADS):
                            taken(pe, JOB["q", l, q])
                        pe.wait_ge(key_ready, HEADS * (l + 1))
                    level(l, 2 * c)
                    level(l, 2 * c + 1)
                    if c == 0:
                        pe.wait_ge(pooled_ready, 5 * (l + 1))
                        pe.wait_ge(poolw_landed, 16 * (l + 1))
                        for g in range(POOL_TILES):
                            n = JOB["mix", l, g]
                            bank_free(pe, n)
                            nc.tensor.matmul(bank(n)[:, 0:T], poolw[:, g, :], pu[:, g, PAD:], start=True, stop=True
                                             ).then_inc(job_done, 1)
                project("g", l, 0, [("g", l, j) for j in range(4)], h_parts, between={(1, 0): lambda: level(l, NL - 1)})
                pe.wait_ge(level_taken, 2 * NL * (l + 1))
                for j in range(TH):
                    taken(pe, JOB["v", l, j])
                for hd in range(HEADS):
                    hs = slice(hd * P, (hd + 1) * P)
                    o_a = acc[hd // 2][:, (hd % 2) * T:(hd % 2) * T + P]
                    o_b = acc[hd // 2][:, (hd % 2) * T + P:(hd % 2) * T + T]
                    nc.tensor.matmul(o_a, v_tok[:, 0, hs], score[:, 0, hd, :], start=True, stop=True)
                    nc.tensor.matmul(o_b, v_tok[:, 0, hs], score_x[:, hd, :], start=True, stop=False)
                    mm = nc.tensor.matmul(o_b, v_tok[:, 1, hs], score[:, 1, hd, :], start=False, stop=True)
                    if hd % 2:
                        mm.then_inc(o_done, 1)

                def o_mean(i):
                    pe.wait_ge(o_sq_ready, 2 * l + i + 1)
                    nc.tensor.matmul(acc[2 + i][:], mean_h[:], o_sq[:, i * 512:(i + 1) * 512], start=True, stop=True
                                     ).then_inc(o_mean_done, 1)

                pe.wait_ge(mix_ready, POOL_TILES * (l + 1))
                project_up("pool_up", l, "y_pool", mix_parts,
                           between={(0, 2): lambda: o_mean(0), (0, 3): lambda: o_mean(1)})
                pe.wait_ge(o_ready, 2 * (l + 1))
                project_up("hgrn_up", l, "y_hgrn", o_parts)
                for c in range(2):
                    project("w_out", l, c, [("w_out", l, 4 * c + j) for j in range(4)], merged_parts,
                            h_wait=(lambda k: pe.wait_ge(merged_ready, 4 * l + k // 2 + 1)) if c == 0 else None,
                            between={(1, 0): lambda: norm_sum(l, 1, 0)} if c == 1 else {})
                norm(l, 1)
                if l == 0:
                    def down(i):
                        parts = 2 if DENSE[i] == GT else 1
                        for part in range(parts):
                            b = split("dense_d", 0, i, part)
                            for f in range(2):
                                ff = 2 * part + f
                                pe.wait_ge(hid_ready, sum(DENSE[:i]) + ff + 1)
                                for d in range(KT):
                                    ds = slice(d * P, (d + 1) * P)
                                    mm = three(acc[d // 2][:, (d % 2) * T:(d % 2) * T + T],
                                               ((fd(w_hi, b)[:, f, ds], fd(w_lo, b)[:, f, ds]),
                                                (hid_parts[0][:, i % 2, ff, :], hid_parts[1][:, i % 2, ff, :])),
                                               i == 0 and ff == 0 and d % 2 == 0,
                                               i == len(DENSE) - 1 and ff == DENSE[i] - 1, skip_group_check=True)
                            mm.then_inc(down_done if part == parts - 1 else unit_done, 1)

                    for i, tiles in enumerate(DENSE):
                        keys = [("ffn", sum(DENSE[:i]) + f) for f in range(tiles)]
                        project("dense_g", 0, i, keys, h_parts, width=tiles * P,
                                h_wait=(lambda k: h_wait(k, l, 1)) if i == 0 else None)
                        project("dense_u", 0, i, keys, h_parts, width=tiles * P, at=T, free=False)
                        if i >= 1:
                            down(i - 1)
                    down(len(DENSE) - 1)

            def token_major(dst, src, kk, a):
                return nc.tensor.transpose(dst[:, kk % 4 * P:(kk % 4 + 1) * P], src[:, kk, a * P:(a + 1) * P], ident[:])

            pe.wait_ge(router_landed, 16)
            for k in range(KT):
                pe.wait_ge(h_full_ready, KT * (2 * DEPTH - 1) + k + 1)
                for a in range(TH):
                    n = JOB["h_tok", 2 * a + k // 4]
                    if k % 4 == 0:
                        bank_free(pe, n)
                    mm = token_major(bank(n), h_full, k, a)
                    if k % 4 == 3:
                        mm.then_inc(job_done, 1)
                for a in range(TH):
                    mm = nc.tensor.matmul(acc[2][:, a * N_EXP:(a + 1) * N_EXP], h_full[:, k, a * P:(a + 1) * P],
                                          router[:, k, :], start=(k == 0 and a == 0), stop=(k == KT - 1),
                                          skip_group_check=True)
            mm.then_inc(logits_done, 1)
            keep_warm(8)
            n = JOB["ranks"]
            bank_free(pe, n)
            pe.wait_ge(consts, 2)
            pe.wait_ge(chosen_ready, 1)
            b = bank(n)
            nc.tensor.matmul(b[:, 0:8], before[:], chosen[:, 0, :], start=True, stop=True)
            nc.tensor.matmul(b[:, 8:16], ones[:], chosen[:, 0, :], start=True, stop=False)
            nc.tensor.matmul(b[:, 8:16], before[:], chosen[:, 1, :], start=False, stop=True)
            nc.tensor.matmul(b[:, 16:24], ones[:], chosen[:, 0, :], start=True, stop=False)
            nc.tensor.matmul(b[:, 16:24], ones[:], chosen[:, 1, :], start=False, stop=True).then_inc(job_done, 1)
            keep_warm(6)

            def gather():
                for k in range(KT):
                    for a in range(TH):
                        mm = nc.tensor.matmul(job_bank[2 + k // 4][:, (k % 4) * CAP:(k % 4 + 1) * CAP],
                                              h_tok[:, a, k * P:(k + 1) * P], sel[:, a, :],
                                              start=(a == 0), stop=(a == TH - 1))
                mm.then_inc(pair_done, 1)

            for i in range(4):
                taken(pe, JOB["h_tok", i])
            for n in range(len(JOB) - 4, len(JOB)):
                taken(pe, n)
            pe.wait_ge(sel_ready, TH)
            gather()
            pe.wait_ge(count_ready, 1)
            n_reg = pe.value_load(n_items[0:1, 0:1], min_val=N_EXP, max_val=ITEMS)
            for i in range(4):
                for k in range(4):
                    mm = token_major(acc[i], xT, 4 * (i % 2) + k, i // 2)
                mm.then_inc(x_tok_done, 1)
            with pe.Fori(0, n_reg) as it:
                def split_i(kind, i, part):
                    n = U_LOOP + MOE_UNIT[kind, i, part]
                    pe.wait_ge(lo_dve, it * ITEM_UNITS + (n + 1))
                    pe.wait_ge(lo_pool, it * ITEM_UNITS + (n + 1))
                    return n % SPLITS

                def hidden(kind, i):
                    ps = job_bank[2 * (i % 2) + (kind == "u")][0:CAP, :]
                    for part in range(2):
                        b = split_i(kind, i, part)
                        for k in range(4):
                            kk = 4 * part + k
                            mm = three(ps, ((xe_parts[0][:, kk, :], xe_parts[1][:, kk, :]),
                                            (kf(w_hi, b)[:, k, :], kf(w_lo, b)[:, k, :])), kk == 0, kk == KT - 1)
                        mm.then_inc(pair_done if (kind, part) == ("u", 1) else unit_done, 1)

                def turn(i):
                    pe.wait_ge(pair_taken[i % 2], it * 4 + (i // 2 + 2))
                    if i < 2:
                        pe.wait_ge(out_taken, it * 4 + 4)
                        pe.wait_ge(x_tok_taken, 4)
                    else:
                        pe.wait_ge(hid_ready, it * NG + (sum(DENSE) + i - 1))
                    for f in range(GT):
                        mm = nc.tensor.transpose(acc[2 + i % 2][:, f * CAP:(f + 1) * CAP],
                                                 th_e[:, i % 2, f * P:(f + 1) * P], ident[0:CAP, 0:CAP])
                    mm.then_inc(turned, 1)

                def down_i(i):
                    last = i == NG - 1
                    for part in range(2):
                        b = split_i("d", i, part)
                        if part == 0:
                            pe.wait_ge(hid_ready, it * NG + (sum(DENSE) + i + 1))
                        elif i == NG - 2:
                            turn(NG - 1)
                        for q in range(2):
                            qs = slice(q * 512, (q + 1) * 512)
                            for f in range(2):
                                ff = 2 * part + f
                                mm = three(acc[q][0:CAP, :],
                                           ((he_parts[0][:, i % 2, ff, :], he_parts[1][:, i % 2, ff, :]),
                                            (fd(w_hi, b)[:, f, qs], fd(w_lo, b)[:, f, qs])),
                                           i == 0 and ff == 0, last and ff == GT - 1)
                            if last and (part, q) == (1, 0):
                                mm.then_inc(y_half_done, 1)
                        mm.then_inc(unit_done if part == 0 else down_done, 1)

                pe.wait_ge(xe_ready, it * 3 + 2)
                for i in range(NG):
                    pe.wait_ge(pair_taken[i % 2], it * 4 + (i // 2 + 1))
                    hidden("g", i)
                    if i >= 1:
                        turn(i - 1)
                    if i == NG - 1:
                        pe.wait_ge(sel_ready, it * 4 + 6)
                        for a in range(TH):
                            nc.tensor.transpose(job_bank[2 + a][0:CAP, 4 * CAP:4 * CAP + P], sel_w[:, a, :], ident[:])
                        gather()
                    hidden("u", i)
                    if i >= 1:
                        down_i(i - 1)
                down_i(NG - 1)
                pe.wait_ge(xe_ready, it * 3 + 5)
                pe.wait_ge(pair_taken[1], it * 4 + (NG // 2 + 2))
                for q in range(4):
                    if q % 2:
                        pe.wait_ge(y_act, it + 1)
                    else:
                        pe.wait_ge(y_dve, it + 1)
                    nc.tensor.matmul(acc[(2 + q) % 4][:], sel_wT[:, q // 2, :],
                                     y_tok[:, (q % 2) * 512:(q % 2) * 512 + 512], start=True, stop=True
                                     ).then_inc(out_done, 1)


_INS = ["x", "attn_norm_w", "w_in", "gate_bias", "pool_w", "pool_scale", "pool_up", "hgrn_lower_bounds",
        "hgrn_norm_w", "hgrn_up", "w_out", "ffn_norm_w", "dense_w_gate", "dense_w_up", "dense_w_down",
        "moe_router", "moe_w_gate", "moe_w_up", "moe_w_down", "final_norm_w"]


def kernel(**inputs):
    import numpy as _np
    import concourse.bacc as _bacc
    from concourse import mybir as _mybir
    from concourse.bass_utils import run_bass_kernel_spmd as _run

    nc = _bacc.Bacc("TRN2", target_bir_lowering=False, num_devices=1)
    arrays, args = {}, []
    for name in _INS:
        a = _np.ascontiguousarray(inputs[name])
        arrays[f"in_{name}"] = a
        args.append(nc.dram_tensor(f"in_{name}", a.shape, _mybir.dt.from_np(a.dtype), kind="ExternalInput").ap())
    args.append(nc.dram_tensor("out_0", (1, T, D), F32, kind="ExternalOutput").ap())
    build(nc, *args)
    r = _run(nc, [arrays], core_ids=[0])
    return r.results[0]["out_0"]
```
